# Optimizing a Trainium2 kernel written in Bass

```python
import math
import jax, jax.numpy as jnp
from jax import lax
import numpy as np

D_MODEL = 1024
BATCH = 1
SEQ = 512
DEPTH = 2

GRID_W = 64
CTX_LEN = 256
BLOCK_Q = 128
CHUNK = 128
ROPE_BASE = 10000.0
EPS = 1e-6

A_HEADS = 6
A_KV_HEADS = 2
A_GROUP = A_HEADS // A_KV_HEADS
A_HEAD_DIM = 64
A_WIDTH = A_HEADS * A_HEAD_DIM
B_GROUPS = 4
B_GROUP_DIM = 64
B_WIDTH = B_GROUPS * B_GROUP_DIM
C_HEADS = 4
C_QK_DIM = 48
C_V_DIM = 2 * C_QK_DIM
C_WIDTH = C_HEADS * C_V_DIM
MIX_WIDTH = A_WIDTH + B_WIDTH + C_WIDTH
IN_SIZES = (A_WIDTH, A_KV_HEADS * A_HEAD_DIM, A_KV_HEADS * A_HEAD_DIM,
            B_WIDTH, B_WIDTH,
            2 * C_HEADS * C_QK_DIM, 2 * C_HEADS * C_QK_DIM, C_WIDTH)
IN_WIDTH = 2304
D_FF = 2816
N_MOD = 9

kernel_name = "hymba_style_gqa_gmlp_diffattn_macaron_dit"

def rms_norm(x, gain):
    xf = x.astype(jnp.float32)
    y = xf * lax.rsqrt(jnp.mean(xf * xf, axis=-1, keepdims=True) + EPS)
    return (y * gain.astype(jnp.float32)).astype(x.dtype)

def modulate(x, gain, shift, scale):
    return rms_norm(x, gain) * (1 + scale) + shift

def swiglu(h, w_in, w_out):
    gate, up = jnp.split(h @ w_in, 2, axis=-1)
    return (jax.nn.silu(gate) * up) @ w_out

def axial_angles(n, dim):
    rows = n // GRID_W
    row = jnp.repeat(jnp.arange(rows, dtype=jnp.float32), GRID_W)
    col = jnp.tile(jnp.arange(GRID_W, dtype=jnp.float32), rows)
    half = dim // 2
    freqs = 1.0 / (ROPE_BASE ** (jnp.arange(0, half, 2, dtype=jnp.float32) / half))
    return row[:, None] * freqs, col[:, None] * freqs

def rope_rotate(x, ang):
    m = ang.shape[-1]
    shape = (1, ang.shape[0]) + (1,) * (x.ndim - 3) + (m,)
    cos = jnp.cos(ang).reshape(shape).astype(x.dtype)
    sin = jnp.sin(ang).reshape(shape).astype(x.dtype)
    x1, x2 = x[..., :m], x[..., m:]
    return jnp.concatenate([x1 * cos - x2 * sin, x2 * cos + x1 * sin], axis=-1)

def axial_rope(x, ang_row, ang_col):
    half = x.shape[-1] // 2
    return jnp.concatenate([rope_rotate(x[..., :half], ang_row),
                            rope_rotate(x[..., half:], ang_col)], axis=-1)

def sweep_query_blocks(fn, q):
    b, n = q.shape[:2]
    qb = jnp.moveaxis(q.reshape((b, n // BLOCK_Q, BLOCK_Q) + q.shape[2:]), 1, 0)
    ob = jnp.moveaxis(lax.map(fn, qb), 0, 1)
    return ob.reshape((b, n) + ob.shape[3:])

def gqa_attend(q, k, v):
    s = jnp.einsum("bqhgd,bkhd->bhgqk", q, k).astype(jnp.float32) * (A_HEAD_DIM ** -0.5)
    p = jax.nn.softmax(s, axis=-1).astype(v.dtype)
    return jnp.einsum("bhgqk,bkhd->bqhgd", p, v)

def diff_attend(q, k, v, lam):
    s = jnp.einsum("bqchd,bkchd->bchqk", q, k).astype(jnp.float32) * (C_QK_DIM ** -0.5)
    p = jax.nn.softmax(s, axis=-1)
    a = (p[:, 0] - lam * p[:, 1]).astype(v.dtype)
    return jnp.einsum("bhqk,bkhe->bqhe", a, v)

def chunk_spatial_gate(u, v, w_s, b_s):
    b, n, _ = v.shape
    vc = v.reshape(b, n // CHUNK, CHUNK, B_GROUPS, B_GROUP_DIM)
    mixed = jnp.einsum("gpq,bnqgc->bnpgc", w_s, vc) + b_s.T[:, :, None]
    return u * mixed.reshape(b, n, B_WIDTH)

def split_heads(p):
    lead = p.shape[:2]
    idx = [int(i) for i in np.cumsum(IN_SIZES)[:-1]]
    qa, ka, va, u, v, qc, kc, vc = jnp.split(p, idx, axis=-1)
    return (qa.reshape(lead + (A_HEADS, A_HEAD_DIM)),
            ka.reshape(lead + (A_KV_HEADS, A_HEAD_DIM)),
            va.reshape(lead + (A_KV_HEADS, A_HEAD_DIM)),
            u, v,
            qc.reshape(lead + (2, C_HEADS, C_QK_DIM)),
            kc.reshape(lead + (2, C_HEADS, C_QK_DIM)),
            vc.reshape(lead + (C_HEADS, C_V_DIM)))

def token_mixing(hx, hc, w_in, w_out, g_q, g_k, g_v, w_s, b_s, lam_vecs, g_sub,
                 layer, ang_a, ang_c, with_ctx_out):
    b, n, _ = hx.shape
    L = hc.shape[1]
    qa_x, ka_x, va_x, u_x, v_x, qc_x, kc_x, vc_x = split_heads(hx @ w_in)
    qa_c, ka_c, va_c, u_c, v_c, qc_c, kc_c, vc_c = split_heads(hc @ w_in)

    qa_x = axial_rope(rms_norm(qa_x, g_q), *ang_a)
    ka_x = axial_rope(rms_norm(ka_x, g_k), *ang_a)
    qa_c = rms_norm(qa_c, g_q)
    ka_c = rms_norm(ka_c, g_k)
    ka_all = jnp.concatenate([ka_x, ka_c], axis=1)
    va_all = jnp.concatenate([va_x, va_c], axis=1)
    ya_x = sweep_query_blocks(lambda qb: gqa_attend(qb, ka_all, va_all),
                              qa_x.reshape(b, n, A_KV_HEADS, A_GROUP, A_HEAD_DIM)).reshape(b, n, A_WIDTH)

    yb_x = chunk_spatial_gate(jax.nn.gelu(u_x), rms_norm(jax.nn.gelu(v_x), g_v), w_s, b_s)

    lambda_init = 0.8 - 0.6 * math.exp(-0.3 * layer)
    lv = lam_vecs.astype(jnp.float32)
    lam = jnp.exp(jnp.sum(lv[0] * lv[1])) - jnp.exp(jnp.sum(lv[2] * lv[3])) + lambda_init
    qc_x = axial_rope(qc_x, *ang_c)
    kc_x = axial_rope(kc_x, *ang_c)
    kc_all = jnp.concatenate([kc_x, kc_c], axis=1)
    vc_all = jnp.concatenate([vc_x, vc_c], axis=1)
    yc_x = sweep_query_blocks(lambda qb: diff_attend(qb, kc_all, vc_all, lam), qc_x)
    yc_x = (rms_norm(yc_x, g_sub) * (1.0 - lambda_init)).reshape(b, n, C_WIDTH)

    out_x = jnp.concatenate([ya_x, yb_x, yc_x], axis=-1) @ w_out
    if not with_ctx_out:
        return out_x, None

    ya_c = gqa_attend(qa_c.reshape(b, L, A_KV_HEADS, A_GROUP, A_HEAD_DIM), ka_c, va_c).reshape(b, L, A_WIDTH)
    yb_c = chunk_spatial_gate(jax.nn.gelu(u_c), rms_norm(jax.nn.gelu(v_c), g_v), w_s, b_s)
    yc_c = (rms_norm(diff_attend(qc_c, kc_c, vc_c, lam), g_sub) * (1.0 - lambda_init)).reshape(b, L, C_WIDTH)
    out_c = jnp.concatenate([ya_c, yb_c, yc_c], axis=-1) @ w_out
    return out_x, out_c

def setup_inputs(seed: int = 0) -> dict:
    key = jax.random.key(seed)
    ks = jax.random.split(key, 24)
    f32 = jnp.float32
    nrm = lambda k, shape, s: jax.random.normal(k, shape, f32) * s
    gain = lambda k, shape: 1.0 + 0.05 * jax.random.normal(k, shape, f32)
    return {
        "x": nrm(ks[0], (BATCH, SEQ, D_MODEL), 1.0),
        "c": nrm(ks[1], (BATCH, D_MODEL), 1.0),
        "ctx": nrm(ks[2], (BATCH, CTX_LEN, D_MODEL), 1.0),
        "c_ctx": nrm(ks[3], (D_MODEL,), 1.0),
        "w_mod": nrm(ks[4], (DEPTH, D_MODEL, N_MOD * D_MODEL), 0.5 * D_MODEL ** -0.5),
        "b_mod": nrm(ks[5], (DEPTH, N_MOD * D_MODEL), 0.02),
        "g_ffn1": gain(ks[6], (DEPTH, D_MODEL)),
        "w_ffn1_in": nrm(ks[7], (DEPTH, D_MODEL, 2 * D_FF), D_MODEL ** -0.5),
        "w_ffn1_out": nrm(ks[8], (DEPTH, D_FF, D_MODEL), D_FF ** -0.5),
        "g_mix": gain(ks[9], (DEPTH, D_MODEL)),
        "w_mix_in": nrm(ks[10], (DEPTH, D_MODEL, IN_WIDTH), D_MODEL ** -0.5),
        "w_mix_out": nrm(ks[11], (DEPTH, MIX_WIDTH, D_MODEL), MIX_WIDTH ** -0.5),
        "g_qnorm": gain(ks[12], (DEPTH, A_HEAD_DIM)),
        "g_knorm": gain(ks[13], (DEPTH, A_HEAD_DIM)),
        "g_vnorm": gain(ks[14], (DEPTH, B_WIDTH)),
        "w_spatial": nrm(ks[15], (DEPTH, B_GROUPS, CHUNK, CHUNK), CHUNK ** -0.5),
        "b_spatial": gain(ks[16], (DEPTH, B_GROUPS, CHUNK)),
        "lambda_vecs": nrm(ks[17], (DEPTH, 4, C_QK_DIM), 0.1),
        "g_subln": gain(ks[18], (DEPTH, C_V_DIM)),
        "g_ffn2": gain(ks[19], (DEPTH, D_MODEL)),
        "w_ffn2_in": nrm(ks[20], (DEPTH, D_MODEL, 2 * D_FF), D_MODEL ** -0.5),
        "w_ffn2_out": nrm(ks[21], (DEPTH, D_FF, D_MODEL), D_FF ** -0.5),
        "g_final": gain(ks[22], (D_MODEL,)),
    }

def reference(x, c, ctx, c_ctx, w_mod, b_mod, g_ffn1, w_ffn1_in, w_ffn1_out, g_mix, w_mix_in,
              w_mix_out, g_qnorm, g_knorm, g_vnorm, w_spatial, b_spatial, lambda_vecs, g_subln,
              g_ffn2, w_ffn2_in, w_ffn2_out, g_final):
    n = x.shape[1]
    ang_a = axial_angles(n, A_HEAD_DIM)
    ang_c = axial_angles(n, C_QK_DIM)
    sc = jax.nn.silu(c)
    scc = jax.nn.silu(c_ctx)
    for l in range(DEPTH):
        last = l == DEPTH - 1
        mx = jnp.split((sc @ w_mod[l] + b_mod[l])[:, None, :], N_MOD, axis=-1)
        mc = jnp.split(scc @ w_mod[l] + b_mod[l], N_MOD, axis=-1)
        x = x + 0.5 * mx[2] * swiglu(modulate(x, g_ffn1[l], mx[0], mx[1]), w_ffn1_in[l], w_ffn1_out[l])
        ctx = ctx + 0.5 * mc[2] * swiglu(modulate(ctx, g_ffn1[l], mc[0], mc[1]), w_ffn1_in[l], w_ffn1_out[l])
        yx, yc = token_mixing(modulate(x, g_mix[l], mx[3], mx[4]), modulate(ctx, g_mix[l], mc[3], mc[4]),
                              w_mix_in[l], w_mix_out[l], g_qnorm[l], g_knorm[l], g_vnorm[l],
                              w_spatial[l], b_spatial[l], lambda_vecs[l], g_subln[l],
                              l, ang_a, ang_c, not last)
        x = x + mx[5] * yx
        x = x + 0.5 * mx[8] * swiglu(modulate(x, g_ffn2[l], mx[6], mx[7]), w_ffn2_in[l], w_ffn2_out[l])
        if not last:
            ctx = ctx + mc[5] * yc
            ctx = ctx + 0.5 * mc[8] * swiglu(modulate(ctx, g_ffn2[l], mc[6], mc[7]), w_ffn2_in[l], w_ffn2_out[l])
    return rms_norm(x, g_final)


_drawn_inputs = setup_inputs


def setup_inputs(seed=0):
    import zlib

    import numpy as np

    out = dict(_drawn_inputs(seed))
    spreads = {}
    factors = {'g_ffn1': 5.155,
     'g_mix': 3.651,
     'g_qnorm': 8.0,
     'g_knorm': 8.0,
     'g_vnorm': 7.899,
     'b_spatial': 7.575,
     'g_subln': 21.244,
     'g_ffn2': 5.705}
    for name, (base, spread) in spreads.items():
        noise = np.random.default_rng([zlib.crc32(name.encode()), seed]).standard_normal(out[name].shape)
        drawn = base * np.exp(spread * noise) if base else spread * noise
        out[name] = __import__('jax').numpy.asarray(drawn.astype(out[name].dtype))
    for name, factor in factors.items():
        out[name] = (out[name] * factor).astype(out[name].dtype)
    return out
```

```python
from contextlib import ExitStack
import math

import numpy as np

import concourse.bass as bass
from concourse import mybir

F32 = mybir.dt.float32
F32R = mybir.dt.float32r
ALU = mybir.AluOpType
ACT = mybir.ActivationFunctionType
AX = mybir.AxisListType
ds = bass.ds

P = 128
D = 1024
KD = D // P
NLAT, NCTX = 512, 256
T = NLAT + NCTX
TT = T // P
TLAT = NLAT // P
DEPTH = 2
D_FF = 2816
FFC = D_FF // P
GROUPS = (8, 8, 6)
NMOD = 9
EPS = 1e-6
HA, KVA, DA = 6, 2, 64
HC, DC, DV = 4, 48, 96
SLOT = 2048
IN_W = 2304
COLS = {"qa": 0, "ka": 384, "va": 512, "u": 640, "v": 896, "qc": 1152, "kc": 1536, "vc": 1920}
MIX_UNITS = ("v", "u", "va_vc", "vc", "qa", "qa_ka", "c0", "c1", "c2")
MIX_PIECES = {
    "v": [(COLS["v"], 256)], "u": [(COLS["u"], 256)],
    "va_vc": [(COLS["va"], 128), (COLS["vc"], 128)], "vc": [(COLS["vc"] + 128, 256)],
    "qa": [(COLS["qa"], 256)], "qa_ka": [(COLS["qa"] + 256, 256)],
    "c0": [(COLS["qc"], 256)], "c1": [(COLS["qc"] + 256, 256)], "c2": [(COLS["qc"] + 512, 256)],
}
NMU = len(MIX_UNITS)
SC_A = DA ** -0.5
SC_C = DC ** -0.5
FFN_UNITS = sum(GROUPS) + 4 * len(GROUPS)


def mix_tiles(unit, last):
    return TLAT if last and unit in ("v", "u", "qa", "c0") else TT


def plan_phases():
    phases = [("start", 0, 0)]
    for l in range(DEPTH):
        phases += [("norm", l, 0), ("ffn", l, 0), ("norm", l, 1), ("mix", l, 0), ("out", l, 0),
                   ("norm", l, 2), ("ffn", l, 1)]
    return phases


def has_ctx(kind, l, which):
    last = l == DEPTH - 1
    if not last:
        return True
    return {"norm": which < 2, "ffn": which == 0, "mix": True, "out": False}[kind]


def background(l, which):
    first = {(0, 0): 3, (0, 1): 8, (1, 0): 13}.get((l, which))
    return [] if first is None else list(range(first, first + 5))


def module_slots(l, which):
    mods = background(l, which)
    if not mods:
        return [None] * 6
    return [mods[0], mods[1], mods[2], mods[3], None, mods[4]]


def att_units(groups_of, last):
    out = []
    g = 0
    for h in range(groups_of):
        sets = [range(0, TLAT)] if last else [range(0, TLAT), range(TLAT, TT)]
        for s in sets:
            s = list(s)
            for t in s:
                out.append((h, g, t, t == s[0], t == s[-1]))
            g += 1
    return out


def adds(kind, l, which):
    last = l == DEPTH - 1
    a = {}
    if kind == "norm":
        a = dict(ss=KD, sq=KD - 1, stat=1, nt=KD, ny=KD, xh=KD, xl=KD)
    if kind == "ffn":
        nmod = len(background(l, which))
        a = dict(units=FFN_UNITS, evac=FFN_UNITS, hidden=FFC, mac=8 * nmod, fin=nmod)
    if kind == "mix":
        ntile = sum(mix_tiles(u, last) for u in MIX_UNITS)
        nlo = sum(mix_tiles(u, last) for u in ("va_vc", "vc"))
        prep = 4 + 2 * HC
        nu = len(att_units(HA, last)), len(att_units(HC, last))
        ng = 1 if last else 2
        a = dict(units=NMU, mix_mm=ntile, mix_lo=nlo, layer=1, v_tiles=TLAT if last else TT, spatial=4, yb=2, prep=prep,
                 score=nu[0] + 2 * nu[1], tile=sum(nu), pv=ng * (HA + HC), ya=ng * HA, yc=ng * HC)
    if kind == "out":
        a = dict(units=KD, evac=KD)
    return a


PHASES = plan_phases()
AT = []
_run = {}
for _ph in PHASES:
    AT.append(dict(_run))
    for _k, _v in adds(*_ph).items():
        _run[_k] = _run.get(_k, 0) + _v
TOTAL = dict(_run)


def plan_units():
    dmas, words, done = [], [], []
    units = tiles = 0
    for kind, l, which in PHASES:
        if kind == "ffn":
            for g in GROUPS:
                words += [((P, 0, SLOT),)] * g + [((P, 0, g * 256),)] * 4
                dmas += [2] * (g + 4)
                for _ in range(g + 4):
                    units += 1
                    done.append(("unit_done", units))
        if kind == "mix":
            for u in MIX_UNITS:
                tiles += mix_tiles(u, l == DEPTH - 1)
                dmas, words, done = dmas + [2], words + [((P, 0, SLOT),)], done + [("mix_mm", tiles)]
        if kind == "out":
            for _ in range(KD):
                units += 1
                dmas, words, done = dmas + [4], words + [((P, 0, 5 * P), (DV, 5 * P, 9 * P))], done + [("unit_done", units)]
    return dmas, words, done


UNIT_DMAS, UNIT_WORDS, UNIT_DONE = plan_units()
LANDED = [16 * sum(UNIT_DMAS[u % 2:u + 1:2]) for u in range(len(UNIT_DMAS))]


def keys(unit):
    return (T, 0) if unit[2] < TLAT else (NCTX, NLAT)


def group_of(units, g):
    mine = [x for x in units if x[1] == g]
    return mine[0][0], [x[2] for x in mine]


def units_first(units, g):
    return group_of(units, g)[1][0]


def new_pair(units, j):
    h = units[j][0]
    return h >= 2 and h % 2 == 0 and units[j - 1][0] != h


def prep_step(units, i):
    h = units[i][0]
    first = min(j for j, x in enumerate(units) if x[0] == h)
    return h + 1 if i == first + 1 and h + 1 < HC else None


def y_steps(units, i):
    g, out = units[i][1], []
    if units[i][3] and g >= 1:
        out.append(g - 1)
    if i == len(units) - 1:
        out.append(g)
    return out


def score_buf(part, i, c):
    return i % 2 if part == "A" else c


def prob_buf(part, i, c):
    return i % 2 if part == "A" else 2 * (i % 2) + c


def a_groups(p):
    return len({x[1] for x in att_units(HA, PHASES[p][1] == DEPTH - 1)})


def pvbase(p, part):
    return AT[p].get("pv", 0) + (a_groups(p) if part == "C" else 0)


def ybase(p, part):
    return AT[p].get("ya", 0) + AT[p].get("yc", 0) + (a_groups(p) if part == "C" else 0)


def c_pieces(unit):
    out = []
    col, end = 256 * unit, 256 * unit + 256
    while col < end:
        b, r = divmod(col, HC * DC)
        h, j = divmod(r, DC)
        stop = min(end, (b + 1) * HC * DC)
        if j or stop - col < DC:
            hn, jn = 1, min(DC - j, stop - col)
        else:
            hn, jn = (stop - col) // DC, DC
        out.append((col - 256 * unit, 8 * (b // 2) + 2 * h + b % 2, hn, j, jn))
        col += hn * jn
    return out


def build(nc, A, out):
    with ExitStack() as ctx:
        base = (nc.sbuf_base + 31) // 32 * 32
        top = nc.sbuf_usable_end

        def at(name, shape, dt, offset):
            n = 4
            for s in shape[1:]:
                n *= s
            assert base + offset + n <= top, (name, offset + n, top - base)
            return nc.alloc_sbuf_tensor_at(name, shape, dt, offset=base + offset)

        o = 0
        X = at("X", [P, KD, T], F32, o); o += 4 * KD * T
        XN_AT = o; o += 8 * KD * T
        R_AT = o; o += 16 * SLOT
        ST_AT = o; o += 8 * SLOT
        M_AT = o
        XN = at("XN", [P, 2, KD, T], F32R, XN_AT)
        XLOAD = at("XLOAD", [P, TT, D], F32, XN_AT)
        R = at("R", [P, 2, 2, SLOT], F32R, R_AT)
        ST = at("ST", [P, 2, SLOT], F32, ST_AT)
        H = at("H", [P, 2, GROUPS[0], T], F32R, M_AT)
        SG = at("SG", [P, T], F32, M_AT + 49152)
        HF = at("HF", [P, T], F32, M_AT + 52224)
        ACC = at("ACC", [P, 2, D], F32, M_AT + 55296)
        MW = at("MW", [P, 2, D], F32, M_AT + 63488)
        NT = at("NT", [P, 2, T], F32, M_AT)
        NY = at("NY", [P, 2, T], F32, M_AT + 8 * T)
        MSW = at("MSW", [P, 6, KD, 256], F32, M_AT)
        VROW = at("VROW", [P, 3, P], F32, M_AT + 55296)
        QA = at("QA", [P, TT, 512], F32, M_AT)
        QC = at("QC", [P, TT, 16, 64], F32, M_AT + 12288)
        VA = at("VA", [P, 2, TT, 128], F32R, M_AT + 36864)
        VC = at("VC", [P, 2, TT, 384], F32R, M_AT + 43008)
        YB = at("YB", [P, 2, 2, T], F32R, M_AT + 61440)
        U = at("U", [P, TT, 256], F32, M_AT)
        VN = at("VN", [P, 2, TT, 256], F32R, M_AT + 6144)
        VJ = at("VJ", [P, TT, 256], F32, M_AT + 6144)
        VF = at("VF", [P, TT, 256], F32, M_AT + 18432)
        WST = at("WST", [P, 2, 4, P], F32R, M_AT + 73728)
        WSR = at("WSR", [P, 4, P], F32, M_AT + 24576)
        ROT = at("ROT", [P, 2, 768], F32, M_AT + 73728)
        SS = at("SS", [P, T], F32, M_AT + 73728)
        SQ = at("SQ", [P, T], F32, M_AT + 73728 + 4 * T)
        Y = at("Y", [P, 2, 7, T], F32R, XN_AT)
        K0 = at("K0", [P, 2, T], F32R, XN_AT + 43008)
        PT = at("PT", [P, 2, TT, NLAT], F32R, R_AT)
        K1 = at("K1", [P, 2, T], F32R, R_AT + 24576)
        Q0 = at("Q0", [P, 2, T], F32R, M_AT + 73728)
        Q1 = at("Q1", [P, 2, T], F32R, M_AT + 36864)
        K23 = at("K23", [P, 2, 2, T], F32R, M_AT)
        PB = at("PB", [P, 4, T], F32, ST_AT)
        YRAW = at("YRAW", [P, NLAT], F32, ST_AT + 12288)
        YSQ = at("YSQ", [P, NLAT], F32, ST_AT + 14336)
        OUTB = at("OUTB", [P, 4, D], F32, XN_AT)
        OJ = at("OJ", [P, 2, D], F32, XN_AT + 16384)
        GF = at("GF", [P, D], F32, XN_AT + 24576)

        o = M_AT + 73728 + 8 * T

        def const(name, shape, dt=F32):
            nonlocal o
            t = at(name, shape, dt, o)
            n = 4
            for s in shape[1:]:
                n *= s
            o += (n + 31) // 32 * 32
            return t

        IDENT = const("IDENT", [P, P])
        ONE = const("ONE", [P, 1])
        NEGH = const("NEGH", [P, 48])
        VEC = const("VEC", [P, 80])
        BM = const("BM", [P, 18 * KD])
        SCV = const("SCV", [P, KD, 2])
        MODS = const("MODS", [P, 18 * KD, 2])
        AA = const("AA", [P, KD, 2])
        GG = const("GG", [P, KD, 2])
        ROPA = const("ROPA", [P, 2, TLAT, DA])
        ROPC = const("ROPC", [P, 2, TLAT, DC])
        GQK = const("GQK", [P, 2, DA])
        GV = const("GV", [P, 256])
        GS = const("GS", [P, 1])
        RST = const("RST", [P, 8])
        MSQ = const("MSQ", [P, 8])
        SM = const("SM", [P, 64])
        LV = at("LV", [P, 4, DC], F32, M_AT + 24576 + 2048)
        LVP = at("LVP", [P, 2, DC], F32, M_AT + 24576 + 2048 + 768)
        LM = const("LM", [P, 8])
        AST = const("AST", [P, TT, 8])
        ASR = const("ASR", [P, TT, 8])
        VSS = const("VSS", [P, 8])
        VSR = const("VSR", [P, 8])
        VMS = const("VMS", [P, 8])
        AMS = const("AMS", [P, TT, 8])
        YMS = const("YMS", [P, 4])
        YRS = const("YRS", [P, 4])
        FSS = const("FSS", [P, TLAT])
        FMS = const("FMS", [P, TLAT])
        FRS = const("FRS", [P, TLAT])

        PS = ctx.enter_context(nc.psum_tensor("PS", [P, 8, 512], F32))
        PF = PS[:, :, :].rearrange("p b n -> p (b n)")

        sems = {}

        def sem(name):
            s = ctx.enter_context(nc.semaphore(name))
            sems[name] = s
            return s

        w_landed = [sem("w_landed0"), sem("w_landed1")]
        w_hi, w_split, unit_done, evacuated = sem("w_hi"), sem("w_split"), sem("unit_done"), sem("evacuated")
        mw_landed = [sem("mw_landed0"), sem("mw_landed1")]
        ms_landed = [sem(f"ms_landed{i}") for i in range(6)]
        ms_used, mac_done, acc_clear, fin_mm, mod_ready = (sem("ms_used"), sem("mac_done"), sem("acc_clear"),
                                                           sem("fin_mm"), sem("mod_ready"))
        gate_ready = sem("gate_ready")
        silu_done, h_hi, h_lo = sem("silu_done"), sem("h_hi"), sem("h_lo")
        sq_done, ss_done, st_mm, ms_done, rstd_done = (sem("sq_done"), sem("ss_done"), sem("st_mm"),
                                                       sem("ms_done"), sem("rstd_done"))
        bc_mm, nt_done, ny_done, xn_hi, xn_lo, ab_done = (sem("bc_mm"), sem("nt_done"), sem("ny_done"),
                                                          sem("xn_hi"), sem("xn_lo"), sem("ab_done"))
        cst, vrow_in, vec_t, vec_ev, scv_done = (sem("cst"), sem("vrow_in"), sem("vec_t"), sem("vec_ev"),
                                                 sem("scv_done"))
        x_in, xt_mm, xt_ev, rope_in, layer_in = (sem("x_in"), sem("xt_mm"), sem("xt_ev"), sem("rope_in"),
                                                 sem("layer_in"))
        mix_mm, mix_act, mix_lo = sem("mix_mm"), sem("mix_act"), sem("mix_lo")
        ws_t, ws_hi, ws_lo = sem("ws_t"), sem("ws_hi"), sem("ws_lo")
        v_sq, v_ms, v_rstd, v_n, v_hi, v_lo = (sem("v_sq"), sem("v_ms"), sem("v_rstd"), sem("v_n"), sem("v_hi"),
                                               sem("v_lo"))
        sp_mm, sp_ev, yb_t, yb_hi, yb_lo, pad_done = (sem("sp_mm"), sem("sp_ev"), sem("yb_t"), sem("yb_hi"),
                                                      sem("yb_lo"), sem("pad_done"))
        a_ms, a_rstd, qk_c, lam_e, dve_step = (sem("a_ms"), sem("a_rstd"), sem("qk_c"),
                                                     sem("lam_e"), sem("dve_step"))
        lam_v = sem("lam_v")
        s_mm, mx_done, ex_done, p_done, t_mm, t_hi, t_lo = (sem("s_mm"), sem("mx_done"), sem("ex_done"),
                                                            sem("p_done"), sem("t_mm"), sem("t_hi"), sem("t_lo"))
        pr_t, pr_hi, pr_lo, pv_mm, y_hi, y_lo = (sem("pr_t"), sem("pr_hi"), sem("pr_lo"), sem("pv_mm"),
                                                 sem("y_hi"), sem("y_lo"))
        yr_done, yst_mm, yms_done, yrs_done, ybc_mm, yn_done = (sem("yr_done"), sem("yst_mm"), sem("yms_done"),
                                                                sem("yrs_done"), sem("ybc_mm"), sem("yn_done"))
        f_t, f_sq, f_ms, f_rs, f_n, out_done, gf_in, out_in = (sem("f_t"), sem("f_sq"), sem("f_ms"), sem("f_rs"),
                                                               sem("f_n"), sem("out_done"), sem("gf_in"),
                                                               sem("out_in"))

        wmod = A["w_mod"].rearrange("l (k p) n -> l p k n", p=P)
        w_in = {0: A["w_ffn1_in"], 1: A["w_ffn2_in"]}
        w_in = {i: w.rearrange("l (k p) n -> l p k n", p=P) for i, w in w_in.items()}
        w_out = {0: A["w_ffn1_out"], 1: A["w_ffn2_out"]}
        w_out = {i: w.rearrange("l (k p) n -> l p k n", p=P) for i, w in w_out.items()}
        w_mi = A["w_mix_in"].rearrange("l (k p) n -> l p k n", p=P)
        w_mo = A["w_mix_out"]
        stv = ST[:, :, :].rearrange("p s (k c) -> p s k c", c=256)
        MS7 = PF[:, 3840:3848]
        BC = PF[:, 3072:3072 + T]
        FN = PF[:, 3856:3872]

        def ring(hl, slot, k, c0, n):
            return R[:, hl, slot, k * 256 + c0:k * 256 + c0 + n]

        def set_views(s):
            return (PS[:, 3 * s, :], PS[:, 3 * s + 1, 0:256], PS[:, 3 * s + 1, 256:512], PS[:, 3 * s + 2, :])

        def c_k(h):
            return (K23[:, 0], K23[:, 1]) if h % 2 == 0 else (K0, K1)

        def c_q(h):
            q = Q0 if h % 2 == 0 else Q1
            return q[:, 0, :], q[:, 1, :]

        def products_done(eng, u, it=None):
            name, value = UNIT_DONE[u] if u >= 0 else ("unit_done", u + 1)
            eng.wait_ge(sems[name], value if it is None else value + 2 * it)

        def parts(p, l, which):
            u, e, h, m, n = AT[p].get("units", 0), AT[p].get("evac", 0), 0, 0, 0
            out_ = []
            slots = module_slots(l, which)
            for g, size in enumerate(GROUPS):
                out_.append((g, "in", u, e, h, size, slots[2 * g]))
                u, e = u + size, e + size
                out_.append((g, "out", u, e, h, 4, slots[2 * g + 1]))
                u, e, h = u + 4, e + 4, h + size
            return out_

        def count(p, key):
            return AT[p].get(key, 0)

        def modules_before(p, l, which, g, part):
            n = count(p, "fin")
            for i, m in enumerate(module_slots(l, which)):
                if i >= 2 * g + (part == "out"):
                    break
                n += m is not None
            return n

        def next_is_prefetched(p, u):
            nxt = u + 1
            if nxt >= TOTAL["units"]:
                return False
            return not any(ph[0] == "out" and AT[i]["units"] == nxt for i, ph in enumerate(PHASES))

        block = ctx.enter_context(nc.Block())

        @block.sync
        def _(sp):
            def slot_free(u, value=None):
                if u >= 2 or value is not None:
                    sp.wait_ge(w_split, (u - 1) if value is None else value)

            def mod_piece(q, k, slot, piece, it=None):
                if piece >= 2 or it is not None:
                    sp.wait_ge(mac_done, piece - 1 if it is None else piece - 1 + 2 * it)
                l_, j = divmod(q, NMOD)
                src = wmod[l_, :, k, j * D:(j + 1) * D] if it is None else \
                    A["w_mod"][l_, ds((2 * it + k) * P, P), j * D:(j + 1) * D]
                sp.dma_start(MW[:, slot, :], src).then_inc(mw_landed[slot], 16)

            sp.wait_ge(cst, 1)
            for r0, n, src in ((0, 8, A["c"].rearrange("b (k p) -> (b k) p", p=P)),
                               (8, 8, A["c_ctx"].rearrange("(k p) -> k p", p=P)),
                               (16, 16, A["g_ffn1"].rearrange("l (k p) -> (l k) p", p=P)),
                               (32, 16, A["g_mix"].rearrange("l (k p) -> (l k) p", p=P)),
                               (48, 16, A["g_ffn2"].rearrange("l (k p) -> (l k) p", p=P)),
                               (64, 8, A["b_spatial"].rearrange("l g p -> (l g) p"))):
                sp.dma_start(VROW[r0:r0 + n, 0, :], src).then_inc(vrow_in, 16)
            sp.dma_start(VROW[72:74, 0, 0:DV], A["g_subln"]).then_inc(vrow_in, 16)
            for l in range(DEPTH):
                sp.dma_start(VROW[0:72, 1 + l, :], A["b_mod"][l].rearrange("(k p) -> k p", p=P)).then_inc(vrow_in, 16)
            sp.dma_start(XLOAD[:, 0:TLAT, :], A["x"].rearrange("b (t p) d -> p (b t) d", p=P)).then_inc(x_in, 16)
            sp.dma_start(XLOAD[:, TLAT:TT, :], A["ctx"].rearrange("b (t p) d -> p (b t) d", p=P)).then_inc(x_in, 16)
            for i in range(12):
                if i >= 6:
                    sp.wait_ge(ms_used, i - 5)
                sp.dma_start(MSW[:, i % 6, :, :], wmod[0, :, :, i * 256:(i + 1) * 256]).then_inc(ms_landed[i % 6], 16)
            for i in range(2):
                sp.dma_start(ROPA[:, i, :, :], A["rope_a"][i]).then_inc(rope_in, 16)
                sp.dma_start(ROPC[:, i, :, :], A["rope_c"][i]).then_inc(rope_in, 16)

            for p, (kind, l, which) in enumerate(PHASES):
                if kind == "ffn":
                    wi, wo = w_in[which][l], w_out[which][l]
                    for g, part, u0, e0, h0, n, q in parts(p, l, which):
                        piece = 8 * modules_before(p, l, which, g, part)
                        if part == "in":
                            def in_weights(u, h, j, it=None):
                                slot_free(u, None if it is None else u - 1 + 2 * it)
                                c0 = h * P if it is None else (2 * it + h) * P
                                for b in range(2):
                                    sp.dma_start(stv[:, u % 2, :, b * P:(b + 1) * P], wi[:, :, ds(c0 + b * D_FF, P)]) \
                                        .then_inc(w_landed[u % 2], 16)

                            for j in range(2):
                                in_weights(u0 + j, h0 + j, j)
                            if q is not None:
                                if g == 0 and u0:
                                    products_done(sp, u0 - 1)
                                for j in range(2):
                                    mod_piece(q, j, j, piece + j)
                            with sp.Fori(1, n // 2) as it:
                                for j in range(2):
                                    in_weights(u0 + j, h0 + j, j, it)
                                    if q is not None:
                                        mod_piece(q, j, j, piece + j, it)
                        else:
                            for i in range(n):
                                u = u0 + i
                                slot_free(u)
                                k = GROUPS[g] // 2
                                for b in range(2):
                                    sp.dma_start(stv[:, u % 2, b * k:(b + 1) * k, :],
                                                 wo[:, h0 + b * k:h0 + (b + 1) * k, i * 256:(i + 1) * 256]) \
                                        .then_inc(w_landed[u % 2], 16)
                                if q is not None:
                                    for j in range(2):
                                        mod_piece(q, 2 * i + j, j, piece + 2 * i + j)
                if kind == "mix":
                    u0 = count(p, "units")
                    for w, name in enumerate(MIX_UNITS):
                        u = u0 + w
                        slot_free(u)
                        if len(MIX_PIECES[name]) == 1:
                            c0, n = MIX_PIECES[name][0]
                            for b in (slice(0, KD // 2), slice(KD // 2, KD)):
                                sp.dma_start(stv[:, u % 2, b, :], w_mi[l, :, b, c0:c0 + n]) \
                                    .then_inc(w_landed[u % 2], 16)
                        else:
                            for i, (c0, n) in enumerate(MIX_PIECES[name]):
                                sp.dma_start(stv[:, u % 2, :, i * P:(i + 1) * P], w_mi[l, :, :, c0:c0 + n]) \
                                    .then_inc(w_landed[u % 2], 16)
                        if w == 1:
                            products_done(sp, u0 - 1)
                            sp.dma_start(GQK[:, 0, :], A["g_qnorm"][l].partition_broadcast(P)).then_inc(layer_in, 16)
                            sp.dma_start(GQK[:, 1, :], A["g_knorm"][l].partition_broadcast(P)).then_inc(layer_in, 16)
                            sp.dma_start(GV[:, :], A["g_vnorm"][l].partition_broadcast(P)).then_inc(layer_in, 16)
                            sp.dma_start(WSR[:, :, :], A["w_spatial"][l].rearrange("g p q -> p g q")) \
                                .then_inc(layer_in, 16)
                            sp.dma_start(LV[:, :, :], A["lambda_vecs"][l].partition_broadcast(P)).then_inc(layer_in, 16)
                if kind == "out":
                    u0 = count(p, "units")
                    sp.wait_ge(y_lo, count(p, "ya") + count(p, "yc"))
                    for m in range(KD):
                        u = u0 + m
                        slot_free(u)
                        dst = ST[:, u % 2, 0:9 * P].rearrange("p (k c) -> p k c", c=P)
                        cols = slice(m * P, (m + 1) * P)
                        for b in range(2):
                            src = w_mo[l, b * 192:(b + 1) * 192, cols].rearrange("(j r) c -> r j c", r=DA)
                            sp.dma_start(dst[b * 64:(b + 1) * 64, 0:3, :], src).then_inc(w_landed[u % 2], 16)
                        src = w_mo[l, 384:640, cols].rearrange("(j r) c -> r j c", r=P)
                        sp.dma_start(dst[:, 3:5, :], src).then_inc(w_landed[u % 2], 16)
                        src = w_mo[l, 640:1024, cols].rearrange("(j r) c -> r j c", r=DV)
                        sp.dma_start(dst[0:DV, 5:9, :], src).then_inc(w_landed[u % 2], 16)
            products_done(sp, TOTAL["units"] - 1)
            sp.dma_start(GF[:, :], A["g_final"].partition_broadcast(P)).then_inc(gf_in, 16)
            for t in range(TLAT):
                sp.wait_ge(f_n, t + 1)
                sp.dma_start(out[0, t * P:(t + 1) * P, :], OUTB[:, t, :]).then_inc(out_done, 16)
            sp.wait_ge(out_done, 16 * TLAT)

        @block.gpsimd
        def _(pool):
            pool.memset(VROW[:, :, :], 0.0).then_inc(cst, 1)
            pool.memset(IDENT[:, :], 0.0).then_inc(cst, 1)
            pool.memset(ONE[:, :], 1.0).then_inc(cst, 1)
            pool.memset(NEGH[:, :], -0.5).then_inc(cst, 1)
            pool.wait_ge(cst, 4)
            pool.affine_select(out=IDENT[:, :], in_=IDENT[:, :], compare_op=ALU.not_equal, fill=1.0, base=0,
                               pattern=[[-1, P]], channel_multiplier=1).then_inc(cst, 1)
            for p, (kind, l, which) in enumerate(PHASES):
                if kind == "norm":
                    tok = T if has_ctx("norm", l, which) else NLAT
                    prev = PHASES[p - 1]
                    for k in range(KD):
                        if prev[0] == "start":
                            pool.wait_ge(xt_ev, k + 1)
                        elif prev[0] == "out":
                            pool.wait_ge(evacuated, count(p, "evac") - KD + k + 1)
                        else:
                            pool.wait_ge(evacuated, count(p, "evac") - 4 + k // 2 + 1)
                        if k == 0:
                            pool.tensor_tensor(SS[:, 0:tok], X[:, 0, 0:tok], X[:, 0, 0:tok], ALU.mult) \
                                .then_inc(ss_done, 1)
                            continue
                        pool.wait_ge(ss_done, count(p, "ss") + k)
                        pool.tensor_tensor(SQ[:, 0:tok], X[:, k, 0:tok], X[:, k, 0:tok], ALU.mult).then_inc(sq_done, 1)
                        pool.wait_ge(sq_done, count(p, "sq") + k)
                        pool.tensor_tensor(SS[:, 0:tok], SS[:, 0:tok], SQ[:, 0:tok], ALU.add).then_inc(ss_done, 1)
                    pool.wait_ge(ms_done, count(p, "stat") + 1)
                    nt = tok // P
                    pool.tensor_tensor(RST[:, 0:nt], MSQ[:, 0:nt], NEGH[:, 0:nt], ALU.pow).then_inc(rstd_done, 1)
                if kind == "mix":
                    last = l == DEPTH - 1
                    ntq = TLAT if last else TT
                    pool.wait_ge(v_ms, l + 1)
                    pool.tensor_tensor(VSR[:, 0:ntq], VMS[:, 0:ntq], NEGH[:, 0:ntq], ALU.pow).then_inc(v_rstd, 1)
                    pool.wait_ge(yb_t, count(p, "yb") + 2)
                    pool.memset(QC[:, :, :, DC:64], 0.0).then_inc(pad_done, 1)
                    pool.wait_ge(a_ms, l + 1)
                    pool.tensor_tensor(ASR[:, :, :], AMS[:, :, :], NEGH[:, :].rearrange("p (t h) -> p t h", h=8),
                                       ALU.pow).then_inc(a_rstd, 1)
                    for g in range((1 if last else 2) * HC):
                        pool.wait_ge(yms_done, count(p, "yc") + g + 1)
                        pool.tensor_tensor(YRS[:, :], YMS[:, :], NEGH[:, 0:4], ALU.pow).then_inc(yrs_done, 1)
            pool.wait_ge(f_ms, 1)
            pool.tensor_tensor(FRS[:, :], FMS[:, :], NEGH[:, 0:TLAT], ALU.pow).then_inc(f_rs, 1)

        def dve_mix(dve, p, l, last, link, split_lo):
            u0, n0, lo0 = count(p, "units"), count(p, "mix_mm"), count(p, "mix_lo")
            ntq = TLAT if last else TT
            tok = NLAT if last else T
            n = lo = 0
            for w, name in enumerate(MIX_UNITS):
                if w + 1 < NMU:
                    split_lo(u0 + w + 1)
                tiles = mix_tiles(name, last)
                if name == "v":
                    dve.wait_ge(layer_in, 80 * (l + 1))
                    link(dve.tensor_tensor(LVP[:, :, :], LV[:, 0:4:2, :], LV[:, 1:4:2, :], ALU.mult))
                    dve.tensor_reduce(LM[:, 0:2], LVP[:, :, :], AX.X, ALU.add).then_inc(lam_v, 1)
                    dve.wait_ge(ws_hi, l + 1)
                    dve.tensor_tensor(WST[:, 1, :, :], PS[:, 6, :].rearrange("p (g q) -> p g q", g=4),
                                      WST[:, 0, :, :].bitcast(F32), ALU.subtract).then_inc(ws_lo, 1)
                if name == "u":
                    dve.wait_ge(v_sq, count(p, "v_tiles") + ntq)
                    dve.tensor_scalar(VMS[:, 0:ntq], VSS[:, 0:ntq], 1.0 / 256, EPS, ALU.mult, ALU.add) \
                        .then_inc(v_ms, 1)
                    dve.wait_ge(v_rstd, l + 1)
                    for t in range(ntq):
                        ins = dve.scalar_tensor_tensor(VF[:, t, :], VF[:, t, :], VSR[:, t:t + 1], GV[:, :],
                                                       ALU.mult, ALU.mult)
                    ins.then_inc(v_n, 1)
                    dve.wait_ge(v_hi, l + 1)
                    dve.tensor_tensor(VN[:, 1, 0:ntq, :], VF[:, 0:ntq, :], VN[:, 0, 0:ntq, :].bitcast(F32),
                                      ALU.subtract).then_inc(v_lo, 1)
                if name in ("va_vc", "vc"):
                    for t in range(tiles):
                        dve.wait_ge(mix_act, n0 + n + t + 1)
                        b = PS[:, (n + t) % 6, 0:256]
                        if name == "va_vc":
                            dve.tensor_tensor(VA[:, 1, t, :], b[:, 0:128], VA[:, 0, t, :].bitcast(F32), ALU.subtract)
                            ins = dve.tensor_tensor(VC[:, 1, t, 0:128], b[:, 128:256],
                                                    VC[:, 0, t, 0:128].bitcast(F32), ALU.subtract)
                        else:
                            ins = dve.tensor_tensor(VC[:, 1, t, 128:384], b, VC[:, 0, t, 128:384].bitcast(F32),
                                                    ALU.subtract)
                        ins.then_inc(mix_lo, 1)
                if name == "va_vc":
                    dve.wait_ge(mix_act, n0 + 2 * ntq)
                    for g in range(4):
                        dve.wait_ge(sp_mm, count(p, "spatial") + g + 1)
                        dve.scalar_tensor_tensor(
                            VF[:, 0:ntq, g * 64:(g + 1) * 64],
                            PS[:, 6 + g % 2, 0:ntq * 64].rearrange("p (t c) -> p t c", c=64),
                            VEC[:, 64 + 4 * l + g:65 + 4 * l + g], U[:, 0:ntq, g * 64:(g + 1) * 64],
                            ALU.add, ALU.mult).then_inc(sp_ev, 1)
                if name == "vc":
                    for c in range(2):
                        dve.wait_ge(yb_hi, count(p, "yb") + c + 1)
                        dve.tensor_tensor(YB[:, 1, c, 0:tok], BC[:, 0:tok], YB[:, 0, c, 0:tok].bitcast(F32),
                                          ALU.subtract).then_inc(yb_lo, 1)
                n += tiles
                if name == "qa_ka":
                    for t in range(TT):
                        h0 = 6 if last and t >= TLAT else 0
                        dve.wait_ge(mix_act, n0 + n - TT + t + 1)
                        link(dve.tensor_tensor(ROT[:, 0, h0 * 64:512], QA[:, t, h0 * 64:512], QA[:, t, h0 * 64:512],
                                               ALU.mult))
                        link(dve.tensor_reduce(AST[:, t, h0:8],
                                               ROT[:, 0, h0 * 64:512].rearrange("p (h d) -> p h d", d=DA),
                                               AX.X, ALU.add))
                    dve.tensor_scalar(AMS[:, :, :], AST[:, :, :], 1.0 / DA, EPS, ALU.mult, ALU.add).then_inc(a_ms, 1)
                if name == "c0":
                    if l == 0:
                        dve.wait_ge(rope_in, 64)
                    dve.wait_ge(a_rstd, l + 1)
                    for t in range(TT):
                        h0 = 6 if last and t >= TLAT else 0
                        x = QA[:, t, h0 * 64:512].rearrange("p (h d) -> p h d", d=DA)
                        link(dve.tensor_tensor(x, x, ASR[:, t, h0:8].unsqueeze(2).broadcast_to([P, 8 - h0, DA]),
                                               ALU.mult))
                        if h0 == 0:
                            xq = QA[:, t, 0:384].rearrange("p (h d) -> p h d", d=DA)
                            dve.tensor_tensor(xq, xq, GQK[:, 0, :].unsqueeze(1).broadcast_to([P, 6, DA]), ALU.mult)
                        xk = QA[:, t, 384:512].rearrange("p (h d) -> p h d", d=DA)
                        link(dve.tensor_tensor(xk, xk, GQK[:, 1, :].unsqueeze(1).broadcast_to([P, 2, DA]), ALU.mult))
                        if t < TLAT:
                            rotate(dve, link, x, ROPA[:, 0, t, :], ROPA[:, 1, t, :], 8, DA)
                if name == "c2":
                    for t in range(TLAT):
                        dve.wait_ge(mix_act, n0 + n - TT + t + 1)
                        rotate(dve, link, QC[:, t, :, 0:DC], ROPC[:, 0, t, :], ROPC[:, 1, t, :], 16, DC)
                    dve.wait_ge(lam_e, l + 1)
                    init = 0.8 - 0.6 * math.exp(-0.3 * l)
                    link(dve.tensor_tensor(LM[:, 4:5], LM[:, 2:3], LM[:, 3:4], ALU.subtract))
                    link(dve.tensor_scalar(LM[:, 5:6], LM[:, 4:5], init, None, ALU.add))
                    dve.tensor_scalar(GS[:, :], VEC[:, 72 + l:73 + l], 1.0 - init, None, ALU.mult).then_inc(qk_c, 1)
                    dve.wait_ge(qk_c, l + 1)

            pr0 = count(p, "prep")

            def prep_lo(i, is_q, dst, tk):
                dve.wait_ge(pr_hi, pr0 + i + 1)
                for b in range(2):
                    rows = slice(64 * b, 64 * b + 64)
                    src = PF[rows, 2048:2048 + tk]
                    if is_q:
                        other = slice(64 - 64 * b, 128 - 64 * b)
                        ins = dve.tensor_tensor(dst[b][other, 0:tk], src, dst[b][rows, 0:tk].bitcast(F32),
                                                ALU.subtract)
                    else:
                        hi = dst[b][rows, 0, 0:tk].bitcast(F32)
                        dve.tensor_tensor(dst[b][0:64, 1, 0:tk], src, hi, ALU.subtract)
                        ins = dve.tensor_tensor(dst[b][64:128, 1, 0:tk], src, hi, ALU.subtract)
                ins.then_inc(pr_lo, 1)

            for part in ("A", "C"):
                heads = HA if part == "A" else HC
                units = att_units(heads, last)
                nua = len(att_units(HA, last))
                ns = 1 if part == "A" else 2
                scale = SC_A if part == "A" else SC_C
                sbase = count(p, "score") + (0 if part == "A" else nua)
                tbase = count(p, "tile") + (0 if part == "A" else nua)
                qtok = NLAT if last else T

                def maxima(i):
                    nk, k0 = keys(units[i])
                    for c in range(ns):
                        sb_, pb = score_buf(part, i, c), prob_buf(part, i, c)
                        dve.wait_ge(s_mm, sbase + ns * i + c + 1)
                        link(dve.tensor_reduce(SM[:, 12 + pb:13 + pb], PF[:, sb_ * 1024:sb_ * 1024 + nk], AX.X,
                                               ALU.max))
                        dve.tensor_scalar(SM[:, pb:pb + 1], SM[:, 12 + pb:13 + pb], -scale, None, ALU.mult) \
                            .then_inc(mx_done, 1)

                def weights(i):
                    nk, k0 = keys(units[i])
                    dve.wait_ge(ex_done, sbase + ns * i + ns)
                    pb = prob_buf(part, i, 0)
                    link(dve.reciprocal(SM[:, 8 + pb:8 + pb + ns], SM[:, 4 + pb:4 + pb + ns]))
                    if part == "A":
                        dve.tensor_scalar(PB[:, pb, 0:nk], PB[:, pb, 0:nk], SM[:, 8 + pb:9 + pb], None, ALU.mult) \
                            .then_inc(p_done, 1)
                    else:
                        link(dve.tensor_scalar(PB[:, pb + 1, 0:nk], PB[:, pb + 1, 0:nk], SM[:, 9 + pb:10 + pb],
                                               LM[:, 5:6], ALU.mult, ALU.mult))
                        dve.scalar_tensor_tensor(PB[:, pb, 0:nk], PB[:, pb, 0:nk], SM[:, 8 + pb:9 + pb],
                                                 PB[:, pb + 1, 0:nk], ALU.mult, ALU.subtract).then_inc(p_done, 1)

                def c_preps(h):
                    prep_lo(4 + 2 * h, False, c_k(h), T)
                    prep_lo(5 + 2 * h, True, c_q(h), qtok)

                if part == "A":
                    prep_lo(0, False, (K0, K1), T)
                    prep_lo(1, True, (Q0[:, 0, :], Q0[:, 1, :]), qtok)
                else:
                    c_preps(0)
                maxima(0)
                npair = 1
                for i, (h, g, t, first, final) in enumerate(units):
                    weights(i)
                    if part == "A" and i + 1 < len(units) and new_pair(units, i + 1):
                        npair += 1
                        prep_lo(npair, True, (Q0[:, 0, :], Q0[:, 1, :]), qtok)
                    if i + 1 < len(units):
                        maxima(i + 1)
                    nk, k0 = keys(units[i])
                    a, b = k0 // P, (k0 + nk) // P
                    q0 = (t - units_first(units, g)) * P
                    dve.wait_ge(t_hi, tbase + i + 1)
                    dve.tensor_tensor(PT[:, 1, a:b, q0:q0 + P],
                                      PF[:, 2048:2048 + nk].rearrange("p (k q) -> p k q", q=P),
                                      PT[:, 0, a:b, q0:q0 + P].bitcast(F32), ALU.subtract).then_inc(t_lo, 1)
                    if part == "C" and prep_step(units, i) is not None:
                        c_preps(prep_step(units, i))
                    for gg in y_steps(units, i):
                        bank = 6 + gg % 2
                        hh, tiles = group_of(units, gg)
                        nq, q0 = len(tiles) * P, tiles[0] * P
                        yb = ybase(p, part) + gg
                        if part == "A":
                            rows, j = slice(64 * (hh // 3), 64 * (hh // 3) + 64), hh % 3
                            dve.wait_ge(y_hi, yb + 1)
                            dve.tensor_tensor(Y[rows, 1, j, q0:q0 + nq], PS[rows, bank, 0:nq],
                                              Y[rows, 0, j, q0:q0 + nq].bitcast(F32), ALU.subtract).then_inc(y_lo, 1)
                            continue
                        yc = count(p, "yc") + gg
                        dve.wait_ge(yst_mm, yc + 1)
                        dve.tensor_scalar(YMS[:, 0:len(tiles)], PS[:, bank, 0:len(tiles)], 1.0 / DV, EPS, ALU.mult,
                                          ALU.add).then_inc(yms_done, 1)
                        dve.wait_ge(ybc_mm, yc + 1)
                        dve.scalar_tensor_tensor(YSQ[0:DV, 0:nq], PS[0:DV, bank, 0:nq], GS[0:DV, :],
                                                 YRAW[0:DV, 0:nq], ALU.mult, ALU.mult).then_inc(yn_done, 1)
                        dve.wait_ge(y_hi, yb + 1)
                        dve.tensor_tensor(Y[0:DV, 1, 3 + hh, q0:q0 + nq], YSQ[0:DV, 0:nq],
                                          Y[0:DV, 0, 3 + hh, q0:q0 + nq].bitcast(F32), ALU.subtract).then_inc(y_lo, 1)

        def rotate(dve, link, x, cos, sin, heads, d):
            m = d // 4
            a = ROT[:, 0, 0:heads * d].rearrange("p (h d) -> p h d", d=d)
            b = ROT[:, 1, 0:heads * d].rearrange("p (h d) -> p h d", d=d)
            dve.tensor_tensor(a, x, cos.unsqueeze(1).broadcast_to([P, heads, d]), ALU.mult)
            for axis in range(2):
                for half in range(2):
                    o1 = axis * 2 * m + half * m
                    o2 = axis * 2 * m + (1 - half) * m
                    ins = dve.tensor_tensor(b[:, :, o1:o1 + m], x[:, :, o2:o2 + m],
                                            sin[:, o1:o1 + m].unsqueeze(1).broadcast_to([P, heads, m]), ALU.mult)
            link(ins)
            link(dve.tensor_tensor(x, a, b, ALU.add))

        def pe_mix(pe, p, l, last, passes):
            u0, n0, lo0 = count(p, "units"), count(p, "mix_mm"), count(p, "mix_lo")
            ntq = TLAT if last else TT
            xl0 = AT[p]["xl"]
            freed = []
            n = nlo = 0
            pe.wait_ge(evacuated, count(p, "evac"))
            for w, name in enumerate(MIX_UNITS):
                s = (u0 + w) % 2
                tiles = mix_tiles(name, last)
                pe.wait_ge(w_split, u0 + w + 1)

                def tile_mm(t, k, m):
                    sl = slice(t * P, (t + 1) * P)
                    return passes(PS[:, m % 6, 0:256], XN[:, 0, k, sl], XN[:, 1, k, sl],
                                  ring(0, s, k, 0, 256), ring(1, s, k, 0, 256), k == 0, k == KD - 1)

                def bank_free(m):
                    if m >= 6:
                        pe.wait_ge(*freed[m - 6])

                if name == "v":
                    for k in range(KD):
                        pe.wait_ge(xn_lo, xl0 - KD + k + 1)
                        for t in range(tiles):
                            ins = tile_mm(t, k, t)
                            if k == KD - 1:
                                ins.then_inc(mix_mm, 1)
                else:
                    for t in range(tiles):
                        bank_free(n + t)
                        for k in range(KD):
                            ins = tile_mm(t, k, n + t)
                        ins.then_inc(mix_mm, 1)
                for t in range(tiles):
                    if name in ("va_vc", "vc"):
                        nlo += 1
                        freed.append((mix_lo, lo0 + nlo))
                    else:
                        freed.append((mix_act, n0 + n + t + 1))
                n += tiles
                if name == "v":
                    pe.wait_ge(layer_in, 80 * (l + 1))
                    for g in range(4):
                        ins = pe.transpose(PS[:, 6, g * P:(g + 1) * P], WSR[:, g, :], IDENT[:, :])
                    ins.then_inc(ws_t, 1)
                if name == "va_vc":
                    pe.wait_ge(ws_lo, l + 1)
                    pe.wait_ge(v_lo, l + 1)
                    for g in range(4):
                        if g >= 2:
                            pe.wait_ge(sp_ev, count(p, "spatial") + g - 1)
                        cols = slice(g * 64, (g + 1) * 64)
                        passes(PS[:, 6 + g % 2, 0:ntq * 64], WST[:, 0, g, :], WST[:, 1, g, :],
                               VN[:, 0, 0:ntq, cols], VN[:, 1, 0:ntq, cols], True, True).then_inc(sp_mm, 1)
                if name == "vc":
                    pe.wait_ge(sp_ev, count(p, "spatial") + 4)
                    for c in range(2):
                        if c:
                            pe.wait_ge(yb_lo, count(p, "yb") + c)
                        for t in range(ntq):
                            ins = pe.transpose(BC[:, t * P:(t + 1) * P], VF[:, t, c * P:(c + 1) * P], IDENT[:, :])
                        ins.then_inc(yb_t, 1)

            pr0 = count(p, "prep")
            turn = [None]

            def prep(i, src, tiles):
                if turn[0] is not None:
                    pe.wait_ge(*turn[0])
                for t in range(tiles):
                    ins = pe.transpose(PF[:, 2048 + t * P:2048 + (t + 1) * P], src(t), IDENT[:, :])
                ins.then_inc(pr_t, 1)
                turn[0] = (pr_lo, pr0 + i + 1)

            def c_preps(h):
                prep(4 + 2 * h, lambda t: QC[:, t, 8 + 2 * h:10 + 2 * h, :].rearrange("p h d -> p (h d)"), TT)
                prep(5 + 2 * h, lambda t: QC[:, t, 2 * h:2 * h + 2, :].rearrange("p h d -> p (h d)"), ntq)

            pe.wait_ge(mix_act, n0 + n)
            pe.wait_ge(mix_lo, lo0 + nlo)
            pe.wait_ge(yb_lo, count(p, "yb") + 2)
            for part in ("A", "C"):
                heads = HA if part == "A" else HC
                units = att_units(heads, last)
                nua = len(att_units(HA, last))
                ns = 1 if part == "A" else 2
                sbase = count(p, "score") + (0 if part == "A" else nua)
                tbase = count(p, "tile") + (0 if part == "A" else nua)

                def scores(i):
                    h, g, t, first, final = units[i]
                    nk, k0 = keys(units[i])
                    for c in range(ns):
                        sb_ = score_buf(part, i, c)
                        if part == "A" and i >= 2:
                            pe.wait_ge(ex_done, sbase + i - 1)
                        if part == "C" and i >= 1:
                            pe.wait_ge(ex_done, sbase + 2 * (i - 1) + c + 1)
                        q = Q0[:, h % 2, t * P:(t + 1) * P] if part == "A" else c_q(h)[c][:, t * P:(t + 1) * P]
                        kk = (K0, K1)[h // 3] if part == "A" else c_k(h)[c]
                        for j0 in range(0, nk, 512):
                            jn = min(512, nk - j0)
                            out_ = PF[:, sb_ * 1024 + j0:sb_ * 1024 + j0 + jn]
                            pe.matmul(out_, q, kk[:, 1, k0 + j0:k0 + j0 + jn], start=True, stop=False)
                            ins = pe.matmul(out_, q, kk[:, 0, k0 + j0:k0 + j0 + jn], start=False, stop=True)
                        ins.then_inc(s_mm, 1)

                def values(g):
                    h, tiles = group_of(units, g)
                    nk, k0 = keys((h, g, tiles[0], True, True))
                    bank, nq = 6 + g % 2, len(tiles) * P
                    final_unit = max(i for i, x in enumerate(units) if x[1] == g)
                    pe.wait_ge(t_lo, tbase + final_unit + 1)
                    if g >= 2:
                        pe.wait_ge(y_lo, ybase(p, part) + g - 1)
                    rows = P if part == "A" else DV
                    kts = range(k0 // P, (k0 + nk) // P)
                    for kt in kts:
                        if part == "A":
                            vh, vl = VA[:, 0, kt, :], VA[:, 1, kt, :]
                        else:
                            vh, vl = VC[:, 0, kt, h * DV:(h + 1) * DV], VC[:, 1, kt, h * DV:(h + 1) * DV]
                        ins = passes(PS[0:rows, bank, 0:nq], vh, vl, PT[:, 0, kt, 0:nq], PT[:, 1, kt, 0:nq],
                                     kt == kts[0], kt == kts[-1])
                    ins.then_inc(pv_mm, 1)

                if part == "A":
                    pe.wait_ge(qk_c, l + 1)
                    prep(0, lambda t: QA[:, t, 384:512], TT)
                    prep(1, lambda t: QA[:, t, 0:128], ntq)
                else:
                    pe.wait_ge(pad_done, l + 1)
                    c_preps(0)
                pe.wait_ge(*turn[0])
                scores(0)
                npair = 1
                for i, (h, g, t, first, final) in enumerate(units):
                    if part == "A" and i + 1 < len(units) and new_pair(units, i + 1):
                        npair += 1
                        j = npair - 1
                        prep(npair, lambda t: QA[:, t, j * 128:(j + 1) * 128], ntq)
                        pe.wait_ge(*turn[0])
                    if part == "C" and i + 1 < len(units) and units[i + 1][0] != h:
                        pe.wait_ge(pr_lo, pr0 + 5 + 2 * (h + 1) + 1)
                    if i + 1 < len(units):
                        scores(i + 1)
                    pe.wait_ge(p_done, tbase + i + 1)
                    pe.wait_ge(*turn[0])
                    nk, k0 = keys(units[i])
                    pb = prob_buf(part, i, 0)
                    for kt in range(nk // P):
                        ins = pe.transpose(PF[:, 2048 + kt * P:2048 + (kt + 1) * P], PB[:, pb, kt * P:(kt + 1) * P],
                                           IDENT[:, :])
                    ins.then_inc(t_mm, 1)
                    turn[0] = (t_lo, tbase + i + 1)
                    if first and g >= 1:
                        values(g - 1)
                    if part == "C" and prep_step(units, i) is not None:
                        c_preps(prep_step(units, i))
                    if i == len(units) - 1:
                        values(g)
                    for gg in y_steps(units, i):
                        if part == "A":
                            continue
                        hh, tiles = group_of(units, gg)
                        yc, bank = count(p, "yc") + gg, 6 + gg % 2
                        pe.wait_ge(yr_done, yc + 1)
                        for tt in range(len(tiles)):
                            ins = pe.matmul(PS[:, bank, tt:tt + 1], YSQ[0:DV, tt * P:(tt + 1) * P], ONE[0:DV, :],
                                            start=True, stop=True)
                        ins.then_inc(yst_mm, 1)
                        pe.wait_ge(yrs_done, yc + 1)
                        for tt in range(len(tiles)):
                            ins = pe.matmul(PS[:, bank, tt * P:(tt + 1) * P], YRS[:, tt:tt + 1].broadcast_to([P, P]),
                                            IDENT[:, :], start=True, stop=True)
                        ins.then_inc(ybc_mm, 1)

        @block.scalar
        def _(act):
            def split_hi(u, it=None):
                act.wait_ge(w_landed[u % 2], LANDED[u] if it is None else LANDED[u] + 32 * it)
                if u >= 2 or it is not None:
                    products_done(act, u - 2, it)
                for r, a, b in UNIT_WORDS[u]:
                    ins = act.activation(R[0:r, 0, u % 2, a:b], ST[0:r, u % 2, a:b], ACT.Copy)
                ins.then_inc(w_hi, 1)

            def act_y(p, part, units, g):
                h, tiles = group_of(units, g)
                bank, toks = 6 + g % 2, slice(tiles[0] * P, (tiles[-1] + 1) * P)
                nq = len(tiles) * P
                act.wait_ge(pv_mm, pvbase(p, part) + g + 1)
                if part == "A":
                    rows = slice(64 * (h // 3), 64 * (h // 3) + 64)
                    act.activation(Y[rows, 0, h % 3, toks], PS[rows, bank, 0:nq], ACT.Copy).then_inc(y_hi, 1)
                    return
                if g >= 1:
                    act.wait_ge(y_lo, ybase(p, part) + g)
                act.activation(YRAW[0:DV, 0:nq], PS[0:DV, bank, 0:nq], ACT.Copy)
                act.activation(YSQ[0:DV, 0:nq], PS[0:DV, bank, 0:nq], ACT.Square).then_inc(yr_done, 1)
                act.wait_ge(yn_done, count(p, "yc") + g + 1)
                act.activation(Y[0:DV, 0, 3 + h, toks], YSQ[0:DV, 0:nq], ACT.Copy).then_inc(y_hi, 1)

            act.wait_ge(vec_ev, 1)
            for i in range(2):
                ins = act.activation(SCV[:, :, i], VEC[:, i * KD:(i + 1) * KD], ACT.Silu)
            ins.then_inc(scv_done, 1)
            split_hi(0)

            for p, (kind, l, which) in enumerate(PHASES):
                last = l == DEPTH - 1
                if kind == "norm":
                    both = has_ctx("norm", l, which)
                    tok = T if both else NLAT
                    shift = (NMOD * l + 3 * which) * KD
                    act.wait_ge(ab_done, 3 * l + which + 1)
                    for k in range(KD):
                        act.wait_ge(nt_done, count(p, "nt") + k + 1)
                        if k >= 2:
                            act.wait_ge(xn_lo, count(p, "xl") + k - 1)
                        ins = act.activation(NY[:, k % 2, 0:NLAT], NT[:, k % 2, 0:NLAT], ACT.Identity,
                                             scale=AA[:, k, 0:1], bias=MODS[:, shift + k, 0:1])
                        if both:
                            ins = act.activation(NY[:, k % 2, NLAT:T], NT[:, k % 2, NLAT:T], ACT.Identity,
                                                 scale=AA[:, k, 1:2], bias=MODS[:, shift + k, 1:2])
                        ins.then_inc(ny_done, 1)
                        act.wait_ge(ny_done, count(p, "ny") + k + 1)
                        act.activation(XN[:, 0, k, 0:tok], NY[:, k % 2, 0:tok], ACT.Copy).then_inc(xn_hi, 1)
                if kind == "ffn":
                    tok = T if has_ctx("ffn", l, which) else NLAT
                    for g, part, u0, e0, h0, n, q in parts(p, l, which):
                        if part == "out":
                            for i in range(n):
                                if next_is_prefetched(p, u0 + i):
                                    split_hi(u0 + i + 1)
                            continue
                        act.preload_act_table(ACT.Silu)
                        with act.Fori(0, n // 2) as it:
                            for j in range(2):
                                u, c = u0 + j, 2 * it + j
                                split_hi(u + 1, it)
                                products_done(act, u, it)
                                act.activation(SG[:, 0:tok], PF[:, 1536 * ((e0 + j) % 2):1536 * ((e0 + j) % 2) + tok],
                                               ACT.Silu).then_inc(silu_done, 1)
                                act.wait_ge(evacuated, e0 + j + 1 + 2 * it)
                                act.activation(H[:, 0, ds(c, 1), 0:tok], HF[:, 0:tok].unsqueeze(1), ACT.Copy) \
                                    .then_inc(h_hi, 1)
                if kind == "mix":
                    u0, n0 = count(p, "units"), count(p, "mix_mm")
                    n = 0
                    for w, name in enumerate(MIX_UNITS):
                        if w + 1 < NMU:
                            split_hi(u0 + w + 1)
                        if name == "va_vc":
                            act.wait_ge(v_n, l + 1)
                            nt = TLAT if last else TT
                            act.activation(VN[:, 0, 0:nt, :], VF[:, 0:nt, :], ACT.Copy).then_inc(v_hi, 1)
                        for t in range(mix_tiles(name, last)):
                            act.wait_ge(mix_mm, n0 + n + 1)
                            b = PS[:, n % 6, 0:256]
                            if name == "v":
                                act.activation(VF[:, t, :], b, ACT.Gelu_apprx_tanh).then_inc(mix_act, 1)
                            elif name == "u":
                                act.activation(U[:, t, :], b, ACT.Gelu_apprx_tanh).then_inc(mix_act, 1)
                            elif name == "va_vc":
                                act.activation(VA[:, 0, t, :], b[:, 0:128], ACT.Copy)
                                act.activation(VC[:, 0, t, 0:128], b[:, 128:256], ACT.Copy).then_inc(mix_act, 1)
                            elif name == "vc":
                                act.activation(VC[:, 0, t, 128:384], b, ACT.Copy).then_inc(mix_act, 1)
                            elif name == "qa":
                                act.activation(QA[:, t, 0:256], b, ACT.Copy).then_inc(mix_act, 1)
                            elif name == "qa_ka":
                                act.activation(QA[:, t, 256:512], b, ACT.Copy).then_inc(mix_act, 1)
                            else:
                                for c0, h0, hn, j0, jn in c_pieces(int(name[1])):
                                    ins = act.activation(
                                        QC[:, t, h0:h0 + 2 * hn - 1:2, j0:j0 + jn],
                                        b[:, c0:c0 + hn * jn].rearrange("p (h j) -> p h j", j=jn), ACT.Copy)
                                ins.then_inc(mix_act, 1)
                            if name == "v":
                                act.wait_ge(mix_act, n0 + n + 1)
                                act.activation(VJ[:, t, :], VF[:, t, :], ACT.Square,
                                               accum_out=VSS[:, t:t + 1]).then_inc(v_sq, 1)
                            n += 1
                        if name == "v":
                            act.wait_ge(ws_t, l + 1)
                            act.activation(WST[:, 0, :, :], PS[:, 6, :].rearrange("p (g q) -> p g q", g=4),
                                           ACT.Copy).then_inc(ws_hi, 1)
                        if name == "vc":
                            for c in range(2):
                                act.wait_ge(yb_t, count(p, "yb") + c + 1)
                                tok = NLAT if last else T
                                act.activation(YB[:, 0, c, 0:tok], BC[:, 0:tok], ACT.Copy).then_inc(yb_hi, 1)
                    act.wait_ge(lam_v, l + 1)
                    act.activation(LM[:, 2:4], LM[:, 0:2], ACT.Exp).then_inc(lam_e, 1)

                    pr0 = count(p, "prep")

                    def prep_hi(i, is_q, dst, tok):
                        act.wait_ge(pr_t, pr0 + i + 1)
                        for b in range(2):
                            rows = slice(64 * b, 64 * b + 64)
                            src = PF[rows, 2048:2048 + tok]
                            if is_q:
                                ins = act.activation(dst[b][rows, 0:tok], src, ACT.Copy)
                            else:
                                act.activation(dst[b][0:64, 0, 0:tok], src, ACT.Copy)
                                ins = act.activation(dst[b][64:128, 0, 0:tok], src, ACT.Copy)
                        ins.then_inc(pr_hi, 1)

                    s0, x0, t0 = count(p, "score"), count(p, "score"), count(p, "tile")
                    for part in ("A", "C"):
                        heads = HA if part == "A" else HC
                        units = att_units(heads, last)
                        ns = 1 if part == "A" else 2
                        scale = SC_A if part == "A" else SC_C
                        sbase = s0 if part == "A" else s0 + len(att_units(HA, last))
                        tbase = t0 if part == "A" else t0 + len(att_units(HA, last))
                        qtok = NLAT if last else T

                        def exps(i):
                            nk, k0 = keys(units[i])
                            for c in range(ns):
                                act.wait_ge(mx_done, sbase + ns * i + c + 1)
                                if i >= 2:
                                    act.wait_ge(t_mm, tbase + i - 1)
                                sb_, pb = score_buf(part, i, c), prob_buf(part, i, c)
                                act.activation(PB[:, pb, 0:nk], PF[:, sb_ * 1024:sb_ * 1024 + nk], ACT.Exp,
                                               scale=scale, bias=SM[:, pb:pb + 1],
                                               accum_out=SM[:, 4 + pb:5 + pb]).then_inc(ex_done, 1)

                        def first_preps():
                            if part == "A":
                                prep_hi(0, False, (K0, K1), T)
                                prep_hi(1, True, (Q0[:, 0, :], Q0[:, 1, :]), qtok)
                            else:
                                c_preps(0)

                        def c_preps(h):
                            prep_hi(4 + 2 * h, False, c_k(h), T)
                            prep_hi(5 + 2 * h, True, c_q(h), qtok)

                        first_preps()
                        exps(0)
                        npair = 1
                        for i, (h, g, t, first, final) in enumerate(units):
                            if part == "A":
                                if i + 1 < len(units) and new_pair(units, i + 1):
                                    npair += 1
                                    prep_hi(npair, True, (Q0[:, 0, :], Q0[:, 1, :]), qtok)
                            if i + 1 < len(units):
                                exps(i + 1)
                            act.wait_ge(t_mm, tbase + i + 1)
                            if first and g >= 1:
                                act.wait_ge(pv_mm, pvbase(p, part) + g)
                            nk, k0 = keys(units[i])
                            a, b = k0 // P, (k0 + nk) // P
                            q0 = (t - units_first(units, g)) * P
                            act.activation(PT[:, 0, a:b, q0:q0 + P],
                                           PF[:, 2048:2048 + nk].rearrange("p (k q) -> p k q", q=P),
                                           ACT.Copy).then_inc(t_hi, 1)
                            if part == "C" and prep_step(units, i) is not None:
                                c_preps(prep_step(units, i))
                            for gg in y_steps(units, i):
                                act_y(p, part, units, gg)

                if kind == "out":
                    u0 = count(p, "units")
                    split_hi(u0)
                    for m in range(KD):
                        if next_is_prefetched(p, u0 + m):
                            split_hi(u0 + m + 1)
            for t in range(TLAT):
                act.wait_ge(f_t, t + 1)
                if t >= 2:
                    act.wait_ge(f_sq, t - 1)
                act.activation(OJ[:, t % 2, :], PF[:, 1024 * (t % 2):1024 * (t % 2) + D], ACT.Square,
                               accum_out=FSS[:, t:t + 1]).then_inc(f_sq, 1)

        @block.vector
        def _(dve):
            steps = [0]

            def link(ins):
                steps[0] += 1
                ins.then_inc(dve_step, 1)
                dve.wait_ge(dve_step, steps[0])

            def split_lo(u, it=None):
                dve.wait_ge(w_hi, u + 1 if it is None else u + 1 + 2 * it)
                for r, a, b in UNIT_WORDS[u]:
                    ins = dve.tensor_tensor(R[0:r, 1, u % 2, a:b], ST[0:r, u % 2, a:b],
                                            R[0:r, 0, u % 2, a:b].bitcast(F32), ALU.subtract)
                ins.then_inc(w_split, 1)

            def mod_piece(slot, k, piece, it=None):
                dve.wait_ge(mw_landed[slot], 16 * (piece // 2 + 1) if it is None else 16 * (piece // 2 + 1) + 16 * it)
                dve.wait_ge(mac_done, piece if it is None else piece + 2 * it)
                for v in range(2):
                    col = SCV[:, k, v:v + 1] if it is None else SCV[:, ds(2 * it + k, 1), v:v + 1]
                    ins = dve.scalar_tensor_tensor(ACC[:, v, :], MW[:, slot, :], col, ACC[:, v, :], ALU.mult, ALU.add)
                ins.then_inc(mac_done, 1)

            def clear_sums(n):
                dve.memset(ACC[:, :, :], 0.0).then_inc(acc_clear, 1)
                dve.wait_ge(acc_clear, n + 1)

            def finish_module(q, n):
                dve.wait_ge(fin_mm, n + 1)
                dve.tensor_tensor(MODS[:, q * KD:(q + 1) * KD, :], FN.rearrange("p (k v) -> p k v", v=2),
                                  BM[:, q * KD:(q + 1) * KD].unsqueeze(2).broadcast_to([P, KD, 2]), ALU.add) \
                    .then_inc(mod_ready, 1)
                dve.wait_ge(mod_ready, n + 2)

            dve.wait_ge(vec_t, 1)
            dve.tensor_copy(VEC[:, :], PS[:, 0, 0:80])
            dve.tensor_copy(BM[:, 0:72], PS[:, 1, 0:72])
            dve.tensor_copy(BM[:, 72:144], PS[:, 1, 128:200]).then_inc(vec_ev, 1)
            dve.wait_ge(vec_ev, 1)
            for k in range(KD):
                dve.wait_ge(xt_mm, k + 1)
                b = 2048 if k % 2 else 1024
                dve.tensor_copy(X[:, k, :], PF[:, b:b + T]).then_inc(xt_ev, 1)
            split_lo(0)
            dve.wait_ge(ms_used, 12)
            dve.tensor_tensor(MODS[:, 0:24, :], PS[:, 0, 0:48].rearrange("p (k v) -> p k v", v=2),
                              BM[:, 0:24].unsqueeze(2).broadcast_to([P, 24, 2]), ALU.add).then_inc(mod_ready, 1)
            dve.wait_ge(mod_ready, 1)

            for p, (kind, l, which) in enumerate(PHASES):
                last = l == DEPTH - 1
                if kind == "norm":
                    both = has_ctx("norm", l, which)
                    tok = T if both else NLAT
                    nt = tok // P
                    sc = (NMOD * l + 3 * which + 1) * KD
                    gcol = 16 + 16 * which + KD * l
                    dve.scalar_tensor_tensor(AA[:, :, :], MODS[:, sc:sc + KD, :], 1.0,
                                             VEC[:, gcol:gcol + KD].unsqueeze(2).broadcast_to([P, KD, 2]),
                                             ALU.add, ALU.mult).then_inc(ab_done, 1)
                    dve.wait_ge(st_mm, count(p, "stat") + 1)
                    dve.tensor_scalar(MSQ[:, 0:nt], MS7[:, 0:nt], 1.0 / D, EPS, ALU.mult, ALU.add).then_inc(ms_done, 1)
                    dve.wait_ge(bc_mm, count(p, "stat") + 1)

                    def scaled(k):
                        if k >= 2:
                            dve.wait_ge(ny_done, count(p, "ny") + k - 1)
                        dve.tensor_tensor(NT[:, k % 2, 0:tok], X[:, k, 0:tok], BC[:, 0:tok], ALU.mult) \
                            .then_inc(nt_done, 1)

                    scaled(0)
                    scaled(1)
                    for k in range(KD):
                        dve.wait_ge(xn_hi, count(p, "xh") + k + 1)
                        dve.tensor_tensor(XN[:, 1, k, 0:tok], NY[:, k % 2, 0:tok],
                                          XN[:, 0, k, 0:tok].bitcast(F32), ALU.subtract).then_inc(xn_lo, 1)
                        if k + 2 < KD:
                            scaled(k + 2)
                if kind == "ffn":
                    both = has_ctx("ffn", l, which)
                    tok = T if both else NLAT
                    gate = (NMOD * l + (2 if which == 0 else 8)) * KD
                    pending = None
                    for g, part, u0, e0, h0, n, q in parts(p, l, which):
                        piece = 8 * modules_before(p, l, which, g, part)
                        if pending is not None:
                            finish_module(*pending)
                            pending = None
                        if q is not None:
                            clear_sums(modules_before(p, l, which, g, part))
                            pending = (q, modules_before(p, l, which, g, part))
                        if part == "in":
                            with dve.Fori(0, n // 2) as it:
                                for j in range(2):
                                    c = 2 * it + j
                                    split_lo(u0 + j + 1, it)
                                    if q is not None:
                                        mod_piece(j, j, piece + j, it)
                                    a_lat, a_ctx, b_ctx, b_lat = set_views((e0 + j) % 2)
                                    dve.wait_ge(silu_done, count(p, "hidden") + h0 + j + 1 + 2 * it)
                                    dve.wait_ge(h_lo, count(p, "hidden") + h0 + j + 2 * it)
                                    ins = dve.tensor_tensor(HF[:, 0:NLAT], b_lat, SG[:, 0:NLAT], ALU.mult)
                                    if both:
                                        ins = dve.tensor_tensor(HF[:, NLAT:T], b_ctx, SG[:, NLAT:T], ALU.mult)
                                    ins.then_inc(evacuated, 1)
                                    dve.wait_ge(h_hi, count(p, "hidden") + h0 + j + 1 + 2 * it)
                                    dve.tensor_tensor(H[:, 1, ds(c, 1), 0:tok], HF[:, 0:tok].unsqueeze(1),
                                                      H[:, 0, ds(c, 1), 0:tok].bitcast(F32), ALU.subtract) \
                                        .then_inc(h_lo, 1)
                            continue
                        if g == 0:
                            dve.tensor_scalar(GG[:, :, :], MODS[:, gate:gate + KD, :], 0.5, None, ALU.mult) \
                                .then_inc(gate_ready, 1)
                            dve.wait_ge(gate_ready, 2 * l + which + 1)
                        for i in range(n):
                            u = u0 + i
                            if next_is_prefetched(p, u):
                                split_lo(u + 1)
                            if q is not None:
                                for j in range(2):
                                    mod_piece(j, 2 * i + j, piece + 2 * i + j)
                            products_done(dve, u)
                            a_lat, a_ctx, b_ctx, b_lat = set_views((e0 + i) % 2)
                            for b, lat, cx in ((0, a_lat, a_ctx), (1, b_lat, b_ctx)):
                                m = 2 * i + b
                                ins = dve.scalar_tensor_tensor(X[:, m, 0:NLAT], lat, GG[:, m, 0:1], X[:, m, 0:NLAT],
                                                               ALU.mult, ALU.add)
                                if both:
                                    ins = dve.scalar_tensor_tensor(X[:, m, NLAT:T], cx, GG[:, m, 1:2],
                                                                   X[:, m, NLAT:T], ALU.mult, ALU.add)
                            ins.then_inc(evacuated, 1)
                    if pending is not None:
                        finish_module(*pending)
                if kind == "mix":
                    dve_mix(dve, p, l, last, link, split_lo)
                if kind == "out":
                    u0, e0 = count(p, "units"), count(p, "evac")
                    split_lo(u0)
                    gate = (NMOD * l + 5) * KD
                    for m in range(KD):
                        u = u0 + m
                        if next_is_prefetched(p, u):
                            split_lo(u + 1)
                        products_done(dve, u)
                        a_lat, a_ctx, b_ctx, b_lat = set_views((e0 + m) % 2)
                        ins = dve.scalar_tensor_tensor(X[:, m, 0:NLAT], a_lat, MODS[:, gate + m, 0:1],
                                                       X[:, m, 0:NLAT], ALU.mult, ALU.add)
                        if not last:
                            ins = dve.scalar_tensor_tensor(X[:, m, NLAT:T], a_ctx, MODS[:, gate + m, 1:2],
                                                           X[:, m, NLAT:T], ALU.mult, ALU.add)
                        ins.then_inc(evacuated, 1)
            dve.wait_ge(f_sq, TLAT)
            dve.tensor_scalar(FMS[:, :], FSS[:, :], 1.0 / D, EPS, ALU.mult, ALU.add).then_inc(f_ms, 1)
            dve.wait_ge(f_rs, 1)
            dve.wait_ge(gf_in, 16)
            for t in range(TLAT):
                dve.wait_ge(f_t, TLAT + t + 1)
                dve.scalar_tensor_tensor(OUTB[:, t, :], PF[:, 1024 * (t % 2):1024 * (t % 2) + D], FRS[:, t:t + 1],
                                         GF[:, :], ALU.mult, ALU.mult).then_inc(f_n, 1)


        @block.tensor
        def _(pe):
            def passes(out_, wh, wl, xh, xl, first, final):
                pe.matmul(out_, wh, xl, start=first, stop=False)
                pe.matmul(out_, wl, xh, start=False, stop=False)
                return pe.matmul(out_, wh, xh, start=False, stop=final)

            def unit(u, e, xh, xl, chunks, both, it=None, wait_chunk=None, blocks=2, rows=None, col=None):
                dyn = 0 if it is None else 2 * it
                pe.wait_ge(w_split, u + 1 + dyn)
                if e >= 2:
                    pe.wait_ge(evacuated, e - 1 + dyn)
                a_lat, a_ctx, b_ctx, b_lat = set_views(e % 2)
                s = u % 2
                w = col or (lambda hl, k, b: ring(hl, s, k, b * P, P))
                ins = None
                for k in range(chunks):
                    if wait_chunk is not None:
                        wait_chunk(k)
                    f, z = k == 0, k == chunks - 1
                    r = P if rows is None else rows(k)
                    for b, lat in ((0, a_lat), (1, b_lat))[:blocks]:
                        ins = passes(lat, w(0, k, b)[0:r], w(1, k, b)[0:r], xh(k, 0)[0:r], xl(k, 0)[0:r], f, z)
                        if b == 0 and both:
                            ins = passes(a_ctx, w(0, k, b)[0:r], w(1, k, b)[0:r], xh(k, 1)[0:r], xl(k, 1)[0:r], f, z)
                if both and blocks == 2:
                    for k in range(chunks):
                        ins = passes(b_ctx, w(0, k, 1), w(1, k, 1), xh(k, 1), xl(k, 1), k == 0, k == chunks - 1)
                ins.then_inc(unit_done, 1)

            def stream(s):
                return slice(0, NLAT) if s == 0 else slice(NLAT, T)

            pe.wait_ge(cst, 5)
            pe.wait_ge(vrow_in, 144)
            pe.transpose(PS[:, 0, 0:P], VROW[:, 0, :], IDENT[:, :])
            pe.transpose(PS[:, 1, 0:P], VROW[:, 1, :], IDENT[:, :])
            pe.transpose(PS[:, 1, P:2 * P], VROW[:, 2, :], IDENT[:, :]).then_inc(vec_t, 1)
            pe.wait_ge(x_in, 32)
            for k in range(KD):
                if k >= 2:
                    pe.wait_ge(xt_ev, k - 1)
                b = 2048 if k % 2 else 1024
                for t in range(TT):
                    ins = pe.transpose(PF[:, b + t * P:b + (t + 1) * P], XLOAD[:, t, k * P:(k + 1) * P], IDENT[:, :])
                ins.then_inc(xt_mm, 1)
            pe.wait_ge(scv_done, 1)
            for i in range(12):
                pe.wait_ge(ms_landed[i % 6], 16 * (i // 6 + 1))
                for c in range(2):
                    o1 = 2 * (2 * i + c)
                    for k in range(KD):
                        ins = pe.matmul(PS[:, 0, o1:o1 + 2], MSW[:, i % 6, k, c * P:(c + 1) * P], SCV[:, k, :],
                                        start=k == 0, stop=k == KD - 1)
                ins.then_inc(ms_used, 1)

            for p, (kind, l, which) in enumerate(PHASES):
                last = l == DEPTH - 1
                if kind == "norm":
                    nt = (T if has_ctx("norm", l, which) else NLAT) // P
                    pe.wait_ge(ss_done, count(p, "ss") + KD)
                    pe.wait_ge(mod_ready, 1 + count(p, "fin"))
                    for t in range(nt):
                        ins = pe.matmul(MS7[:, t:t + 1], SS[:, t * P:(t + 1) * P], ONE[:, :], start=True, stop=True)
                    ins.then_inc(st_mm, 1)
                    pe.wait_ge(rstd_done, count(p, "stat") + 1)
                    for t in range(nt):
                        ins = pe.matmul(BC[:, t * P:(t + 1) * P], RST[:, t:t + 1].broadcast_to([P, P]), IDENT[:, :],
                                        start=True, stop=True)
                    ins.then_inc(bc_mm, 1)
                if kind == "ffn":
                    both = has_ctx("ffn", l, which)
                    xl0 = AT[p]["xl"]
                    pending = None

                    def finish_module(q, n):
                        pe.wait_ge(mac_done, 8 * (n + 1))
                        pe.wait_ge(mod_ready, n + 1)
                        for k in range(KD):
                            for v in range(2):
                                ins = pe.matmul(FN[:, 2 * k + v:2 * k + v + 1], ACC[:, v, k * P:(k + 1) * P],
                                                ONE[:, :], start=True, stop=True)
                        ins.then_inc(fin_mm, 1)

                    for g, part, u0, e0, h0, n, q in parts(p, l, which):
                        if pending is not None:
                            finish_module(*pending)
                            pending = None
                        if q is not None:
                            pending = (q, modules_before(p, l, which, g, part))
                        if part == "in":
                            xh = lambda k, s: XN[:, 0, k, stream(s)]
                            xl = lambda k, s: XN[:, 1, k, stream(s)]
                            lead = 0
                            if g == 0:
                                lead = 2
                                unit(u0, e0, xh, xl, KD, both,
                                     wait_chunk=lambda k: pe.wait_ge(xn_lo, xl0 - KD + k + 1))
                                unit(u0 + 1, e0 + 1, xh, xl, KD, both)
                            with pe.Fori(lead // 2, n // 2) as it:
                                for j in range(2):
                                    unit(u0 + j, e0 + j, xh, xl, KD, both, it)
                        else:
                            xh = lambda k, s: H[:, 0, k, stream(s)]
                            xl = lambda k, s: H[:, 1, k, stream(s)]
                            hid = count(p, "hidden") + h0
                            for i in range(n):
                                unit(u0 + i, e0 + i, xh, xl, GROUPS[g], both,
                                     wait_chunk=(lambda k: pe.wait_ge(h_lo, hid + k + 1)) if i == 0 else None)
                    if pending is not None:
                        finish_module(*pending)
                if kind == "mix":
                    pe_mix(pe, p, l, last, passes)
                if kind == "out":
                    u0, e0 = count(p, "units"), count(p, "evac")

                    def y_part(hl, k, s):
                        if k < 3:
                            return Y[:, hl, k, stream(s)]
                        if k < 5:
                            return YB[:, hl, k - 3, stream(s)]
                        return Y[:, hl, k - 2, stream(s)]

                    for m in range(KD):
                        slot = (u0 + m) % 2
                        unit(u0 + m, e0 + m, lambda k, s: y_part(0, k, s), lambda k, s: y_part(1, k, s), 9, not last,
                             blocks=1, rows=lambda k: P if k < 5 else DV,
                             col=lambda hl, k, b: R[:, hl, slot, k * P:(k + 1) * P])
            pe.wait_ge(evacuated, TOTAL["evac"])
            for r in range(2):
                for t in range(TLAT):
                    if r or t >= 2:
                        if 4 * r + t - 2 < TLAT:
                            pe.wait_ge(f_sq, 4 * r + t - 1)
                        else:
                            pe.wait_ge(f_n, 4 * r + t - 1 - TLAT)
                    for k in range(KD):
                        ins = pe.transpose(PF[:, 1024 * (t % 2) + k * P:1024 * (t % 2) + (k + 1) * P],
                                           X[:, k, t * P:(t + 1) * P], IDENT[:, :])
                    ins.then_inc(f_t, 1)


_INS = ["x", "c", "ctx", "c_ctx", "w_mod", "b_mod", "g_ffn1", "w_ffn1_in", "w_ffn1_out", "g_mix", "w_mix_in",
        "w_mix_out", "g_qnorm", "g_knorm", "g_vnorm", "w_spatial", "b_spatial", "lambda_vecs", "g_subln", "g_ffn2",
        "w_ffn2_in", "w_ffn2_out", "g_final"]
GRID_W = 64
ROPE_BASE = 10000.0


def rope_tables(d):
    half, m = d // 2, d // 4
    freqs = (1.0 / ROPE_BASE ** (np.arange(0, half, 2, dtype=np.float32) / half)).astype(np.float32)
    tokens = np.arange(NLAT)
    out = np.empty((2, NLAT, d), np.float32)
    for axis, pos in enumerate((tokens // GRID_W, tokens % GRID_W)):
        ang = (pos.astype(np.float32)[:, None] * freqs).astype(np.float32)
        o = axis * half
        out[0, :, o:o + half] = np.concatenate([np.cos(ang), np.cos(ang)], 1)
        out[1, :, o:o + half] = np.concatenate([-np.sin(ang), np.sin(ang)], 1)
    return np.ascontiguousarray(out.reshape(2, TLAT, P, d).transpose(0, 2, 1, 3))


def kernel(**inputs):
    import concourse.bacc as _bacc
    from concourse.bass_utils import run_bass_kernel_spmd as _run

    nc = _bacc.Bacc("TRN2", target_bir_lowering=False, num_devices=1)
    arrays = {name: np.ascontiguousarray(inputs[name]) for name in _INS}
    arrays["rope_a"], arrays["rope_c"] = rope_tables(DA), rope_tables(DC)
    A = {name: nc.dram_tensor(name, a.shape, mybir.dt.from_np(a.dtype), kind="ExternalInput").ap()
         for name, a in arrays.items()}
    out = nc.dram_tensor("out", (1, NLAT, D), F32, kind="ExternalOutput").ap()
    build(nc, A, out)
    return _run(nc, [arrays], core_ids=[0]).results[0]["out"]
```

```python
from contextlib import ExitStack
import math

import numpy as np

import concourse.bass as bass
from concourse import mybir

F32 = mybir.dt.float32
F32R = mybir.dt.float32r
ALU = mybir.AluOpType
ACT = mybir.ActivationFunctionType
AX = mybir.AxisListType
ds = bass.ds

P = 128
D = 1024
KD = D // P
NLAT, NCTX = 512, 256
T = NLAT + NCTX
TT = T // P
TLAT = NLAT // P
DEPTH = 2
D_FF = 2816
FFC = D_FF // P
GROUPS = (8, 8, 6)
NMOD = 9
EPS = 1e-6
HA, KVA, DA = 6, 2, 64
HC, DC, DV = 4, 48, 96
SLOT = 2048
IN_W = 2304
COLS = {"qa": 0, "ka": 384, "va": 512, "u": 640, "v": 896, "qc": 1152, "kc": 1536, "vc": 1920}
MIX_UNITS = ("v", "u", "va_vc", "vc", "qa", "qa_ka", "c0", "c1", "c2")
MIX_PIECES = {
    "v": [(COLS["v"], 256)], "u": [(COLS["u"], 256)],
    "va_vc": [(COLS["va"], 128), (COLS["vc"], 128)], "vc": [(COLS["vc"] + 128, 256)],
    "qa": [(COLS["qa"], 256)], "qa_ka": [(COLS["qa"] + 256, 256)],
    "c0": [(COLS["qc"], 256)], "c1": [(COLS["qc"] + 256, 256)], "c2": [(COLS["qc"] + 512, 256)],
}
NMU = len(MIX_UNITS)
SC_A = DA ** -0.5
SC_C = DC ** -0.5
FFN_UNITS = sum(GROUPS) + 4 * len(GROUPS)


def mix_tiles(unit, last):
    return TLAT if last and unit in ("v", "u", "qa", "c0") else TT


def plan_phases():
    phases = [("start", 0, 0)]
    for l in range(DEPTH):
        phases += [("norm", l, 0), ("ffn", l, 0), ("norm", l, 1), ("mix", l, 0), ("out", l, 0),
                   ("norm", l, 2), ("ffn", l, 1)]
    return phases


def has_ctx(kind, l, which):
    last = l == DEPTH - 1
    if not last:
        return True
    return {"norm": which < 2, "ffn": which == 0, "mix": True, "out": False}[kind]


def background(l, which):
    first = {(0, 0): 3, (0, 1): 8, (1, 0): 13}.get((l, which))
    return [] if first is None else list(range(first, first + 5))


def module_slots(l, which):
    mods = background(l, which)
    if not mods:
        return [None] * 6
    return [mods[0], mods[1], mods[2], mods[3], None, mods[4]]


class Attention:

    def __init__(self, last):
        groups = [(0, 1), (2, 3)] if last else [(0, 1), (2, 3), (4, 5)]
        self.units, self.groups = [], []
        for part, heads in (("A", HA), ("C", HC)):
            for h in range(heads):
                for tiles in groups:
                    for t in tiles:
                        self.units.append((part, h, len(self.groups), t))
                    self.groups.append((part, h, tiles, len(self.units) - 1))
        self.n, self.ng, self.na = len(self.units), len(self.groups), HA * 2 * len(groups)
        self.nga = HA * len(groups)
        self.steps = range(-3, self.n + 5)
        per = 2 * len(groups)
        self.first_preps = [("A", "k", 0), ("A", "q", 0)]
        self.preps = {1: [("A", "q", 1)], 3: [("A", "q", 2)],
                      2 * per: [("C", "k", 0)], 2 * per + 1: [("C", "q", 0)]}
        for h in range(1, HC):
            f = self.na + (h - 1) * per
            self.preps[f - 2] = [("C", "k", h)]
            self.preps[f] = [("C", "q", h)]
        self.half, n = {}, 0
        for job in self.first_preps:
            self.half[job] = n
            n += 2
        for i in self.steps:
            for job in self.preps.get(i, []) + ([i + 1] if 0 <= i + 1 < self.n else []):
                self.half[job] = n
                n += 2
        self.halves = n

    def job(self, i):
        return i if i < self.na else 2 * i - self.na

    def comps(self, i):
        return 1 if i < self.na else 2

    def keys(self, i):
        return (T, 0) if self.units[i][3] < TLAT else (NCTX, NLAT)

    def parts(self, i):
        nk, k0 = self.keys(i)
        m = nk // P // 2
        return [(self.half[i] + b, k0 // P + b * m, m) for b in range(2)]

    def prob_buf(self, i, c):
        return 3 if c else i % 3

    def col(self, i, c):
        return i % 4 if i < self.na else 2 * (i % 2) + c

    def score_buf(self, i, c):
        return i % 2 if i < self.na else c

    def ends(self, i, r):
        for g, x in enumerate(self.groups):
            if x[3] == i - r:
                return g
        return None

    def needs(self, i):
        part, h = self.units[i][:2]
        return max(self.half[(part, "k", 0 if part == "A" else h)],
                   self.half[(part, "q", h // 2 if part == "A" else h)]) + 2


def adds(kind, l, which):
    last = l == DEPTH - 1
    a = {}
    if kind == "norm":
        a = dict(ss=KD, sq=KD - 1, stat=1, nt=KD, ny=KD, xh=KD, xl=KD)
    if kind == "ffn":
        nmod = len(background(l, which))
        a = dict(units=FFN_UNITS, evac=FFN_UNITS, hidden=FFC, mac=8 * nmod, fin=nmod)
    if kind == "mix":
        ntile = sum(mix_tiles(u, last) for u in MIX_UNITS)
        nlo = sum(mix_tiles(u, last) for u in ("va_vc", "vc"))
        att = Attention(last)
        a = dict(units=NMU, mix_mm=ntile, mix_lo=nlo, layer=1, v_tiles=TLAT if last else TT, spatial=4, yb=2,
                 score=att.na + 2 * (att.n - att.na), tile=att.n, half=att.halves, group=att.ng,
                 yc=att.ng - att.nga)
    if kind == "out":
        a = dict(units=KD, evac=KD)
    return a


PHASES = plan_phases()
AT = []
_run = {}
for _ph in PHASES:
    AT.append(dict(_run))
    for _k, _v in adds(*_ph).items():
        _run[_k] = _run.get(_k, 0) + _v
TOTAL = dict(_run)


def plan_units():
    dmas, words, done = [], [], []
    units, tiles = 1, 0
    for kind, l, which in PHASES:
        if kind == "ffn":
            for g in GROUPS:
                words += [((P, 0, SLOT),)] * g + [((P, 0, g * 256),)] * 4
                dmas += [2] * (g + 4)
                for _ in range(g + 4):
                    units += 1
                    done.append(("unit_done", units))
        if kind == "mix":
            for u in MIX_UNITS:
                tiles += mix_tiles(u, l == DEPTH - 1)
                dmas, words, done = dmas + [2], words + [((P, 0, SLOT),)], done + [("mix_mm", tiles)]
        if kind == "out":
            for _ in range(KD):
                units += 1
                dmas, words, done = dmas + [4], words + [((P, 0, 5 * P), (DV, 5 * P, 9 * P))], done + [("unit_done", units)]
    return dmas, words, done


UNIT_DMAS, UNIT_WORDS, UNIT_DONE = plan_units()
LANDED = [16 * sum(UNIT_DMAS[u % 2:u + 1:2]) for u in range(len(UNIT_DMAS))]


def c_pieces(unit):
    out = []
    col, end = 256 * unit, 256 * unit + 256
    while col < end:
        b, r = divmod(col, HC * DC)
        h, j = divmod(r, DC)
        stop = min(end, (b + 1) * HC * DC)
        if j or stop - col < DC:
            hn, jn = 1, min(DC - j, stop - col)
        else:
            hn, jn = (stop - col) // DC, DC
        out.append((col - 256 * unit, 8 * (b // 2) + 2 * h + b % 2, hn, j, jn))
        col += hn * jn
    return out


def build(nc, A, out):
    with ExitStack() as ctx:
        base = (nc.sbuf_base + 31) // 32 * 32
        top = nc.sbuf_usable_end

        def at(name, shape, dt, offset):
            n = 4
            for s in shape[1:]:
                n *= s
            assert base + offset + n <= top, (name, offset + n, top - base)
            return nc.alloc_sbuf_tensor_at(name, shape, dt, offset=base + offset)

        o = 0
        X = at("X", [P, KD, T], F32, o); o += 4 * KD * T
        XN_AT = o; o += 8 * KD * T
        R_AT = o; o += 16 * SLOT
        ST_AT = o; o += 8 * SLOT
        M_AT = o
        XN = at("XN", [P, 2, KD, T], F32R, XN_AT)
        XLOAD = at("XLOAD", [P, TT, D], F32, XN_AT)
        R = at("R", [P, 2, 2, SLOT], F32R, R_AT)
        ST = at("ST", [P, 2, SLOT], F32, ST_AT)
        H = at("H", [P, 2, GROUPS[0], T], F32R, M_AT)
        SG = at("SG", [P, T], F32, M_AT + 49152)
        HF = at("HF", [P, T], F32, M_AT + 52224)
        ACC = at("ACC", [P, 2, D], F32, M_AT + 55296)
        MW = at("MW", [P, 2, D], F32, M_AT + 63488)
        NT = at("NT", [P, 2, T], F32, M_AT)
        NY = at("NY", [P, 2, T], F32, M_AT + 8 * T)
        MSW = at("MSW", [P, 6, KD, 256], F32, M_AT)
        VROW = at("VROW", [P, 3, P], F32, M_AT + 55296)
        QA = at("QA", [P, TT, 512], F32, M_AT)
        QC = at("QC", [P, TT, 16, 64], F32, M_AT + 12288)
        VA = at("VA", [P, 2, TT, 128], F32R, M_AT + 36864)
        VC = at("VC", [P, 2, TT, 384], F32R, M_AT + 43008)
        YB = at("YB", [P, 2, 2, T], F32R, M_AT + 61440)
        U = at("U", [P, TT, 256], F32, M_AT)
        VN = at("VN", [P, 2, TT, 256], F32R, M_AT + 6144)
        VJ = at("VJ", [P, TT, 256], F32, M_AT + 6144)
        VF = at("VF", [P, TT, 256], F32, M_AT + 18432)
        WST = at("WST", [P, 2, 4, P], F32R, M_AT + 73728)
        WSR = at("WSR", [P, 4, P], F32, M_AT + 24576)
        ROT = at("ROT", [P, 2, 768], F32, M_AT + 73728)
        SS = at("SS", [P, T], F32, M_AT + 73728)
        SQ = at("SQ", [P, T], F32, M_AT + 73728 + 4 * T)
        Y = at("Y", [P, 2, 7, T], F32R, XN_AT)
        K0 = at("K0", [P, 2, T], F32R, XN_AT + 43008)
        PT = at("PT", [P, 2, 2, TT, 2 * P], F32R, R_AT)
        K1 = at("K1", [P, 2, T], F32R, R_AT + 24576)
        Q0 = at("Q0", [P, 2, T], F32R, M_AT + 73728)
        Q1 = at("Q1", [P, 2, T], F32R, M_AT + 36864)
        QB = at("QB", [P, 2, 2, T], F32R, XN_AT + 3 * 4 * T)
        K23 = at("K23", [P, 2, 2, T], F32R, M_AT)
        PB = at("PB", [P, 4, T], F32, ST_AT)
        YRAW = at("YRAW", [P, 2, 2 * P], F32, ST_AT + 12288)
        YSQ = at("YSQ", [P, 2, 2 * P], F32, ST_AT + 14336)
        OUTB = at("OUTB", [P, 4, D], F32, XN_AT)
        OJ = at("OJ", [P, 2, D], F32, XN_AT + 16384)
        GF = at("GF", [P, D], F32, XN_AT + 24576)

        o = M_AT + 73728 + 8 * T

        def const(name, shape, dt=F32):
            nonlocal o
            t = at(name, shape, dt, o)
            n = 4
            for s in shape[1:]:
                n *= s
            o += (n + 31) // 32 * 32
            return t

        IDENT = const("IDENT", [P, P])
        ONE = const("ONE", [P, 1])
        NEGH = const("NEGH", [P, 48])
        VEC = const("VEC", [P, 80])
        BM = const("BM", [P, 18 * KD])
        SCV = const("SCV", [P, KD, 2])
        MODS = const("MODS", [P, 18 * KD, 2])
        AA = const("AA", [P, KD, 2])
        GG = const("GG", [P, KD, 2])
        ROPA = const("ROPA", [P, 2, TLAT, DA])
        ROPC = const("ROPC", [P, 2, TLAT, DC])
        GQK = const("GQK", [P, 2, DA])
        GV = const("GV", [P, 256])
        GS = const("GS", [P, 1])
        RST = const("RST", [P, 8])
        MSQ = const("MSQ", [P, 8])
        SM = const("SM", [P, 64])
        LV = at("LV", [P, 4, DC], F32, M_AT + 24576 + 2048)
        LVP = at("LVP", [P, 2, DC], F32, M_AT + 24576 + 2048 + 768)
        LM = const("LM", [P, 8])
        AST = const("AST", [P, TT, 8])
        ASR = const("ASR", [P, TT, 8])
        VSS = const("VSS", [P, 8])
        VSR = const("VSR", [P, 8])
        VMS = const("VMS", [P, 8])
        AMS = const("AMS", [P, TT, 8])
        YMS = const("YMS", [P, 4])
        YRS = const("YRS", [P, 4])
        FSS = const("FSS", [P, TLAT])
        FMS = const("FMS", [P, TLAT])
        FRS = const("FRS", [P, TLAT])

        PS = ctx.enter_context(nc.psum_tensor("PS", [P, 8, 512], F32))
        PF = PS[:, :, :].rearrange("p b n -> p (b n)")

        sems = {}

        def sem(name):
            s = ctx.enter_context(nc.semaphore(name))
            sems[name] = s
            return s

        w_landed = [sem("w_landed0"), sem("w_landed1")]
        w_hi, w_split, unit_done, evacuated = sem("w_hi"), sem("w_split"), sem("unit_done"), sem("evacuated")
        mw_landed = [sem("mw_landed0"), sem("mw_landed1")]
        ms_landed = [sem(f"ms_landed{i}") for i in range(6)]
        ms_used, mac_done, acc_clear, fin_mm, mod_ready = (sem("ms_used"), sem("mac_done"), sem("acc_clear"),
                                                           sem("fin_mm"), sem("mod_ready"))
        gate_ready = sem("gate_ready")
        silu_done, h_hi, h_lo = sem("silu_done"), sem("h_hi"), sem("h_lo")
        sq_done, ss_done, st_mm, ms_done, rstd_done = (sem("sq_done"), sem("ss_done"), sem("st_mm"),
                                                       sem("ms_done"), sem("rstd_done"))
        bc_mm, nt_done, ny_done, xn_hi, xn_lo, ab_done = (sem("bc_mm"), sem("nt_done"), sem("ny_done"),
                                                          sem("xn_hi"), sem("xn_lo"), sem("ab_done"))
        cst, vrow_in, vec_t, vec_ev, scv_done = (sem("cst"), sem("vrow_in"), sem("vec_t"), sem("vec_ev"),
                                                 sem("scv_done"))
        x_in, xt_mm, xt_ev, rope_in, layer_in = (sem("x_in"), sem("xt_mm"), sem("xt_ev"), sem("rope_in"),
                                                 sem("layer_in"))
        mix_mm, mix_act, mix_lo = sem("mix_mm"), sem("mix_act"), sem("mix_lo")
        ws_t, ws_hi, ws_lo = sem("ws_t"), sem("ws_hi"), sem("ws_lo")
        v_sq, v_ms, v_rstd, v_n, v_hi, v_lo = (sem("v_sq"), sem("v_ms"), sem("v_rstd"), sem("v_n"), sem("v_hi"),
                                               sem("v_lo"))
        sp_mm, sp_ev, yb_t, yb_hi, yb_lo, pad_done = (sem("sp_mm"), sem("sp_ev"), sem("yb_t"), sem("yb_hi"),
                                                      sem("yb_lo"), sem("pad_done"))
        a_ms, a_rstd, qk_c, lam_e, dve_step = (sem("a_ms"), sem("a_rstd"), sem("qk_c"),
                                                     sem("lam_e"), sem("dve_step"))
        lam_v = sem("lam_v")
        s_mm, mx_done, ex_done, p_done, t_mm, t_hi, t_lo = (sem("s_mm"), sem("mx_done"), sem("ex_done"),
                                                            sem("p_done"), sem("t_mm"), sem("t_hi"), sem("t_lo"))
        pv_mm, y_hi, y_lo = sem("pv_mm"), sem("y_hi"), sem("y_lo")
        yr_done, yst_mm, yms_done, yrs_done, ybc_mm, yn_done = (sem("yr_done"), sem("yst_mm"), sem("yms_done"),
                                                                sem("yrs_done"), sem("ybc_mm"), sem("yn_done"))
        f_t, f_sq, f_ms, f_rs, f_n, out_done, gf_in, out_in = (sem("f_t"), sem("f_sq"), sem("f_ms"), sem("f_rs"),
                                                               sem("f_n"), sem("out_done"), sem("gf_in"),
                                                               sem("out_in"))

        wmod = A["w_mod"].rearrange("l (k p) n -> l p k n", p=P)
        w_in = {0: A["w_ffn1_in"], 1: A["w_ffn2_in"]}
        w_in = {i: w.rearrange("l (k p) n -> l p k n", p=P) for i, w in w_in.items()}
        w_out = {0: A["w_ffn1_out"], 1: A["w_ffn2_out"]}
        w_out = {i: w.rearrange("l (k p) n -> l p k n", p=P) for i, w in w_out.items()}
        w_mi = A["w_mix_in"].rearrange("l (k p) n -> l p k n", p=P)
        w_mo = A["w_mix_out"]
        stv = ST[:, :, :].rearrange("p s (k c) -> p s k c", c=256)
        MS7 = PF[:, 3840:3848]
        BC = PF[:, 3072:3072 + T]
        FN = PF[:, 3856:3872]

        def ring(hl, slot, k, c0, n):
            return R[:, hl, slot, k * 256 + c0:k * 256 + c0 + n]

        def set_views(s):
            return (PS[:, 3 * s, :], PS[:, 3 * s + 1, 0:256], PS[:, 3 * s + 1, 256:512], PS[:, 3 * s + 2, :])

        def c_k(h):
            return (K23[:, 0], K23[:, 1]) if h % 2 == 0 else (K0, K1)

        def c_q(h):
            q = Q0 if h % 2 == 0 else Q1
            return q[:, 0, :], q[:, 1, :]

        def prep_dst(job):
            part, what, h = job
            if what == "k":
                return (K0, K1) if part == "A" else c_k(h)
            if part == "C":
                return c_q(h)
            q = Q0 if h == 0 else QB[:, h - 1]
            return q[:, 0, :], q[:, 1, :]

        def half_bank(n, m):
            return PS[:, 4 + n % 2, 0:m * P]

        def y_places(att, g):
            part, h, tiles, _ = att.groups[g]
            return part, h, slice(tiles[0] * P, (tiles[-1] + 1) * P), 6 + g % 2

        def prep_tiles(att, job):
            nt = TT if job[1] == "k" or att.ng > 20 else TLAT
            return [(att.half[job] + b, b * (nt // 2), nt // 2) for b in range(2)]

        def products_done(eng, u, it=None):
            name, value = UNIT_DONE[u] if u >= 0 else ("unit_done", u + 2)
            eng.wait_ge(sems[name], value if it is None else value + 2 * it)

        def parts(p, l, which):
            u, e, h, m, n = AT[p].get("units", 0), AT[p].get("evac", 0), 0, 0, 0
            out_ = []
            slots = module_slots(l, which)
            for g, size in enumerate(GROUPS):
                out_.append((g, "in", u, e, h, size, slots[2 * g]))
                u, e = u + size, e + size
                out_.append((g, "out", u, e, h, 4, slots[2 * g + 1]))
                u, e, h = u + 4, e + 4, h + size
            return out_

        def count(p, key):
            return AT[p].get(key, 0)

        def modules_before(p, l, which, g, part):
            n = count(p, "fin")
            for i, m in enumerate(module_slots(l, which)):
                if i >= 2 * g + (part == "out"):
                    break
                n += m is not None
            return n

        def next_is_prefetched(p, u):
            nxt = u + 1
            if nxt >= TOTAL["units"]:
                return False
            return not any(ph[0] == "out" and AT[i]["units"] == nxt for i, ph in enumerate(PHASES))

        block = ctx.enter_context(nc.Block())

        @block.sync
        def _(sp):
            def slot_free(u, value=None):
                if u >= 2 or value is not None:
                    sp.wait_ge(w_split, (u - 1) if value is None else value)

            def mod_piece(q, k, slot, piece, it=None):
                if piece >= 2 or it is not None:
                    sp.wait_ge(mac_done, piece if it is None else piece + 2 * it)
                l_, j = divmod(q, NMOD)
                src = wmod[l_, :, k, j * D:(j + 1) * D] if it is None else \
                    A["w_mod"][l_, ds((2 * it + k) * P, P), j * D:(j + 1) * D]
                sp.dma_start(MW[:, slot, :], src).then_inc(mw_landed[slot], 16)

            sp.wait_ge(cst, 1)
            for r0, n, src in ((0, 8, A["c"].rearrange("b (k p) -> (b k) p", p=P)),
                               (8, 8, A["c_ctx"].rearrange("(k p) -> k p", p=P)),
                               (16, 16, A["g_ffn1"].rearrange("l (k p) -> (l k) p", p=P)),
                               (32, 16, A["g_mix"].rearrange("l (k p) -> (l k) p", p=P)),
                               (48, 16, A["g_ffn2"].rearrange("l (k p) -> (l k) p", p=P)),
                               (64, 8, A["b_spatial"].rearrange("l g p -> (l g) p"))):
                sp.dma_start(VROW[r0:r0 + n, 0, :], src).then_inc(vrow_in, 16)
            sp.dma_start(VROW[72:74, 0, 0:DV], A["g_subln"]).then_inc(vrow_in, 16)
            for l in range(DEPTH):
                sp.dma_start(VROW[0:72, 1 + l, :], A["b_mod"][l].rearrange("(k p) -> k p", p=P)).then_inc(vrow_in, 16)
            sp.dma_start(XLOAD[:, 0:TLAT, :], A["x"].rearrange("b (t p) d -> p (b t) d", p=P)).then_inc(x_in, 16)
            sp.dma_start(XLOAD[:, TLAT:TT, :], A["ctx"].rearrange("b (t p) d -> p (b t) d", p=P)).then_inc(x_in, 16)
            for i in range(12):
                if i >= 6:
                    sp.wait_ge(ms_used, i - 5)
                sp.dma_start(MSW[:, i % 6, :, :], wmod[0, :, :, i * 256:(i + 1) * 256]).then_inc(ms_landed[i % 6], 16)
            for i in range(2):
                sp.dma_start(ROPA[:, i, :, :], A["rope_a"][i]).then_inc(rope_in, 16)
                sp.dma_start(ROPC[:, i, :, :], A["rope_c"][i]).then_inc(rope_in, 16)

            for p, (kind, l, which) in enumerate(PHASES):
                if kind == "ffn":
                    wi, wo = w_in[which][l], w_out[which][l]
                    for g, part, u0, e0, h0, n, q in parts(p, l, which):
                        piece = 8 * modules_before(p, l, which, g, part)
                        if part == "in":
                            def in_weights(u, h, j, it=None):
                                slot_free(u, None if it is None else u - 1 + 2 * it)
                                c0 = h * P if it is None else (2 * it + h) * P
                                for b in range(2):
                                    sp.dma_start(stv[:, u % 2, :, b * P:(b + 1) * P], wi[:, :, ds(c0 + b * D_FF, P)]) \
                                        .then_inc(w_landed[u % 2], 16)

                            for j in range(2):
                                in_weights(u0 + j, h0 + j, j)
                            if q is not None:
                                if g == 0 and u0:
                                    products_done(sp, u0 - 1)
                                for j in range(2):
                                    mod_piece(q, j, j, piece + j)
                            with sp.Fori(1, n // 2) as it:
                                for j in range(2):
                                    in_weights(u0 + j, h0 + j, j, it)
                                    if q is not None:
                                        mod_piece(q, j, j, piece + j, it)
                        else:
                            for i in range(n):
                                u = u0 + i
                                slot_free(u)
                                k = GROUPS[g] // 2
                                for b in range(2):
                                    sp.dma_start(stv[:, u % 2, b * k:(b + 1) * k, :],
                                                 wo[:, h0 + b * k:h0 + (b + 1) * k, i * 256:(i + 1) * 256]) \
                                        .then_inc(w_landed[u % 2], 16)
                                if q is not None:
                                    for j in range(2):
                                        mod_piece(q, 2 * i + j, j, piece + 2 * i + j)
                if kind == "mix":
                    u0 = count(p, "units")
                    for w, name in enumerate(MIX_UNITS):
                        u = u0 + w
                        slot_free(u)
                        if len(MIX_PIECES[name]) == 1:
                            c0, n = MIX_PIECES[name][0]
                            for b in (slice(0, KD // 2), slice(KD // 2, KD)):
                                sp.dma_start(stv[:, u % 2, b, :], w_mi[l, :, b, c0:c0 + n]) \
                                    .then_inc(w_landed[u % 2], 16)
                        else:
                            for i, (c0, n) in enumerate(MIX_PIECES[name]):
                                sp.dma_start(stv[:, u % 2, :, i * P:(i + 1) * P], w_mi[l, :, :, c0:c0 + n]) \
                                    .then_inc(w_landed[u % 2], 16)
                        if w == 1:
                            products_done(sp, u0 - 1)
                            sp.dma_start(GQK[:, 0, :], A["g_qnorm"][l].partition_broadcast(P)).then_inc(layer_in, 16)
                            sp.dma_start(GQK[:, 1, :], A["g_knorm"][l].partition_broadcast(P)).then_inc(layer_in, 16)
                            sp.dma_start(GV[:, :], A["g_vnorm"][l].partition_broadcast(P)).then_inc(layer_in, 16)
                            sp.dma_start(WSR[:, :, :], A["w_spatial"][l].rearrange("g p q -> p g q")) \
                                .then_inc(layer_in, 16)
                            sp.dma_start(LV[:, :, :], A["lambda_vecs"][l].partition_broadcast(P)).then_inc(layer_in, 16)
                if kind == "out":
                    u0 = count(p, "units")
                    sp.wait_ge(y_lo, count(p, "group"))
                    for m in range(KD):
                        u = u0 + m
                        slot_free(u)
                        dst = ST[:, u % 2, 0:9 * P].rearrange("p (k c) -> p k c", c=P)
                        cols = slice(m * P, (m + 1) * P)
                        for b in range(2):
                            src = w_mo[l, b * 192:(b + 1) * 192, cols].rearrange("(j r) c -> r j c", r=DA)
                            sp.dma_start(dst[b * 64:(b + 1) * 64, 0:3, :], src).then_inc(w_landed[u % 2], 16)
                        src = w_mo[l, 384:640, cols].rearrange("(j r) c -> r j c", r=P)
                        sp.dma_start(dst[:, 3:5, :], src).then_inc(w_landed[u % 2], 16)
                        src = w_mo[l, 640:1024, cols].rearrange("(j r) c -> r j c", r=DV)
                        sp.dma_start(dst[0:DV, 5:9, :], src).then_inc(w_landed[u % 2], 16)
            products_done(sp, TOTAL["units"] - 1)
            sp.dma_start(GF[:, :], A["g_final"].partition_broadcast(P)).then_inc(gf_in, 16)
            for t in range(TLAT):
                sp.wait_ge(f_n, t + 1)
                sp.dma_start(out[0, t * P:(t + 1) * P, :], OUTB[:, t, :]).then_inc(out_done, 16)
            sp.wait_ge(out_done, 16 * TLAT)

        @block.gpsimd
        def _(pool):
            pool.memset(VROW[:, :, :], 0.0).then_inc(cst, 1)
            pool.memset(IDENT[:, :], 0.0).then_inc(cst, 1)
            pool.memset(ONE[:, :], 1.0).then_inc(cst, 1)
            pool.memset(NEGH[:, :], -0.5).then_inc(cst, 1)
            pool.wait_ge(cst, 4)
            pool.affine_select(out=IDENT[:, :], in_=IDENT[:, :], compare_op=ALU.not_equal, fill=1.0, base=0,
                               pattern=[[-1, P]], channel_multiplier=1).then_inc(cst, 1)
            for p, (kind, l, which) in enumerate(PHASES):
                if kind == "norm":
                    tok = T if has_ctx("norm", l, which) else NLAT
                    prev = PHASES[p - 1]
                    for k in range(KD):
                        if prev[0] == "start":
                            pool.wait_ge(xt_ev, k + 1)
                        elif prev[0] == "out":
                            pool.wait_ge(evacuated, count(p, "evac") - KD + k + 1)
                        else:
                            pool.wait_ge(evacuated, count(p, "evac") - 4 + k // 2 + 1)
                        if k == 0:
                            pool.tensor_tensor(SS[:, 0:tok], X[:, 0, 0:tok], X[:, 0, 0:tok], ALU.mult) \
                                .then_inc(ss_done, 1)
                            continue
                        pool.wait_ge(ss_done, count(p, "ss") + k)
                        pool.tensor_tensor(SQ[:, 0:tok], X[:, k, 0:tok], X[:, k, 0:tok], ALU.mult).then_inc(sq_done, 1)
                        pool.wait_ge(sq_done, count(p, "sq") + k)
                        pool.tensor_tensor(SS[:, 0:tok], SS[:, 0:tok], SQ[:, 0:tok], ALU.add).then_inc(ss_done, 1)
                    pool.wait_ge(ms_done, count(p, "stat") + 1)
                    nt = tok // P
                    pool.tensor_tensor(RST[:, 0:nt], MSQ[:, 0:nt], NEGH[:, 0:nt], ALU.pow).then_inc(rstd_done, 1)
                if kind == "mix":
                    last = l == DEPTH - 1
                    ntq = TLAT if last else TT
                    pool.wait_ge(v_ms, l + 1)
                    pool.tensor_tensor(VSR[:, 0:ntq], VMS[:, 0:ntq], NEGH[:, 0:ntq], ALU.pow).then_inc(v_rstd, 1)
                    pool.wait_ge(yb_t, count(p, "yb") + 2)
                    pool.memset(QC[:, :, :, DC:64], 0.0).then_inc(pad_done, 1)
                    pool.wait_ge(a_ms, l + 1)
                    pool.tensor_tensor(ASR[:, :, :], AMS[:, :, :], NEGH[:, :].rearrange("p (t h) -> p t h", h=8),
                                       ALU.pow).then_inc(a_rstd, 1)
                    att = Attention(last)
                    for g in range(att.ng - att.nga):
                        pool.wait_ge(yms_done, count(p, "yc") + g + 1)
                        b = 2 * ((att.nga + g) % 2)
                        pool.tensor_tensor(YRS[:, b:b + 2], YMS[:, b:b + 2], NEGH[:, 0:2], ALU.pow) \
                            .then_inc(yrs_done, 1)
            pool.wait_ge(f_ms, 1)
            pool.tensor_tensor(FRS[:, :], FMS[:, :], NEGH[:, 0:TLAT], ALU.pow).then_inc(f_rs, 1)

        def dve_mix(dve, p, l, last, link, split_lo):
            u0, n0, lo0 = count(p, "units"), count(p, "mix_mm"), count(p, "mix_lo")
            ntq = TLAT if last else TT
            tok = NLAT if last else T
            n = lo = 0
            for w, name in enumerate(MIX_UNITS):
                if w + 1 < NMU:
                    split_lo(u0 + w + 1)
                tiles = mix_tiles(name, last)
                if name == "v":
                    dve.wait_ge(layer_in, 80 * (l + 1))
                    link(dve.tensor_tensor(LVP[:, :, :], LV[:, 0:4:2, :], LV[:, 1:4:2, :], ALU.mult))
                    dve.tensor_reduce(LM[:, 0:2], LVP[:, :, :], AX.X, ALU.add).then_inc(lam_v, 1)
                    dve.wait_ge(ws_hi, l + 1)
                    dve.tensor_tensor(WST[:, 1, :, :], PS[:, 6, :].rearrange("p (g q) -> p g q", g=4),
                                      WST[:, 0, :, :].bitcast(F32), ALU.subtract).then_inc(ws_lo, 1)
                if name == "u":
                    dve.wait_ge(v_sq, count(p, "v_tiles") + ntq)
                    dve.tensor_scalar(VMS[:, 0:ntq], VSS[:, 0:ntq], 1.0 / 256, EPS, ALU.mult, ALU.add) \
                        .then_inc(v_ms, 1)
                    dve.wait_ge(v_rstd, l + 1)
                    for t in range(ntq):
                        ins = dve.scalar_tensor_tensor(VF[:, t, :], VF[:, t, :], VSR[:, t:t + 1], GV[:, :],
                                                       ALU.mult, ALU.mult)
                    ins.then_inc(v_n, 1)
                    dve.wait_ge(v_hi, l + 1)
                    dve.tensor_tensor(VN[:, 1, 0:ntq, :], VF[:, 0:ntq, :], VN[:, 0, 0:ntq, :].bitcast(F32),
                                      ALU.subtract).then_inc(v_lo, 1)
                if name in ("va_vc", "vc"):
                    for t in range(tiles):
                        dve.wait_ge(mix_act, n0 + n + t + 1)
                        b = PS[:, (n + t) % 6, 0:256]
                        if name == "va_vc":
                            dve.tensor_tensor(VA[:, 1, t, :], b[:, 0:128], VA[:, 0, t, :].bitcast(F32), ALU.subtract)
                            ins = dve.tensor_tensor(VC[:, 1, t, 0:128], b[:, 128:256],
                                                    VC[:, 0, t, 0:128].bitcast(F32), ALU.subtract)
                        else:
                            ins = dve.tensor_tensor(VC[:, 1, t, 128:384], b, VC[:, 0, t, 128:384].bitcast(F32),
                                                    ALU.subtract)
                        ins.then_inc(mix_lo, 1)
                if name == "va_vc":
                    dve.wait_ge(mix_act, n0 + 2 * ntq)
                    for g in range(4):
                        dve.wait_ge(sp_mm, count(p, "spatial") + g + 1)
                        dve.scalar_tensor_tensor(
                            VF[:, 0:ntq, g * 64:(g + 1) * 64],
                            PS[:, 6 + g % 2, 0:ntq * 64].rearrange("p (t c) -> p t c", c=64),
                            VEC[:, 64 + 4 * l + g:65 + 4 * l + g], U[:, 0:ntq, g * 64:(g + 1) * 64],
                            ALU.add, ALU.mult).then_inc(sp_ev, 1)
                if name == "vc":
                    for c in range(2):
                        dve.wait_ge(yb_hi, count(p, "yb") + c + 1)
                        dve.tensor_tensor(YB[:, 1, c, 0:tok], BC[:, 0:tok], YB[:, 0, c, 0:tok].bitcast(F32),
                                          ALU.subtract).then_inc(yb_lo, 1)
                n += tiles
                if name == "qa_ka":
                    for t in range(TT):
                        h0 = 6 if last and t >= TLAT else 0
                        dve.wait_ge(mix_act, n0 + n - TT + t + 1)
                        link(dve.tensor_tensor(ROT[:, 0, h0 * 64:512], QA[:, t, h0 * 64:512], QA[:, t, h0 * 64:512],
                                               ALU.mult))
                        link(dve.tensor_reduce(AST[:, t, h0:8],
                                               ROT[:, 0, h0 * 64:512].rearrange("p (h d) -> p h d", d=DA),
                                               AX.X, ALU.add))
                    dve.tensor_scalar(AMS[:, :, :], AST[:, :, :], 1.0 / DA, EPS, ALU.mult, ALU.add).then_inc(a_ms, 1)
                if name == "c0":
                    if l == 0:
                        dve.wait_ge(rope_in, 64)
                    dve.wait_ge(a_rstd, l + 1)
                    for t in range(TT):
                        h0 = 6 if last and t >= TLAT else 0
                        x = QA[:, t, h0 * 64:512].rearrange("p (h d) -> p h d", d=DA)
                        link(dve.tensor_tensor(x, x, ASR[:, t, h0:8].unsqueeze(2).broadcast_to([P, 8 - h0, DA]),
                                               ALU.mult))
                        if h0 == 0:
                            xq = QA[:, t, 0:384].rearrange("p (h d) -> p h d", d=DA)
                            dve.tensor_tensor(xq, xq, GQK[:, 0, :].unsqueeze(1).broadcast_to([P, 6, DA]), ALU.mult)
                        xk = QA[:, t, 384:512].rearrange("p (h d) -> p h d", d=DA)
                        link(dve.tensor_tensor(xk, xk, GQK[:, 1, :].unsqueeze(1).broadcast_to([P, 2, DA]), ALU.mult))
                        if t < TLAT:
                            rotate(dve, link, x, ROPA[:, 0, t, :], ROPA[:, 1, t, :], 8, DA)
                if name == "c2":
                    for t in range(TLAT):
                        dve.wait_ge(mix_act, n0 + n - TT + t + 1)
                        rotate(dve, link, QC[:, t, :, 0:DC], ROPC[:, 0, t, :], ROPC[:, 1, t, :], 16, DC)
                    dve.wait_ge(lam_e, l + 1)
                    init = 0.8 - 0.6 * math.exp(-0.3 * l)
                    link(dve.tensor_tensor(LM[:, 4:5], LM[:, 2:3], LM[:, 3:4], ALU.subtract))
                    link(dve.tensor_scalar(LM[:, 5:6], LM[:, 4:5], init, None, ALU.add))
                    dve.tensor_scalar(GS[:, :], VEC[:, 72 + l:73 + l], 1.0 - init, None, ALU.mult).then_inc(qk_c, 1)
                    dve.wait_ge(qk_c, l + 1)

            att = Attention(last)
            sb, tb, hb, gb, cb = (count(p, k) for k in ("score", "tile", "half", "group", "yc"))

            def prep_lo(job):
                dst = prep_dst(job)
                for n, t0, m in prep_tiles(att, job):
                    dve.wait_ge(t_hi, hb + n + 1)
                    tok_ = slice(t0 * P, (t0 + m) * P)
                    for b in range(2):
                        rows = slice(64 * b, 64 * b + 64)
                        src = half_bank(n, m)[rows]
                        if job[1] == "q":
                            other = slice(64 - 64 * b, 128 - 64 * b)
                            ins = dve.tensor_tensor(dst[b][other, tok_], src, dst[b][rows, tok_].bitcast(F32),
                                                    ALU.subtract)
                        else:
                            for half in ((rows,) if job[0] == "C" else (slice(0, 64), slice(64, 128))):
                                ins = dve.tensor_tensor(dst[b][half, 1, tok_], src,
                                                        dst[b][rows, 0, tok_].bitcast(F32), ALU.subtract)
                    ins.then_inc(t_lo, 1)

            def maxima(i, c):
                nk, k0 = att.keys(i)
                scale = SC_A if i < att.na else SC_C
                b, j = att.score_buf(i, c), att.col(i, c)
                dve.wait_ge(s_mm, sb + att.job(i) + c + 1)
                link(dve.tensor_reduce(SM[:, 12 + j:13 + j], PF[:, b * 1024:b * 1024 + nk], AX.X, ALU.max))
                dve.tensor_scalar(SM[:, j:j + 1], SM[:, 12 + j:13 + j], -scale, None, ALU.mult).then_inc(mx_done, 1)

            def weights(i):
                nk, k0 = att.keys(i)
                nc_ = att.comps(i)
                dve.wait_ge(ex_done, sb + att.job(i) + nc_)
                pb, j = att.prob_buf(i, 0), att.col(i, 0)
                link(dve.reciprocal(SM[:, 8 + j:8 + j + nc_], SM[:, 4 + j:4 + j + nc_]))
                if nc_ == 1:
                    dve.tensor_scalar(PB[:, pb, 0:nk], PB[:, pb, 0:nk], SM[:, 8 + j:9 + j], None, ALU.mult) \
                        .then_inc(p_done, 1)
                else:
                    link(dve.tensor_scalar(PB[:, 3, 0:nk], PB[:, 3, 0:nk], SM[:, 9 + j:10 + j], LM[:, 5:6],
                                           ALU.mult, ALU.mult))
                    dve.scalar_tensor_tensor(PB[:, pb, 0:nk], PB[:, pb, 0:nk], SM[:, 8 + j:9 + j],
                                             PB[:, 3, 0:nk], ALU.mult, ALU.subtract).then_inc(p_done, 1)

            for job in att.first_preps:
                prep_lo(job)
            for i in att.steps:
                g = att.ends(i, 3)
                if g is not None:
                    part, h, toks, bank = y_places(att, g)
                    if part == "A":
                        rows = slice(64 * (h // 3), 64 * (h // 3) + 64)
                        dve.wait_ge(y_hi, gb + g + 1)
                        dve.tensor_tensor(Y[rows, 1, h % 3, toks], PS[rows, bank, 0:2 * P],
                                          Y[rows, 0, h % 3, toks].bitcast(F32), ALU.subtract).then_inc(y_lo, 1)
                    else:
                        dve.wait_ge(yst_mm, cb + g - att.nga + 1)
                        b = 2 * (g % 2)
                        dve.tensor_scalar(YMS[:, b:b + 2], PS[:, bank, 0:2], 1.0 / DV, EPS, ALU.mult, ALU.add) \
                            .then_inc(yms_done, 1)
                g = att.ends(i, 4)
                if g is not None and g >= att.nga:
                    part, h, toks, bank = y_places(att, g)
                    dve.wait_ge(ybc_mm, cb + g - att.nga + 1)
                    dve.scalar_tensor_tensor(YSQ[0:DV, g % 2, :], PS[0:DV, bank, 0:2 * P], GS[0:DV, :],
                                             YRAW[0:DV, g % 2, :], ALU.mult, ALU.mult).then_inc(yn_done, 1)
                g = att.ends(i, 5)
                if g is not None and g >= att.nga:
                    part, h, toks, bank = y_places(att, g)
                    dve.wait_ge(y_hi, gb + g + 1)
                    dve.tensor_tensor(Y[0:DV, 1, 3 + h, toks], YSQ[0:DV, g % 2, :],
                                      Y[0:DV, 0, 3 + h, toks].bitcast(F32), ALU.subtract).then_inc(y_lo, 1)
                if 0 <= i + 1 < att.n:
                    weights(i + 1)
                if i + 3 < att.n:
                    maxima(i + 3, 0)
                if 0 <= i < att.n:
                    g = att.units[i][2]
                    q0 = (att.units[i][3] % 2) * P
                    for n, a, m in att.parts(i):
                        dve.wait_ge(t_hi, hb + n + 1)
                        dve.tensor_tensor(PT[:, g % 2, 1, a:a + m, q0:q0 + P],
                                          half_bank(n, m).rearrange("p (k q) -> p k q", q=P),
                                          PT[:, g % 2, 0, a:a + m, q0:q0 + P].bitcast(F32), ALU.subtract) \
                            .then_inc(t_lo, 1)
                if att.na <= i + 3 < att.n:
                    maxima(i + 3, 1)
                for job in att.preps.get(i, []):
                    prep_lo(job)

        def rotate(dve, link, x, cos, sin, heads, d):
            m = d // 4
            a = ROT[:, 0, 0:heads * d].rearrange("p (h d) -> p h d", d=d)
            b = ROT[:, 1, 0:heads * d].rearrange("p (h d) -> p h d", d=d)
            dve.tensor_tensor(a, x, cos.unsqueeze(1).broadcast_to([P, heads, d]), ALU.mult)
            for axis in range(2):
                for half in range(2):
                    o1 = axis * 2 * m + half * m
                    o2 = axis * 2 * m + (1 - half) * m
                    ins = dve.tensor_tensor(b[:, :, o1:o1 + m], x[:, :, o2:o2 + m],
                                            sin[:, o1:o1 + m].unsqueeze(1).broadcast_to([P, heads, m]), ALU.mult)
            link(ins)
            link(dve.tensor_tensor(x, a, b, ALU.add))

        def pe_mix(pe, p, l, last, passes):
            u0, n0, lo0 = count(p, "units"), count(p, "mix_mm"), count(p, "mix_lo")
            ntq = TLAT if last else TT
            xl0 = AT[p]["xl"]
            freed = []
            n = nlo = 0
            pe.wait_ge(evacuated, count(p, "evac"))
            for w, name in enumerate(MIX_UNITS):
                s = (u0 + w) % 2
                tiles = mix_tiles(name, last)
                pe.wait_ge(w_split, u0 + w + 1)

                def tile_mm(t, k, m):
                    sl = slice(t * P, (t + 1) * P)
                    return passes(PS[:, m % 6, 0:256], XN[:, 0, k, sl], XN[:, 1, k, sl],
                                  ring(0, s, k, 0, 256), ring(1, s, k, 0, 256), k == 0, k == KD - 1)

                def bank_free(m):
                    if m >= 6:
                        pe.wait_ge(*freed[m - 6])

                if name == "v":
                    for k in range(KD):
                        pe.wait_ge(xn_lo, xl0 - KD + k + 1)
                        for t in range(tiles):
                            ins = tile_mm(t, k, t)
                            if k == KD - 1:
                                ins.then_inc(mix_mm, 1)
                else:
                    for t in range(tiles):
                        bank_free(n + t)
                        for k in range(KD):
                            ins = tile_mm(t, k, n + t)
                        ins.then_inc(mix_mm, 1)
                for t in range(tiles):
                    if name in ("va_vc", "vc"):
                        nlo += 1
                        freed.append((mix_lo, lo0 + nlo))
                    else:
                        freed.append((mix_act, n0 + n + t + 1))
                n += tiles
                if name == "v":
                    pe.wait_ge(layer_in, 80 * (l + 1))
                    for g in range(4):
                        ins = pe.transpose(PS[:, 6, g * P:(g + 1) * P], WSR[:, g, :], IDENT[:, :])
                    ins.then_inc(ws_t, 1)
                if name == "va_vc":
                    pe.wait_ge(ws_lo, l + 1)
                    pe.wait_ge(v_lo, l + 1)
                    for g in range(4):
                        if g >= 2:
                            pe.wait_ge(sp_ev, count(p, "spatial") + g - 1)
                        cols = slice(g * 64, (g + 1) * 64)
                        passes(PS[:, 6 + g % 2, 0:ntq * 64], WST[:, 0, g, :], WST[:, 1, g, :],
                               VN[:, 0, 0:ntq, cols], VN[:, 1, 0:ntq, cols], True, True).then_inc(sp_mm, 1)
                if name == "vc":
                    pe.wait_ge(sp_ev, count(p, "spatial") + 4)
                    for c in range(2):
                        if c:
                            pe.wait_ge(yb_lo, count(p, "yb") + c)
                        for t in range(ntq):
                            ins = pe.transpose(BC[:, t * P:(t + 1) * P], VF[:, t, c * P:(c + 1) * P], IDENT[:, :])
                        ins.then_inc(yb_t, 1)

            att = Attention(last)
            sb, tb, hb, gb, cb = (count(p, k) for k in ("score", "tile", "half", "group", "yc"))

            def half_free(n):
                if n >= 2:
                    pe.wait_ge(t_lo, hb + n - 1)

            def prep(job):
                part, what, h = job
                for n, t0, m in prep_tiles(att, job):
                    half_free(n)
                    for t in range(t0, t0 + m):
                        if part == "A":
                            src = QA[:, t, 384:512] if what == "k" else QA[:, t, h * 128:(h + 1) * 128]
                        else:
                            j = 2 * h + (8 if what == "k" else 0)
                            src = QC[:, t, j:j + 2, :].rearrange("p h d -> p (h d)")
                        ins = pe.transpose(PS[:, 4 + n % 2, (t - t0) * P:(t - t0 + 1) * P], src, IDENT[:, :])
                    ins.then_inc(t_mm, 1)

            def scores(i):
                part, h, g, t = att.units[i]
                nk, k0 = att.keys(i)
                if i == 0 or att.units[i - 1][:2] != (part, h):
                    pe.wait_ge(t_lo, hb + att.needs(i))
                for c in range(att.comps(i)):
                    b, n = att.score_buf(i, c), att.job(i) + c
                    if n >= 2:
                        pe.wait_ge(ex_done, sb + n - 1)
                    if part == "A":
                        q, k = prep_dst(("A", "q", h // 2))[h % 2], (K0, K1)[h // 3]
                    else:
                        q, k = c_q(h)[c], c_k(h)[c]
                    q = q[:, t * P:(t + 1) * P]
                    second = h % 2 if part == "A" else c
                    hi = slice(64 * second, 64 * second + 64)
                    for j0 in range(0, nk, 512):
                        jn = min(512, nk - j0)
                        dst = PF[:, b * 1024 + j0:b * 1024 + j0 + jn]
                        pe.matmul(dst, q[hi], k[hi, 1, k0 + j0:k0 + j0 + jn], start=True, stop=False)
                        ins = pe.matmul(dst, q, k[:, 0, k0 + j0:k0 + j0 + jn], start=False, stop=True)
                    ins.then_inc(s_mm, 1)

            def transposes(i):
                pe.wait_ge(p_done, tb + i + 1)
                nk, k0 = att.keys(i)
                pb = att.prob_buf(i, 0)
                for n, a, m in att.parts(i):
                    half_free(n)
                    for k in range(m):
                        c = a * P - k0 + k * P
                        ins = pe.transpose(PS[:, 4 + n % 2, k * P:(k + 1) * P], PB[:, pb, c:c + P], IDENT[:, :])
                    ins.then_inc(t_mm, 1)

            def values(g):
                part, h, tiles, final = att.groups[g]
                nk, k0 = att.keys(final)
                pe.wait_ge(t_lo, hb + att.half[final] + 2)
                if g >= 2:
                    pe.wait_ge(y_lo, gb + g - 1)
                rows = P if part == "A" else DV
                kts = range(k0 // P, (k0 + nk) // P)
                for kt in kts:
                    v = [VA[:, i, kt, :] if part == "A" else VC[:, i, kt, h * DV:(h + 1) * DV] for i in range(2)]
                    ins = passes(PS[0:rows, 6 + g % 2, 0:2 * P], v[0], v[1], PT[:, g % 2, 0, kt, :],
                                 PT[:, g % 2, 1, kt, :], kt == kts[0], kt == kts[-1])
                ins.then_inc(pv_mm, 1)

            pe.wait_ge(qk_c, l + 1)
            pe.wait_ge(pad_done, l + 1)
            for job in att.first_preps:
                prep(job)
            for i in att.steps:
                if i + 3 < att.n:
                    scores(i + 3)
                g = att.ends(i, 1)
                if g is not None:
                    values(g)
                for job in att.preps.get(i, []):
                    prep(job)
                if 0 <= i + 1 < att.n:
                    transposes(i + 1)
                g = att.ends(i, 2)
                if g is not None and g >= att.nga:
                    pe.wait_ge(yr_done, cb + g - att.nga + 1)
                    for t in range(2):
                        ins = pe.matmul(PS[:, 6 + g % 2, t:t + 1], YSQ[0:DV, g % 2, t * P:(t + 1) * P],
                                        ONE[0:DV, :], start=True, stop=True)
                    ins.then_inc(yst_mm, 1)
                g = att.ends(i, 3)
                if g is not None and g >= att.nga:
                    pe.wait_ge(yrs_done, cb + g - att.nga + 1)
                    for t in range(2):
                        j = 2 * (g % 2) + t
                        ins = pe.matmul(PS[:, 6 + g % 2, t * P:(t + 1) * P], YRS[:, j:j + 1].broadcast_to([P, P]),
                                        IDENT[:, :], start=True, stop=True)
                    ins.then_inc(ybc_mm, 1)

        @block.scalar
        def _(act):
            def split_hi(u, it=None):
                act.wait_ge(w_landed[u % 2], LANDED[u] if it is None else LANDED[u] + 32 * it)
                if u >= 2 or it is not None:
                    products_done(act, u - 2, it)
                for r, a, b in UNIT_WORDS[u]:
                    ins = act.activation(R[0:r, 0, u % 2, a:b], ST[0:r, u % 2, a:b], ACT.Copy)
                ins.then_inc(w_hi, 1)

            act.wait_ge(vec_ev, 1)
            for i in range(2):
                ins = act.activation(SCV[:, :, i], VEC[:, i * KD:(i + 1) * KD], ACT.Silu)
            ins.then_inc(scv_done, 1)
            split_hi(0)

            for p, (kind, l, which) in enumerate(PHASES):
                last = l == DEPTH - 1
                if kind == "norm":
                    both = has_ctx("norm", l, which)
                    tok = T if both else NLAT
                    shift = (NMOD * l + 3 * which) * KD
                    act.wait_ge(ab_done, 3 * l + which + 1)
                    for k in range(KD):
                        act.wait_ge(nt_done, count(p, "nt") + k + 1)
                        if k >= 2:
                            act.wait_ge(xn_lo, count(p, "xl") + k - 1)
                        ins = act.activation(NY[:, k % 2, 0:NLAT], NT[:, k % 2, 0:NLAT], ACT.Identity,
                                             scale=AA[:, k, 0:1], bias=MODS[:, shift + k, 0:1])
                        if both:
                            ins = act.activation(NY[:, k % 2, NLAT:T], NT[:, k % 2, NLAT:T], ACT.Identity,
                                                 scale=AA[:, k, 1:2], bias=MODS[:, shift + k, 1:2])
                        ins.then_inc(ny_done, 1)
                        act.wait_ge(ny_done, count(p, "ny") + k + 1)
                        act.activation(XN[:, 0, k, 0:tok], NY[:, k % 2, 0:tok], ACT.Copy).then_inc(xn_hi, 1)
                if kind == "ffn":
                    tok = T if has_ctx("ffn", l, which) else NLAT
                    for g, part, u0, e0, h0, n, q in parts(p, l, which):
                        if part == "out":
                            for i in range(n):
                                if next_is_prefetched(p, u0 + i):
                                    split_hi(u0 + i + 1)
                            continue
                        act.preload_act_table(ACT.Silu)
                        with act.Fori(0, n // 2) as it:
                            for j in range(2):
                                u, c = u0 + j, 2 * it + j
                                split_hi(u + 1, it)
                                products_done(act, u, it)
                                act.activation(SG[:, 0:tok], PF[:, 1536 * ((e0 + j) % 2):1536 * ((e0 + j) % 2) + tok],
                                               ACT.Silu).then_inc(silu_done, 1)
                                act.wait_ge(evacuated, e0 + j + 1 + 2 * it)
                                act.activation(H[:, 0, ds(c, 1), 0:tok], HF[:, 0:tok].unsqueeze(1), ACT.Copy) \
                                    .then_inc(h_hi, 1)
                if kind == "mix":
                    u0, n0 = count(p, "units"), count(p, "mix_mm")
                    n = 0
                    for w, name in enumerate(MIX_UNITS):
                        if w + 1 < NMU:
                            split_hi(u0 + w + 1)
                        if name == "va_vc":
                            act.wait_ge(v_n, l + 1)
                            nt = TLAT if last else TT
                            act.activation(VN[:, 0, 0:nt, :], VF[:, 0:nt, :], ACT.Copy).then_inc(v_hi, 1)
                        for t in range(mix_tiles(name, last)):
                            act.wait_ge(mix_mm, n0 + n + 1)
                            b = PS[:, n % 6, 0:256]
                            if name == "v":
                                act.activation(VF[:, t, :], b, ACT.Gelu_apprx_tanh).then_inc(mix_act, 1)
                            elif name == "u":
                                act.activation(U[:, t, :], b, ACT.Gelu_apprx_tanh).then_inc(mix_act, 1)
                            elif name == "va_vc":
                                act.activation(VA[:, 0, t, :], b[:, 0:128], ACT.Copy)
                                act.activation(VC[:, 0, t, 0:128], b[:, 128:256], ACT.Copy).then_inc(mix_act, 1)
                            elif name == "vc":
                                act.activation(VC[:, 0, t, 128:384], b, ACT.Copy).then_inc(mix_act, 1)
                            elif name == "qa":
                                act.activation(QA[:, t, 0:256], b, ACT.Copy).then_inc(mix_act, 1)
                            elif name == "qa_ka":
                                act.activation(QA[:, t, 256:512], b, ACT.Copy).then_inc(mix_act, 1)
                            else:
                                for c0, h0, hn, j0, jn in c_pieces(int(name[1])):
                                    ins = act.activation(
                                        QC[:, t, h0:h0 + 2 * hn - 1:2, j0:j0 + jn],
                                        b[:, c0:c0 + hn * jn].rearrange("p (h j) -> p h j", j=jn), ACT.Copy)
                                ins.then_inc(mix_act, 1)
                            if name == "v":
                                act.wait_ge(mix_act, n0 + n + 1)
                                act.activation(VJ[:, t, :], VF[:, t, :], ACT.Square,
                                               accum_out=VSS[:, t:t + 1]).then_inc(v_sq, 1)
                            n += 1
                        if name == "v":
                            act.wait_ge(ws_t, l + 1)
                            act.activation(WST[:, 0, :, :], PS[:, 6, :].rearrange("p (g q) -> p g q", g=4),
                                           ACT.Copy).then_inc(ws_hi, 1)
                        if name == "vc":
                            for c in range(2):
                                act.wait_ge(yb_t, count(p, "yb") + c + 1)
                                tok = NLAT if last else T
                                act.activation(YB[:, 0, c, 0:tok], BC[:, 0:tok], ACT.Copy).then_inc(yb_hi, 1)
                    act.wait_ge(lam_v, l + 1)
                    act.activation(LM[:, 2:4], LM[:, 0:2], ACT.Exp).then_inc(lam_e, 1)

                    att = Attention(last)
                    sb, tb, hb, gb, cb = (count(p, k) for k in ("score", "tile", "half", "group", "yc"))

                    def prep_hi(job):
                        dst = prep_dst(job)
                        for n, t0, m in prep_tiles(att, job):
                            act.wait_ge(t_mm, hb + n + 1)
                            tok_ = slice(t0 * P, (t0 + m) * P)
                            for b in range(2):
                                rows = slice(64 * b, 64 * b + 64)
                                src = half_bank(n, m)[rows]
                                if job[1] == "q":
                                    ins = act.activation(dst[b][rows, tok_], src, ACT.Copy)
                                else:
                                    act.activation(dst[b][0:64, 0, tok_], src, ACT.Copy)
                                    ins = act.activation(dst[b][64:128, 0, tok_], src, ACT.Copy)
                            ins.then_inc(t_hi, 1)

                    def exps(i, c):
                        nk, k0 = att.keys(i)
                        b, pb, j = att.score_buf(i, c), att.prob_buf(i, c), att.col(i, c)
                        act.wait_ge(mx_done, sb + att.job(i) + c + 1)
                        if c and i > att.na:
                            act.wait_ge(p_done, tb + i)
                        act.activation(PB[:, pb, 0:nk], PF[:, b * 1024:b * 1024 + nk], ACT.Exp,
                                       scale=SC_A if i < att.na else SC_C, bias=SM[:, j:j + 1],
                                       accum_out=SM[:, 4 + j:5 + j]).then_inc(ex_done, 1)

                    for job in att.first_preps:
                        prep_hi(job)
                    for i in att.steps:
                        g = att.ends(i, 2)
                        if g is not None:
                            part, h, toks, bank = y_places(att, g)
                            act.wait_ge(pv_mm, gb + g + 1)
                            if part == "A":
                                rows = slice(64 * (h // 3), 64 * (h // 3) + 64)
                                act.activation(Y[rows, 0, h % 3, toks], PS[rows, bank, 0:2 * P], ACT.Copy) \
                                    .then_inc(y_hi, 1)
                            else:
                                act.activation(YRAW[0:DV, g % 2, :], PS[0:DV, bank, 0:2 * P], ACT.Copy)
                                act.activation(YSQ[0:DV, g % 2, :], PS[0:DV, bank, 0:2 * P], ACT.Square) \
                                    .then_inc(yr_done, 1)
                        if 0 <= i + 2 < att.n:
                            exps(i + 2, 0)
                        if 0 <= i < att.n:
                            g = att.units[i][2]
                            if g >= 2:
                                act.wait_ge(pv_mm, gb + g - 1)
                            q0 = (att.units[i][3] % 2) * P
                            for n, a, m in att.parts(i):
                                act.wait_ge(t_mm, hb + n + 1)
                                act.activation(PT[:, g % 2, 0, a:a + m, q0:q0 + P],
                                               half_bank(n, m).rearrange("p (k q) -> p k q", q=P),
                                               ACT.Copy).then_inc(t_hi, 1)
                        if att.na <= i + 2 < att.n:
                            exps(i + 2, 1)
                        for job in att.preps.get(i, []):
                            prep_hi(job)
                        g = att.ends(i, 4)
                        if g is not None and g >= att.nga:
                            part, h, toks, bank = y_places(att, g)
                            act.wait_ge(yn_done, cb + g - att.nga + 1)
                            act.activation(Y[0:DV, 0, 3 + h, toks], YSQ[0:DV, g % 2, :], ACT.Copy) \
                                .then_inc(y_hi, 1)

                if kind == "out":
                    u0 = count(p, "units")
                    split_hi(u0)
                    for m in range(KD):
                        if next_is_prefetched(p, u0 + m):
                            split_hi(u0 + m + 1)
            for t in range(TLAT):
                act.wait_ge(f_t, t + 1)
                if t >= 2:
                    act.wait_ge(f_sq, t - 1)
                act.activation(OJ[:, t % 2, :], PF[:, 1024 * (t % 2):1024 * (t % 2) + D], ACT.Square,
                               accum_out=FSS[:, t:t + 1]).then_inc(f_sq, 1)

        @block.vector
        def _(dve):
            steps = [0]

            def link(ins):
                steps[0] += 1
                ins.then_inc(dve_step, 1)
                dve.wait_ge(dve_step, steps[0])

            def split_lo(u, it=None):
                dve.wait_ge(w_hi, u + 1 if it is None else u + 1 + 2 * it)
                for r, a, b in UNIT_WORDS[u]:
                    ins = dve.tensor_tensor(R[0:r, 1, u % 2, a:b], ST[0:r, u % 2, a:b],
                                            R[0:r, 0, u % 2, a:b].bitcast(F32), ALU.subtract)
                ins.then_inc(w_split, 1)

            def mod_piece(slot, k, piece, it=None):
                dve.wait_ge(mw_landed[slot], 16 * (piece // 2 + 1) if it is None else 16 * (piece // 2 + 1) + 16 * it)
                dve.wait_ge(mac_done, piece + 1 if it is None else piece + 1 + 2 * it)
                for v in range(2):
                    col = SCV[:, k, v:v + 1] if it is None else SCV[:, ds(2 * it + k, 1), v:v + 1]
                    ins = dve.scalar_tensor_tensor(ACC[:, v, :], MW[:, slot, :], col, ACC[:, v, :], ALU.mult, ALU.add)
                ins.then_inc(mac_done, 1)

            def clear_sums(n):
                dve.memset(ACC[:, :, :], 0.0).then_inc(acc_clear, 1)
                dve.wait_ge(acc_clear, n + 1)

            def finish_module(q, n):
                dve.wait_ge(fin_mm, n + 1)
                dve.tensor_tensor(MODS[:, q * KD:(q + 1) * KD, :], FN.rearrange("p (k v) -> p k v", v=2),
                                  BM[:, q * KD:(q + 1) * KD].unsqueeze(2).broadcast_to([P, KD, 2]), ALU.add) \
                    .then_inc(mod_ready, 1)
                dve.wait_ge(mod_ready, n + 2)

            dve.wait_ge(vec_t, 1)
            dve.tensor_copy(VEC[:, :], PS[:, 0, 0:80]).then_inc(h_lo, 1)
            dve.tensor_copy(BM[:, 0:72], PS[:, 1, 0:72]).then_inc(mac_done, 1)
            dve.tensor_copy(BM[:, 72:144], PS[:, 1, 128:200]).then_inc(vec_ev, 1)
            dve.wait_ge(vec_ev, 1)
            for k in range(KD):
                dve.wait_ge(xt_mm, k + 1)
                b = 2048 if k % 2 else 1024
                dve.tensor_copy(X[:, k, :], PF[:, b:b + T]).then_inc(xt_ev, 1)
            split_lo(0)
            dve.wait_ge(ms_used, 12)
            dve.tensor_tensor(MODS[:, 0:24, :], PS[:, 0, 0:48].rearrange("p (k v) -> p k v", v=2),
                              BM[:, 0:24].unsqueeze(2).broadcast_to([P, 24, 2]), ALU.add).then_inc(mod_ready, 1)
            dve.wait_ge(mod_ready, 1)

            for p, (kind, l, which) in enumerate(PHASES):
                last = l == DEPTH - 1
                if kind == "norm":
                    both = has_ctx("norm", l, which)
                    tok = T if both else NLAT
                    nt = tok // P
                    sc = (NMOD * l + 3 * which + 1) * KD
                    gcol = 16 + 16 * which + KD * l
                    dve.scalar_tensor_tensor(AA[:, :, :], MODS[:, sc:sc + KD, :], 1.0,
                                             VEC[:, gcol:gcol + KD].unsqueeze(2).broadcast_to([P, KD, 2]),
                                             ALU.add, ALU.mult).then_inc(ab_done, 1)
                    dve.wait_ge(st_mm, count(p, "stat") + 1)
                    dve.tensor_scalar(MSQ[:, 0:nt], MS7[:, 0:nt], 1.0 / D, EPS, ALU.mult, ALU.add).then_inc(ms_done, 1)
                    dve.wait_ge(bc_mm, count(p, "stat") + 1)

                    def scaled(k):
                        if k >= 2:
                            dve.wait_ge(ny_done, count(p, "ny") + k - 1)
                        dve.tensor_tensor(NT[:, k % 2, 0:tok], X[:, k, 0:tok], BC[:, 0:tok], ALU.mult) \
                            .then_inc(nt_done, 1)

                    scaled(0)
                    scaled(1)
                    for k in range(KD):
                        dve.wait_ge(xn_hi, count(p, "xh") + k + 1)
                        dve.tensor_tensor(XN[:, 1, k, 0:tok], NY[:, k % 2, 0:tok],
                                          XN[:, 0, k, 0:tok].bitcast(F32), ALU.subtract).then_inc(xn_lo, 1)
                        if k + 2 < KD:
                            scaled(k + 2)
                if kind == "ffn":
                    both = has_ctx("ffn", l, which)
                    tok = T if both else NLAT
                    gate = (NMOD * l + (2 if which == 0 else 8)) * KD
                    pending = None
                    for g, part, u0, e0, h0, n, q in parts(p, l, which):
                        piece = 8 * modules_before(p, l, which, g, part)
                        if pending is not None:
                            finish_module(*pending)
                            pending = None
                        if q is not None:
                            clear_sums(modules_before(p, l, which, g, part))
                            pending = (q, modules_before(p, l, which, g, part))
                        if part == "in":
                            with dve.Fori(0, n // 2) as it:
                                for j in range(2):
                                    c = 2 * it + j
                                    split_lo(u0 + j + 1, it)
                                    if q is not None:
                                        mod_piece(j, j, piece + j, it)
                                    a_lat, a_ctx, b_ctx, b_lat = set_views((e0 + j) % 2)
                                    dve.wait_ge(silu_done, count(p, "hidden") + h0 + j + 1 + 2 * it)
                                    dve.wait_ge(h_lo, count(p, "hidden") + h0 + j + 1 + 2 * it)
                                    ins = dve.tensor_tensor(HF[:, 0:NLAT], b_lat, SG[:, 0:NLAT], ALU.mult)
                                    if both:
                                        ins = dve.tensor_tensor(HF[:, NLAT:T], b_ctx, SG[:, NLAT:T], ALU.mult)
                                    ins.then_inc(evacuated, 1)
                                    dve.wait_ge(h_hi, count(p, "hidden") + h0 + j + 1 + 2 * it)
                                    dve.tensor_tensor(H[:, 1, ds(c, 1), 0:tok], HF[:, 0:tok].unsqueeze(1),
                                                      H[:, 0, ds(c, 1), 0:tok].bitcast(F32), ALU.subtract) \
                                        .then_inc(h_lo, 1)
                            continue
                        if g == 0:
                            dve.tensor_scalar(GG[:, :, :], MODS[:, gate:gate + KD, :], 0.5, None, ALU.mult) \
                                .then_inc(gate_ready, 1)
                            dve.wait_ge(gate_ready, 2 * l + which + 1)
                        for i in range(n):
                            u = u0 + i
                            if next_is_prefetched(p, u):
                                split_lo(u + 1)
                            if q is not None:
                                for j in range(2):
                                    mod_piece(j, 2 * i + j, piece + 2 * i + j)
                            products_done(dve, u)
                            a_lat, a_ctx, b_ctx, b_lat = set_views((e0 + i) % 2)
                            for b, lat, cx in ((0, a_lat, a_ctx), (1, b_lat, b_ctx)):
                                m = 2 * i + b
                                ins = dve.scalar_tensor_tensor(X[:, m, 0:NLAT], lat, GG[:, m, 0:1], X[:, m, 0:NLAT],
                                                               ALU.mult, ALU.add)
                                if both:
                                    ins = dve.scalar_tensor_tensor(X[:, m, NLAT:T], cx, GG[:, m, 1:2],
                                                                   X[:, m, NLAT:T], ALU.mult, ALU.add)
                            ins.then_inc(evacuated, 1)
                    if pending is not None:
                        finish_module(*pending)
                if kind == "mix":
                    dve_mix(dve, p, l, last, link, split_lo)
                if kind == "out":
                    u0, e0 = count(p, "units"), count(p, "evac")
                    split_lo(u0)
                    gate = (NMOD * l + 5) * KD
                    for m in range(KD):
                        u = u0 + m
                        if next_is_prefetched(p, u):
                            split_lo(u + 1)
                        products_done(dve, u)
                        a_lat, a_ctx, b_ctx, b_lat = set_views((e0 + m) % 2)
                        ins = dve.scalar_tensor_tensor(X[:, m, 0:NLAT], a_lat, MODS[:, gate + m, 0:1],
                                                       X[:, m, 0:NLAT], ALU.mult, ALU.add)
                        if not last:
                            ins = dve.scalar_tensor_tensor(X[:, m, NLAT:T], a_ctx, MODS[:, gate + m, 1:2],
                                                           X[:, m, NLAT:T], ALU.mult, ALU.add)
                        ins.then_inc(evacuated, 1)
            dve.wait_ge(f_sq, TLAT)
            dve.tensor_scalar(FMS[:, :], FSS[:, :], 1.0 / D, EPS, ALU.mult, ALU.add).then_inc(f_ms, 1)
            dve.wait_ge(f_rs, 1)
            dve.wait_ge(gf_in, 16)
            for t in range(TLAT):
                dve.wait_ge(f_t, TLAT + t + 1)
                dve.scalar_tensor_tensor(OUTB[:, t, :], PF[:, 1024 * (t % 2):1024 * (t % 2) + D], FRS[:, t:t + 1],
                                         GF[:, :], ALU.mult, ALU.mult).then_inc(f_n, 1)


        @block.tensor
        def _(pe):
            def passes(out_, wh, wl, xh, xl, first, final):
                pe.matmul(out_, wh, xl, start=first, stop=False)
                pe.matmul(out_, wl, xh, start=False, stop=False)
                return pe.matmul(out_, wh, xh, start=False, stop=final)

            def unit(u, e, xh, xl, chunks, both, it=None, wait_chunk=None, blocks=2, rows=None, col=None):
                dyn = 0 if it is None else 2 * it
                pe.wait_ge(w_split, u + 1 + dyn)
                if e >= 2:
                    pe.wait_ge(evacuated, e - 1 + dyn)
                a_lat, a_ctx, b_ctx, b_lat = set_views(e % 2)
                s = u % 2
                w = col or (lambda hl, k, b: ring(hl, s, k, b * P, P))
                ins = None
                for k in range(chunks):
                    if wait_chunk is not None:
                        wait_chunk(k)
                    f, z = k == 0, k == chunks - 1
                    r = P if rows is None else rows(k)
                    for b, lat in ((0, a_lat), (1, b_lat))[:blocks]:
                        ins = passes(lat, w(0, k, b)[0:r], w(1, k, b)[0:r], xh(k, 0)[0:r], xl(k, 0)[0:r], f, z)
                        if b == 0 and both:
                            ins = passes(a_ctx, w(0, k, b)[0:r], w(1, k, b)[0:r], xh(k, 1)[0:r], xl(k, 1)[0:r], f, z)
                if both and blocks == 2:
                    for k in range(chunks):
                        ins = passes(b_ctx, w(0, k, 1), w(1, k, 1), xh(k, 1), xl(k, 1), k == 0, k == chunks - 1)
                ins.then_inc(unit_done, 1)

            def stream(s):
                return slice(0, NLAT) if s == 0 else slice(NLAT, T)

            pe.wait_ge(cst, 5)
            pe.wait_ge(vrow_in, 144)
            pe.transpose(PS[:, 0, 0:P], VROW[:, 0, :], IDENT[:, :]).then_inc(unit_done, 1)
            pe.transpose(PS[:, 1, 0:P], VROW[:, 1, :], IDENT[:, :])
            pe.transpose(PS[:, 1, P:2 * P], VROW[:, 2, :], IDENT[:, :]).then_inc(vec_t, 1)
            pe.wait_ge(x_in, 32)
            for k in range(KD):
                if k >= 2:
                    pe.wait_ge(xt_ev, k - 1)
                b = 2048 if k % 2 else 1024
                for t in range(TT):
                    ins = pe.transpose(PF[:, b + t * P:b + (t + 1) * P], XLOAD[:, t, k * P:(k + 1) * P], IDENT[:, :])
                ins.then_inc(xt_mm, 1)
            pe.wait_ge(scv_done, 1)
            for i in range(12):
                pe.wait_ge(ms_landed[i % 6], 16 * (i // 6 + 1))
                for c in range(2):
                    o1 = 2 * (2 * i + c)
                    for k in range(KD):
                        ins = pe.matmul(PS[:, 0, o1:o1 + 2], MSW[:, i % 6, k, c * P:(c + 1) * P], SCV[:, k, :],
                                        start=k == 0, stop=k == KD - 1)
                ins.then_inc(ms_used, 1)

            for p, (kind, l, which) in enumerate(PHASES):
                last = l == DEPTH - 1
                if kind == "norm":
                    nt = (T if has_ctx("norm", l, which) else NLAT) // P
                    pe.wait_ge(ss_done, count(p, "ss") + KD)
                    pe.wait_ge(mod_ready, 1 + count(p, "fin"))
                    for t in range(nt):
                        ins = pe.matmul(MS7[:, t:t + 1], SS[:, t * P:(t + 1) * P], ONE[:, :], start=True, stop=True)
                    ins.then_inc(st_mm, 1)
                    pe.wait_ge(rstd_done, count(p, "stat") + 1)
                    for t in range(nt):
                        ins = pe.matmul(BC[:, t * P:(t + 1) * P], RST[:, t:t + 1].broadcast_to([P, P]), IDENT[:, :],
                                        start=True, stop=True)
                    ins.then_inc(bc_mm, 1)
                if kind == "ffn":
                    both = has_ctx("ffn", l, which)
                    xl0 = AT[p]["xl"]
                    pending = None

                    def finish_module(q, n):
                        pe.wait_ge(mac_done, 8 * (n + 1) + 1)
                        pe.wait_ge(mod_ready, n + 1)
                        for k in range(KD):
                            for v in range(2):
                                ins = pe.matmul(FN[:, 2 * k + v:2 * k + v + 1], ACC[:, v, k * P:(k + 1) * P],
                                                ONE[:, :], start=True, stop=True)
                        ins.then_inc(fin_mm, 1)

                    for g, part, u0, e0, h0, n, q in parts(p, l, which):
                        if pending is not None:
                            finish_module(*pending)
                            pending = None
                        if q is not None:
                            pending = (q, modules_before(p, l, which, g, part))
                        if part == "in":
                            xh = lambda k, s: XN[:, 0, k, stream(s)]
                            xl = lambda k, s: XN[:, 1, k, stream(s)]
                            lead = 0
                            if g == 0:
                                lead = 2
                                unit(u0, e0, xh, xl, KD, both,
                                     wait_chunk=lambda k: pe.wait_ge(xn_lo, xl0 - KD + k + 1))
                                unit(u0 + 1, e0 + 1, xh, xl, KD, both)
                            with pe.Fori(lead // 2, n // 2) as it:
                                for j in range(2):
                                    unit(u0 + j, e0 + j, xh, xl, KD, both, it)
                        else:
                            xh = lambda k, s: H[:, 0, k, stream(s)]
                            xl = lambda k, s: H[:, 1, k, stream(s)]
                            hid = count(p, "hidden") + h0
                            for i in range(n):
                                unit(u0 + i, e0 + i, xh, xl, GROUPS[g], both,
                                     wait_chunk=(lambda k: pe.wait_ge(h_lo, hid + k + 2)) if i == 0 else None)
                    if pending is not None:
                        finish_module(*pending)
                if kind == "mix":
                    pe_mix(pe, p, l, last, passes)
                if kind == "out":
                    u0, e0 = count(p, "units"), count(p, "evac")

                    def y_part(hl, k, s):
                        if k < 3:
                            return Y[:, hl, k, stream(s)]
                        if k < 5:
                            return YB[:, hl, k - 3, stream(s)]
                        return Y[:, hl, k - 2, stream(s)]

                    for m in range(KD):
                        slot = (u0 + m) % 2
                        unit(u0 + m, e0 + m, lambda k, s: y_part(0, k, s), lambda k, s: y_part(1, k, s), 9, not last,
                             blocks=1, rows=lambda k: P if k < 5 else DV,
                             col=lambda hl, k, b: R[:, hl, slot, k * P:(k + 1) * P])
            pe.wait_ge(evacuated, TOTAL["evac"])
            for r in range(2):
                for t in range(TLAT):
                    if r or t >= 2:
                        if 4 * r + t - 2 < TLAT:
                            pe.wait_ge(f_sq, 4 * r + t - 1)
                        else:
                            pe.wait_ge(f_n, 4 * r + t - 1 - TLAT)
                    for k in range(KD):
                        ins = pe.transpose(PF[:, 1024 * (t % 2) + k * P:1024 * (t % 2) + (k + 1) * P],
                                           X[:, k, t * P:(t + 1) * P], IDENT[:, :])
                    ins.then_inc(f_t, 1)


_INS = ["x", "c", "ctx", "c_ctx", "w_mod", "b_mod", "g_ffn1", "w_ffn1_in", "w_ffn1_out", "g_mix", "w_mix_in",
        "w_mix_out", "g_qnorm", "g_knorm", "g_vnorm", "w_spatial", "b_spatial", "lambda_vecs", "g_subln", "g_ffn2",
        "w_ffn2_in", "w_ffn2_out", "g_final"]
GRID_W = 64
ROPE_BASE = 10000.0


def rope_tables(d):
    half, m = d // 2, d // 4
    freqs = (1.0 / ROPE_BASE ** (np.arange(0, half, 2, dtype=np.float32) / half)).astype(np.float32)
    tokens = np.arange(NLAT)
    out = np.empty((2, NLAT, d), np.float32)
    for axis, pos in enumerate((tokens // GRID_W, tokens % GRID_W)):
        ang = (pos.astype(np.float32)[:, None] * freqs).astype(np.float32)
        o = axis * half
        out[0, :, o:o + half] = np.concatenate([np.cos(ang), np.cos(ang)], 1)
        out[1, :, o:o + half] = np.concatenate([-np.sin(ang), np.sin(ang)], 1)
    return np.ascontiguousarray(out.reshape(2, TLAT, P, d).transpose(0, 2, 1, 3))


def kernel(**inputs):
    import concourse.bacc as _bacc
    from concourse.bass_utils import run_bass_kernel_spmd as _run

    nc = _bacc.Bacc("TRN2", target_bir_lowering=False, num_devices=1)
    arrays = {name: np.ascontiguousarray(inputs[name]) for name in _INS}
    arrays["rope_a"], arrays["rope_c"] = rope_tables(DA), rope_tables(DC)
    A = {name: nc.dram_tensor(name, a.shape, mybir.dt.from_np(a.dtype), kind="ExternalInput").ap()
         for name, a in arrays.items()}
    out = nc.dram_tensor("out", (1, NLAT, D), F32, kind="ExternalOutput").ap()
    build(nc, A, out)
    return _run(nc, [arrays], core_ids=[0]).results[0]["out"]
```

```python
from contextlib import ExitStack
import math

import numpy as np

import concourse.bass as bass
from concourse import mybir

F32 = mybir.dt.float32
F32R = mybir.dt.float32r
ALU = mybir.AluOpType
ACT = mybir.ActivationFunctionType
AX = mybir.AxisListType
ds = bass.ds

P = 128
D = 1024
KD = D // P
NLAT, NCTX = 512, 256
T = NLAT + NCTX
TT = T // P
TLAT = NLAT // P
DEPTH = 2
D_FF = 2816
FFC = D_FF // P
GROUPS = (8, 8, 6)
NMOD = 9
EPS = 1e-6
HA, KVA, DA = 6, 2, 64
HC, DC, DV = 4, 48, 96
SLOT = 2048
COLS = {"qa": 0, "ka": 384, "va": 512, "u": 640, "v": 896, "qc": 1152, "kc": 1536, "vc": 1920}
MIX_UNITS = ("v", "u", "va_vc", "vc", "qa", "qa_ka", "c0", "c1", "c2")
MIX_PIECES = {
    "v": [(COLS["v"], 256)], "u": [(COLS["u"], 256)],
    "va_vc": [(COLS["va"], 128), (COLS["vc"], 128)], "vc": [(COLS["vc"] + 128, 256)],
    "qa": [(COLS["qa"], 256)], "qa_ka": [(COLS["qa"] + 256, 256)],
    "c0": [(COLS["qc"], 256)], "c1": [(COLS["qc"] + 256, 256)], "c2": [(COLS["qc"] + 512, 256)],
}
NMU = len(MIX_UNITS)
SC_A = DA ** -0.5
SC_C = DC ** -0.5
FFN_UNITS = sum(GROUPS) + 4 * len(GROUPS)


def mix_tiles(unit, last):
    return TLAT if last and unit in ("v", "u", "qa", "c0") else TT


def plan_phases():
    phases = [("start", 0, 0)]
    for l in range(DEPTH):
        phases += [("norm", l, 0), ("ffn", l, 0), ("norm", l, 1), ("mix", l, 0), ("out", l, 0),
                   ("norm", l, 2), ("ffn", l, 1)]
    return phases


def has_ctx(kind, l, which):
    last = l == DEPTH - 1
    if not last:
        return True
    return {"norm": which < 2, "ffn": which == 0, "mix": True, "out": False}[kind]


START_MODULES = 2


def background(l, which):
    first, n = {(0, 0): (2, 6), (0, 1): (8, 5), (1, 0): (13, 5)}.get((l, which), (0, 0))
    return list(range(first, first + n))


def module_slots(l, which):
    mods = background(l, which)
    if len(mods) == 5:
        mods.insert(4, None)
    return mods or [None] * 6


def out_pieces(g, i):
    cuts = (0, 3, 6, 8, 8) if g == len(GROUPS) - 1 else (0, 2, 4, 6, 8)
    return range(cuts[i], cuts[i + 1])


class Attention:

    def __init__(self, last):
        groups = [(0, 1), (2, 3)] if last else [(0, 1), (2, 3), (4, 5)]
        self.units, self.groups = [], []
        for part, heads in (("A", HA), ("C", HC)):
            for h in range(heads):
                for tiles in groups:
                    for t in tiles:
                        self.units.append((part, h, len(self.groups), t))
                    self.groups.append((part, h, tiles, len(self.units) - 1))
        self.n, self.ng, self.na = len(self.units), len(self.groups), HA * 2 * len(groups)
        self.nga = HA * len(groups)
        self.steps = range(-4, self.n + 6)
        per = 2 * len(groups)
        self.first_preps = [("A", "k", 0), ("A", "q", 0)]
        self.preps = {1: [("A", "q", 1)], 2 * per + 1: [("A", "q", 2)],
                      2 * per + 3: [("C", "k", 0)], 2 * per + 6: [("C", "q", 0)]}
        for h in range(1, HC):
            f = self.na + (h - 1) * per
            self.preps[f - 1] = [("C", "k", h)]
            self.preps.setdefault(f - (h > 1), []).append(("C", "q", h))
        self.half, n = {}, 0
        for job in self.first_preps:
            self.half[job] = n
            n += 2
        for i in self.steps:
            for job in self.preps.get(i, []) + ([i + 1] if 0 <= i + 1 < self.n else []):
                self.half[job] = n
                n += 2
        self.halves = n

    def job(self, i):
        return i if i < self.na else 2 * i - self.na

    def comps(self, i):
        return 1 if i < self.na else 2

    def keys(self, i):
        return (T, 0) if self.units[i][3] < TLAT else (NCTX, NLAT)

    def parts(self, i):
        nk, k0 = self.keys(i)
        m = nk // P // 2
        return [(self.half[i] + b, k0 // P + b * m, m) for b in range(2)]

    def prob_buf(self, i, c):
        return 3 if c else i % 3

    def col(self, i, c):
        return i % 4 if i < self.na else 2 * (i % 2) + c

    def score_buf(self, i, c):
        return i % 2 if i < self.na else c

    def ends(self, i, r):
        for g, x in enumerate(self.groups):
            if x[3] == i - r:
                return g
        return None

    def needs(self, i):
        part, h = self.units[i][:2]
        return max(self.half[(part, "k", 0 if part == "A" else h)],
                   self.half[(part, "q", h // 2 if part == "A" else h)]) + 2


def adds(kind, l, which):
    last = l == DEPTH - 1
    a = {}
    if kind == "norm":
        a = dict(ss=KD - 2, sq=KD - 3, sqa=2, stat=1, nt=KD, ny=KD, xh=KD, xl=KD)
    if kind == "ffn":
        nmod = len(background(l, which))
        a = dict(units=FFN_UNITS, evac=FFN_UNITS, hidden=FFC, mac=8 * nmod, fin=nmod)
    if kind == "mix":
        ntile = sum(mix_tiles(u, last) for u in MIX_UNITS)
        nlo = sum(mix_tiles(u, last) for u in ("va_vc", "vc"))
        att = Attention(last)
        a = dict(units=NMU, mix_mm=ntile, mix_lo=nlo, layer=1, v_tiles=TLAT if last else TT, spatial=4, yb=2,
                 score=att.na + 2 * (att.n - att.na), tile=att.n, half=att.halves, group=att.ng,
                 yc=att.ng - att.nga)
    if kind == "out":
        a = dict(units=KD, evac=KD)
    return a


PHASES = plan_phases()
AT = []
_run = {}
for _ph in PHASES:
    AT.append(dict(_run))
    for _k, _v in adds(*_ph).items():
        _run[_k] = _run.get(_k, 0) + _v
TOTAL = dict(_run)


def plan_units():
    dmas, words, done = [], [], []
    units, tiles = 1, 0
    for kind, l, which in PHASES:
        if kind == "ffn":
            for g in GROUPS:
                words += [((P, 0, SLOT),)] * g + [((P, 0, g * 256),)] * 4
                dmas += [2] * (g + 4)
                for _ in range(g + 4):
                    units += 1
                    done.append(("unit_done", units))
        if kind == "mix":
            for u in MIX_UNITS:
                tiles += mix_tiles(u, l == DEPTH - 1)
                dmas, words, done = dmas + [2], words + [((P, 0, SLOT),)], done + [("mix_mm", tiles)]
        if kind == "out":
            for _ in range(KD):
                units += 1
                dmas, words, done = dmas + [4], words + [((P, 0, 5 * P), (DV, 5 * P, 9 * P))], done + [("unit_done", units)]
    return dmas, words, done


UNIT_DMAS, UNIT_WORDS, UNIT_DONE = plan_units()
LANDED = [16 * sum(UNIT_DMAS[u % 2:u + 1:2]) for u in range(len(UNIT_DMAS))]


def c_pieces(unit):
    out = []
    col, end = 256 * unit, 256 * unit + 256
    while col < end:
        b, r = divmod(col, HC * DC)
        h, j = divmod(r, DC)
        stop = min(end, (b + 1) * HC * DC)
        if j or stop - col < DC:
            hn, jn = 1, min(DC - j, stop - col)
        else:
            hn, jn = (stop - col) // DC, DC
        out.append((col - 256 * unit, 8 * (b // 2) + 2 * h + b % 2, hn, j, jn))
        col += hn * jn
    return out


def build(nc, A, out):
    with ExitStack() as ctx:
        base = (nc.sbuf_base + 31) // 32 * 32
        top = nc.sbuf_usable_end

        def at(name, shape, dt, offset):
            n = 4
            for s in shape[1:]:
                n *= s
            assert base + offset + n <= top, (name, offset + n, top - base)
            return nc.alloc_sbuf_tensor_at(name, shape, dt, offset=base + offset)

        o = 0
        X = at("X", [P, KD, T], F32, o); o += 4 * KD * T
        XN_AT = o; o += 8 * KD * T
        R_AT = o; o += 16 * SLOT
        ST_AT = o; o += 8 * SLOT
        M_AT = o
        XN = at("XN", [P, 2, KD, T], F32R, XN_AT)
        XLOAD = at("XLOAD", [P, TT, D], F32, XN_AT)
        R = at("R", [P, 2, 2, SLOT], F32R, R_AT)
        ST = at("ST", [P, 2, SLOT], F32, ST_AT)
        H = at("H", [P, 2, GROUPS[0], T], F32R, M_AT)
        SG = at("SG", [P, T], F32, M_AT + 49152)
        HF = at("HF", [P, T], F32, M_AT + 52224)
        ACC = at("ACC", [P, 2, D], F32, M_AT + 55296)
        MW = at("MW", [P, 2, D], F32, M_AT + 63488)
        NT = at("NT", [P, 2, T], F32, M_AT)
        NY = at("NY", [P, 2, T], F32, M_AT + 8 * T)
        SQA = at("SQA", [P, 2, T], F32, M_AT + 49152)
        MSW = at("MSW", [P, 3, KD, 512], F32, M_AT)
        MR = at("MR", [2, 2, 512], F32, M_AT + 57344)
        VROW = at("VROW", [P, 3, P], F32, M_AT + 55296)
        QA = at("QA", [P, TT, 512], F32, M_AT)
        QC = at("QC", [P, TT, 16, 64], F32, M_AT + 12288)
        VA = at("VA", [P, 2, TT, 128], F32R, M_AT + 36864)
        VC = at("VC", [P, 2, TT, 384], F32R, M_AT + 43008)
        YB = at("YB", [P, 2, 2, T], F32R, M_AT + 61440)
        U = at("U", [P, TT, 256], F32, M_AT)
        VN = at("VN", [P, 2, TT, 256], F32R, M_AT + 6144)
        VJ = at("VJ", [P, TT, 256], F32, M_AT + 6144)
        VF = at("VF", [P, TT, 256], F32, M_AT + 18432)
        WST = at("WST", [P, 2, 4, P], F32R, M_AT + 73728)
        WSR = at("WSR", [P, 4, P], F32, M_AT + 24576)
        ROT = at("ROT", [P, 2, 768], F32, M_AT + 73728)
        SS = at("SS", [P, T], F32, M_AT + 73728)
        SQ = at("SQ", [P, T], F32, M_AT + 73728 + 4 * T)
        Y = at("Y", [P, 2, 7, T], F32R, XN_AT)
        K0 = at("K0", [P, 2, T], F32R, XN_AT + 43008)
        PT = at("PT", [P, 2, 2, TT, 2 * P], F32R, R_AT)
        K1 = at("K1", [P, 2, T], F32R, R_AT + 24576)
        Q0 = at("Q0", [P, 2, T], F32R, M_AT + 73728)
        Q1 = at("Q1", [P, 2, T], F32R, M_AT + 36864)
        QB = at("QB", [P, 2, 2, T], F32R, XN_AT + 3 * 4 * T)
        K23 = at("K23", [P, 2, 2, T], F32R, M_AT)
        OST = at("OST", [P, 2, 9 * P], F32, M_AT)
        OR = at("OR", [P, 2, 2, 9 * P], F32R, M_AT + 12288)
        PB = at("PB", [P, 4, T], F32, ST_AT)
        YRAW = at("YRAW", [P, 2, 2 * P], F32, ST_AT + 12288)
        YSQ = at("YSQ", [P, 2, 2 * P], F32, ST_AT + 14336)
        OUTB = at("OUTB", [P, 4, D], F32, XN_AT)
        OJ = at("OJ", [P, 2, D], F32, XN_AT + 16384)
        GF = at("GF", [P, D], F32, XN_AT + 24576)

        o = M_AT + 73728 + 8 * T

        def const(name, shape, dt=F32):
            nonlocal o
            t = at(name, shape, dt, o)
            n = 4
            for s in shape[1:]:
                n *= s
            o += (n + 31) // 32 * 32
            return t

        IDENT = const("IDENT", [P, P])
        ONE = const("ONE", [P, 1])
        IDR = const("IDR", [P, P], F32R)
        RSR = const("RSR", [P, 2, 8], F32R)
        NEGH = const("NEGH", [P, 48])
        VEC = const("VEC", [P, 80])
        BM = const("BM", [P, 18 * KD])
        SCV = const("SCV", [P, KD, 2])
        MODS = const("MODS", [P, 18 * KD, 2])
        AA = const("AA", [P, KD, 2])
        GG = const("GG", [P, KD, 2])
        ROPA = const("ROPA", [P, 2, TLAT, DA])
        ROPC = const("ROPC", [P, 2, TLAT, DC])
        GQK = const("GQK", [P, 2, DA])
        GV = const("GV", [P, 256])
        GS = const("GS", [P, 1])
        RST = const("RST", [P, 8])
        MSQ = const("MSQ", [P, 8])
        MSS = const("MSS", [P, 8])
        SM = const("SM", [P, 64])
        LV = at("LV", [P, 4, DC], F32, M_AT + 24576 + 2048)
        LVP = at("LVP", [P, 2, DC], F32, M_AT + 24576 + 2048 + 768)
        LM = const("LM", [P, 8])
        AST = const("AST", [P, TT, 8])
        ASR = const("ASR", [P, TT, 8])
        VSS = const("VSS", [P, 8])
        VSR = const("VSR", [P, 8])
        VMS = const("VMS", [P, 8])
        AMS = const("AMS", [P, TT, 8])
        YMS = const("YMS", [P, 4])
        YRS = const("YRS", [P, 4])
        FSS = const("FSS", [P, TLAT])
        FMS = const("FMS", [P, TLAT])
        FRS = const("FRS", [P, TLAT])

        PS = ctx.enter_context(nc.psum_tensor("PS", [P, 8, 512], F32))
        PF = PS[:, :, :].rearrange("p b n -> p (b n)")

        sems = {}

        def sem(name):
            s = ctx.enter_context(nc.semaphore(name))
            sems[name] = s
            return s

        w_landed = [sem("w_landed0"), sem("w_landed1")]
        w_hi, w_split, unit_done, evacuated = sem("w_hi"), sem("w_split"), sem("unit_done"), sem("evacuated")
        mw_landed = [sem("mw_landed0"), sem("mw_landed1")]
        ms_landed = [sem(f"ms_landed{i}") for i in range(3)]
        mr_done, mr_t = sem("mr_done"), sem("mr_t")
        ms_used, mac_done, acc_clear, fin_mm, mod_ready = (sem("ms_used"), sem("mac_done"), sem("acc_clear"),
                                                           sem("fin_mm"), sem("mod_ready"))
        gate_ready = sem("gate_ready")
        silu_done, h_hi, h_lo = sem("silu_done"), sem("h_hi"), sem("h_lo")
        sqa_done, rs_split = sem("sqa_done"), sem("rs_split")
        sq_done, ss_done, st_mm, ms_done, rstd_done = (sem("sq_done"), sem("ss_done"), sem("st_mm"),
                                                       sem("ms_done"), sem("rstd_done"))
        bc_mm, nt_done, ny_done, xn_hi, xn_lo, ab_done = (sem("bc_mm"), sem("nt_done"), sem("ny_done"),
                                                          sem("xn_hi"), sem("xn_lo"), sem("ab_done"))
        cst, vrow_in, vec_t, vec_ev, scv_done = (sem("cst"), sem("vrow_in"), sem("vec_t"), sem("vec_ev"),
                                                 sem("scv_done"))
        x_in, xt_mm, xt_ev, rope_in, layer_in = (sem("x_in"), sem("xt_mm"), sem("xt_ev"), sem("rope_in"),
                                                 sem("layer_in"))
        mix_mm, mix_act, mix_lo = sem("mix_mm"), sem("mix_act"), sem("mix_lo")
        ws_t, ws_hi, ws_lo = sem("ws_t"), sem("ws_hi"), sem("ws_lo")
        v_sq, v_ms, v_rstd, v_n, v_hi, v_lo = (sem("v_sq"), sem("v_ms"), sem("v_rstd"), sem("v_n"), sem("v_hi"),
                                               sem("v_lo"))
        sp_mm, sp_ev, yb_t, yb_hi, yb_lo, pad_done = (sem("sp_mm"), sem("sp_ev"), sem("yb_t"), sem("yb_hi"),
                                                      sem("yb_lo"), sem("pad_done"))
        a_ms, a_rstd, qk_c, lam_e, dve_step = (sem("a_ms"), sem("a_rstd"), sem("qk_c"),
                                                     sem("lam_e"), sem("dve_step"))
        lam_v, qk_a, pool_step = sem("lam_v"), sem("qk_a"), sem("pool_step")
        s_mm, mx_done, ex_done, p_done, t_mm, t_hi, t_lo = (sem("s_mm"), sem("mx_done"), sem("ex_done"),
                                                            sem("p_done"), sem("t_mm"), sem("t_hi"), sem("t_lo"))
        pv_mm, y_hi, y_lo = sem("pv_mm"), sem("y_hi"), sem("y_lo")
        yr_done, yst_mm, yms_done, yrs_done, ybc_mm, yn_done = (sem("yr_done"), sem("yst_mm"), sem("yms_done"),
                                                                sem("yrs_done"), sem("ybc_mm"), sem("yn_done"))
        f_t, f_sq, f_ms, f_rs, f_n, out_done, gf_in = (sem("f_t"), sem("f_sq"), sem("f_ms"), sem("f_rs"), sem("f_n"),
                                                       sem("out_done"), sem("gf_in"))

        wmod = A["w_mod"].rearrange("l (k p) n -> l p k n", p=P)
        w_in = {0: A["w_ffn1_in"], 1: A["w_ffn2_in"]}
        w_in = {i: w.rearrange("l (k p) n -> l p k n", p=P) for i, w in w_in.items()}
        w_out = {0: A["w_ffn1_out"], 1: A["w_ffn2_out"]}
        w_out = {i: w.rearrange("l (k p) n -> l p k n", p=P) for i, w in w_out.items()}
        w_mi = A["w_mix_in"].rearrange("l (k p) n -> l p k n", p=P)
        w_mo = A["w_mix_out"]
        stv = ST[:, :, :].rearrange("p s (k c) -> p s k c", c=256)
        MS7 = PF[:, 3872:3896]
        BC = PF[:, 3072:3072 + T]
        FN = PF[:, 3856:3872]
        FN5 = PF[:, 2560:2576]

        def ring(hl, slot, k, c0, n):
            return R[:, hl, slot, k * 256 + c0:k * 256 + c0 + n]

        def set_views(s):
            return (PS[:, 3 * s, :], PS[:, 3 * s + 1, 0:256], PS[:, 3 * s + 1, 256:512], PS[:, 3 * s + 2, :])

        def c_k(h):
            return (K23[:, 0], K23[:, 1]) if h % 2 == 0 else (K0, K1)

        def c_q(h):
            q = (QB[:, 1], Q1, Q0, Q1)[h]
            return q[:, 0, :], q[:, 1, :]

        def prep_dst(job):
            part, what, h = job
            if what == "k":
                return (K0, K1) if part == "A" else c_k(h)
            if part == "C":
                return c_q(h)
            q = (QB[:, 1], QB[:, 0], Q0)[h]
            return q[:, 0, :], q[:, 1, :]

        def half_bank(n, m):
            return PS[:, 4 + n % 2, 0:m * P]

        def y_places(att, g):
            part, h, tiles, _ = att.groups[g]
            return part, h, slice(tiles[0] * P, (tiles[-1] + 1) * P), 6 + g % 2 if part == "A" else 6

        def prep_tiles(att, job):
            nt = TT if job[1] == "k" or att.ng > 20 else TLAT
            return [(att.half[job] + b, b * (nt // 2), nt // 2) for b in range(2)]

        def stage_ring(u):
            out_phase = any(ph[0] == "out" and 0 <= u - AT[i]["units"] < KD for i, ph in enumerate(PHASES))
            return (OST, OR) if out_phase else (ST, R)

        def products_done(eng, u, it=None):
            name, value = UNIT_DONE[u] if u >= 0 else ("unit_done", u + 2)
            eng.wait_ge(sems[name], value if it is None else value + 2 * it)

        def parts(p, l, which):
            u, e, h, m, n = AT[p].get("units", 0), AT[p].get("evac", 0), 0, 0, 0
            out_ = []
            slots = module_slots(l, which)
            for g, size in enumerate(GROUPS):
                out_.append((g, "in", u, e, h, size, slots[2 * g]))
                u, e = u + size, e + size
                out_.append((g, "out", u, e, h, 4, slots[2 * g + 1]))
                u, e, h = u + 4, e + 4, h + size
            return out_

        def count(p, key):
            return AT[p].get(key, 0)

        def modules_before(p, l, which, g, part):
            n = count(p, "fin")
            for i, m in enumerate(module_slots(l, which)):
                if i >= 2 * g + (part == "out"):
                    break
                n += m is not None
            return n

        def next_is_prefetched(p, u):
            nxt = u + 1
            if nxt >= TOTAL["units"]:
                return False
            return not any(ph[0] == "out" and AT[i]["units"] == nxt for i, ph in enumerate(PHASES))

        def norm_module(p):
            kind, l, which = PHASES[p - 1]
            return background(l, which)[-1] if kind == "ffn" and background(l, which) else None

        FINAL_TILES = (3, 0, 1, 2)
        MS_BANKS = (0, 1, 6, 7)

        def rotate(eng, link, x, cos, sin, heads, d):
            m = d // 4
            a = ROT[:, 0, 0:heads * d].rearrange("p (h d) -> p h d", d=d)
            b = ROT[:, 1, 0:heads * d].rearrange("p (h d) -> p h d", d=d)
            eng.tensor_tensor(a, x, cos.unsqueeze(1).broadcast_to([P, heads, d]), ALU.mult)
            for axis in range(2):
                for half in range(2):
                    o1 = axis * 2 * m + half * m
                    o2 = axis * 2 * m + (1 - half) * m
                    ins = eng.tensor_tensor(b[:, :, o1:o1 + m], x[:, :, o2:o2 + m],
                                            sin[:, o1:o1 + m].unsqueeze(1).broadcast_to([P, heads, m]), ALU.mult)
            link(ins)
            link(eng.tensor_tensor(x, a, b, ALU.add))

        block = ctx.enter_context(nc.Block())

        @block.sync
        def _(sp):
            def slot_free(u, value=None):
                if u >= 2 or value is not None:
                    sp.wait_ge(w_split, (u - 1) if value is None else value)

            def mod_piece(q, k, slot, piece, it=None):
                if piece >= 2 or it is not None:
                    sp.wait_ge(mac_done, piece if it is None else piece + 2 * it)
                l_, j = divmod(q, NMOD)
                src = wmod[l_, :, k, j * D:(j + 1) * D] if it is None else \
                    A["w_mod"][l_, ds((2 * it + k) * P, P), j * D:(j + 1) * D]
                sp.dma_start(MW[:, slot, :], src).then_inc(mw_landed[slot], 16)

            sp.wait_ge(cst, 1)
            for r0, n, src in ((0, 8, A["c"].rearrange("b (k p) -> (b k) p", p=P)),
                               (8, 8, A["c_ctx"].rearrange("(k p) -> k p", p=P)),
                               (16, 16, A["g_ffn1"].rearrange("l (k p) -> (l k) p", p=P)),
                               (32, 16, A["g_mix"].rearrange("l (k p) -> (l k) p", p=P)),
                               (48, 16, A["g_ffn2"].rearrange("l (k p) -> (l k) p", p=P)),
                               (64, 8, A["b_spatial"].rearrange("l g p -> (l g) p"))):
                sp.dma_start(VROW[r0:r0 + n, 0, :], src).then_inc(vrow_in, 16)
            sp.dma_start(VROW[72:74, 0, 0:DV], A["g_subln"]).then_inc(vrow_in, 16)
            for l in range(DEPTH):
                sp.dma_start(VROW[0:72, 1 + l, :], A["b_mod"][l].rearrange("(k p) -> k p", p=P)).then_inc(vrow_in, 16)
            sp.dma_start(XLOAD[:, 0:TLAT, :], A["x"].rearrange("b (t p) d -> p (b t) d", p=P)).then_inc(x_in, 16)
            sp.dma_start(XLOAD[:, TLAT:TT, :], A["ctx"].rearrange("b (t p) d -> p (b t) d", p=P)).then_inc(x_in, 16)
            for i in range(2 * START_MODULES):
                if i >= 3:
                    sp.wait_ge(ms_used, i - 2)
                sp.dma_start(MSW[:, i % 3, :, :], wmod[0, :, :, i * 512:(i + 1) * 512]).then_inc(ms_landed[i % 3], 16)
            for i in range(2):
                sp.dma_start(ROPA[:, i, :, :], A["rope_a"][i]).then_inc(rope_in, 16)
                sp.dma_start(ROPC[:, i, :, :], A["rope_c"][i]).then_inc(rope_in, 16)

            for p, (kind, l, which) in enumerate(PHASES):
                if kind == "ffn":
                    wi, wo = w_in[which][l], w_out[which][l]
                    for g, part, u0, e0, h0, n, q in parts(p, l, which):
                        piece = 8 * modules_before(p, l, which, g, part)
                        if part == "in":
                            def in_weights(u, h, j, it=None):
                                slot_free(u, None if it is None else u - 1 + 2 * it)
                                c0 = h * P if it is None else (2 * it + h) * P
                                for b in range(2):
                                    sp.dma_start(stv[:, u % 2, :, b * P:(b + 1) * P], wi[:, :, ds(c0 + b * D_FF, P)]) \
                                        .then_inc(w_landed[u % 2], 16)

                            for j in range(2):
                                in_weights(u0 + j, h0 + j, j)
                            if q is not None:
                                if g == 0 and u0:
                                    products_done(sp, u0 - 1)
                                for j in range(2):
                                    mod_piece(q, j, j, piece + j)
                            with sp.Fori(1, n // 2) as it:
                                for j in range(2):
                                    in_weights(u0 + j, h0 + j, j, it)
                                    if q is not None:
                                        mod_piece(q, j, j, piece + j, it)
                        else:
                            for i in range(n):
                                u = u0 + i
                                slot_free(u)
                                k = GROUPS[g] // 2
                                for b in range(2):
                                    sp.dma_start(stv[:, u % 2, b * k:(b + 1) * k, :],
                                                 wo[:, h0 + b * k:h0 + (b + 1) * k, i * 256:(i + 1) * 256]) \
                                        .then_inc(w_landed[u % 2], 16)
                                before = module_slots(l, which)[2 * g]
                                if i == 1 and before is not None:
                                    for k in range(GROUPS[g], KD):
                                        mod_piece(before, k, k % 2, piece - KD + k)
                                if i >= 1 and q is not None:
                                    for k in out_pieces(g, i - 1):
                                        mod_piece(q, k, k % 2, piece + k)
                            if q is not None:
                                for k in out_pieces(g, n - 1):
                                    mod_piece(q, k, k % 2, piece + k)
                if kind == "mix":
                    u0 = count(p, "units")
                    for w, name in enumerate(MIX_UNITS):
                        u = u0 + w
                        slot_free(u)
                        if len(MIX_PIECES[name]) == 1:
                            c0, n = MIX_PIECES[name][0]
                            for b in (slice(0, KD // 2), slice(KD // 2, KD)):
                                sp.dma_start(stv[:, u % 2, b, :], w_mi[l, :, b, c0:c0 + n]) \
                                    .then_inc(w_landed[u % 2], 16)
                        else:
                            for i, (c0, n) in enumerate(MIX_PIECES[name]):
                                sp.dma_start(stv[:, u % 2, :, i * P:(i + 1) * P], w_mi[l, :, :, c0:c0 + n]) \
                                    .then_inc(w_landed[u % 2], 16)
                        if w == 1:
                            products_done(sp, u0 - 1)
                            sp.dma_start(GQK[:, 0, :], A["g_qnorm"][l].partition_broadcast(P)).then_inc(layer_in, 16)
                            sp.dma_start(GQK[:, 1, :], A["g_knorm"][l].partition_broadcast(P)).then_inc(layer_in, 16)
                            sp.dma_start(GV[:, :], A["g_vnorm"][l].partition_broadcast(P)).then_inc(layer_in, 16)
                            sp.dma_start(WSR[:, :, :], A["w_spatial"][l].rearrange("g p q -> p g q")) \
                                .then_inc(layer_in, 16)
                            sp.dma_start(LV[:, :, :], A["lambda_vecs"][l].partition_broadcast(P)).then_inc(layer_in, 16)
                if kind == "out":
                    u0 = count(p, "units")
                    att = Attention(l == DEPTH - 1)
                    third = max(i for i, x in enumerate(att.units) if x[:2] == ("C", 2))
                    sp.wait_ge(s_mm, count(p - 1, "score") + att.job(third) + 2)
                    for m in range(KD):
                        u = u0 + m
                        slot_free(u)
                        dst = OST[:, u % 2, :].rearrange("p (k c) -> p k c", c=P)
                        cols = slice(m * P, (m + 1) * P)
                        for b in range(2):
                            src = w_mo[l, b * 192:(b + 1) * 192, cols].rearrange("(j r) c -> r j c", r=DA)
                            sp.dma_start(dst[b * 64:(b + 1) * 64, 0:3, :], src).then_inc(w_landed[u % 2], 16)
                        src = w_mo[l, 384:640, cols].rearrange("(j r) c -> r j c", r=P)
                        sp.dma_start(dst[:, 3:5, :], src).then_inc(w_landed[u % 2], 16)
                        src = w_mo[l, 640:1024, cols].rearrange("(j r) c -> r j c", r=DV)
                        sp.dma_start(dst[0:DV, 5:9, :], src).then_inc(w_landed[u % 2], 16)
            products_done(sp, TOTAL["units"] - 1)
            sp.dma_start(GF[:, :], A["g_final"].partition_broadcast(P)).then_inc(gf_in, 16)
            for i, t in enumerate(FINAL_TILES):
                sp.wait_ge(f_n, i + 1)
                sp.dma_start(out[0, t * P:(t + 1) * P, :], OUTB[:, t, :]).then_inc(out_done, 16)
            sp.wait_ge(out_done, 16 * TLAT)

        @block.gpsimd
        def _(pool):
            steps = [0]

            def pool_link(ins):
                steps[0] += 1
                ins.then_inc(pool_step, 1)
                pool.wait_ge(pool_step, steps[0])

            pool.memset(VROW[:, :, :], 0.0).then_inc(cst, 1)
            pool.memset(IDENT[:, :], 0.0).then_inc(cst, 1)
            pool.memset(ONE[:, :], 1.0).then_inc(cst, 1)
            pool.memset(NEGH[:, :], -0.5).then_inc(cst, 1)
            pool.wait_ge(cst, 4)
            pool.affine_select(out=IDENT[:, :], in_=IDENT[:, :], compare_op=ALU.not_equal, fill=1.0, base=0,
                               pattern=[[-1, P]], channel_multiplier=1).then_inc(cst, 1)
            for p, (kind, l, which) in enumerate(PHASES):
                if kind == "norm":
                    tok = T if has_ctx("norm", l, which) else NLAT
                    prev = PHASES[p - 1]
                    for k in range(KD - 2):
                        if prev[0] == "start":
                            pool.wait_ge(xt_ev, k + 1)
                        elif prev[0] == "out":
                            pool.wait_ge(evacuated, count(p, "evac") - KD + k + 1)
                        else:
                            pool.wait_ge(evacuated, count(p, "evac") - 4 + k // 2 + 1)
                        if k == 0:
                            pool.tensor_tensor(SS[:, 0:tok], X[:, 0, 0:tok], X[:, 0, 0:tok], ALU.mult) \
                                .then_inc(ss_done, 1)
                            continue
                        pool.wait_ge(ss_done, count(p, "ss") + k)
                        pool.tensor_tensor(SQ[:, 0:tok], X[:, k, 0:tok], X[:, k, 0:tok], ALU.mult).then_inc(sq_done, 1)
                        pool.wait_ge(sq_done, count(p, "sq") + k)
                        pool.tensor_tensor(SS[:, 0:tok], SS[:, 0:tok], SQ[:, 0:tok], ALU.add).then_inc(ss_done, 1)
                    pool.wait_ge(ms_done, count(p, "stat") + 1)
                    nt = tok // P
                    pool.tensor_tensor(RST[:, 0:nt], MSQ[:, 0:nt], NEGH[:, 0:nt], ALU.pow).then_inc(rstd_done, 1)
                if kind == "mix":
                    last = l == DEPTH - 1
                    ntq = TLAT if last else TT
                    pool.wait_ge(v_ms, l + 1)
                    pool.tensor_tensor(VSR[:, 0:ntq], VMS[:, 0:ntq], NEGH[:, 0:ntq], ALU.pow).then_inc(v_rstd, 1)
                    pool.wait_ge(yb_t, count(p, "yb") + 2)
                    pool.memset(QC[:, :, :, DC:64], 0.0).then_inc(pad_done, 1)
                    pool.wait_ge(a_ms, l + 1)
                    pool.tensor_tensor(ASR[:, :, :], AMS[:, :, :], NEGH[:, :].rearrange("p (t h) -> p t h", h=8),
                                       ALU.pow).then_inc(a_rstd, 1)
                    if l == 0:
                        pool.wait_ge(rope_in, 64)
                    pool.wait_ge(qk_a, l + 1)
                    pool.wait_ge(mix_act, count(p, "mix_mm") + sum(mix_tiles(u, last) for u in MIX_UNITS))
                    for t in range(TLAT):
                        rotate(pool, pool_link, QC[:, t, :, 0:DC], ROPC[:, 0, t, :], ROPC[:, 1, t, :], 16, DC)
                    pool.memset(YRS[:, :], 1.0).then_inc(qk_c, 1)
                    att = Attention(last)
                    for i in att.steps:
                        g = att.ends(i, 4)
                        if g is not None and g >= att.nga:
                            pool.wait_ge(yms_done, count(p, "yc") + g - att.nga + 1)
                            b = 2 * (g % 2)
                            pool.tensor_tensor(YRS[:, b:b + 2], YMS[:, b:b + 2], NEGH[:, 0:2], ALU.pow) \
                                .then_inc(yrs_done, 1)
            for i, t in enumerate(FINAL_TILES):
                pool.wait_ge(f_ms, i + 1)
                pool.tensor_tensor(FRS[:, t:t + 1], FMS[:, t:t + 1], NEGH[:, 0:1], ALU.pow).then_inc(f_rs, 1)

        def dve_mix(dve, p, l, last, link, split_lo):
            u0, n0 = count(p, "units"), count(p, "mix_mm")
            ntq = TLAT if last else TT
            tok = NLAT if last else T
            init = 0.8 - 0.6 * math.exp(-0.3 * l)
            n = 0
            for w, name in enumerate(MIX_UNITS):
                if w + 1 < NMU:
                    split_lo(u0 + w + 1)
                tiles = mix_tiles(name, last)
                if name == "v":
                    dve.wait_ge(layer_in, 80 * (l + 1))
                    link(dve.tensor_scalar(GQK[:, 0, :], GQK[:, 0, :], SC_A, None, ALU.mult))
                    link(dve.tensor_tensor(LVP[:, :, :], LV[:, 0:4:2, :], LV[:, 1:4:2, :], ALU.mult))
                    dve.tensor_reduce(LM[:, 0:2], LVP[:, :, :], AX.X, ALU.add).then_inc(lam_v, 1)
                    dve.wait_ge(ws_hi, l + 1)
                    dve.tensor_tensor(WST[:, 1, :, :], PS[:, 6, :].rearrange("p (g q) -> p g q", g=4),
                                      WST[:, 0, :, :].bitcast(F32), ALU.subtract).then_inc(ws_lo, 1)
                if name == "u":
                    dve.wait_ge(v_sq, count(p, "v_tiles") + ntq)
                    dve.tensor_scalar(VMS[:, 0:ntq], VSS[:, 0:ntq], 1.0 / 256, EPS, ALU.mult, ALU.add) \
                        .then_inc(v_ms, 1)
                    dve.wait_ge(v_rstd, l + 1)
                    for t in range(ntq):
                        ins = dve.scalar_tensor_tensor(VF[:, t, :], VF[:, t, :], VSR[:, t:t + 1], GV[:, :],
                                                       ALU.mult, ALU.mult)
                    ins.then_inc(v_n, 1)
                    dve.wait_ge(v_hi, l + 1)
                    dve.tensor_tensor(VN[:, 1, 0:ntq, :], VF[:, 0:ntq, :], VN[:, 0, 0:ntq, :].bitcast(F32),
                                      ALU.subtract).then_inc(v_lo, 1)
                if name in ("va_vc", "vc"):
                    for t in range(tiles):
                        dve.wait_ge(mix_act, n0 + n + t + 1)
                        b = PS[:, (n + t) % 6, 0:256]
                        if name == "va_vc":
                            dve.tensor_tensor(VA[:, 1, t, :], b[:, 0:128], VA[:, 0, t, :].bitcast(F32), ALU.subtract)
                            ins = dve.tensor_tensor(VC[:, 1, t, 0:128], b[:, 128:256],
                                                    VC[:, 0, t, 0:128].bitcast(F32), ALU.subtract)
                        else:
                            ins = dve.tensor_tensor(VC[:, 1, t, 128:384], b, VC[:, 0, t, 128:384].bitcast(F32),
                                                    ALU.subtract)
                        ins.then_inc(mix_lo, 1)
                if name == "va_vc":
                    dve.wait_ge(mix_act, n0 + 2 * ntq)
                    for g in range(4):
                        dve.wait_ge(sp_mm, count(p, "spatial") + g + 1)
                        dve.scalar_tensor_tensor(
                            VF[:, 0:ntq, g * 64:(g + 1) * 64],
                            PS[:, 6 + g % 2, 0:ntq * 64].rearrange("p (t c) -> p t c", c=64),
                            VEC[:, 64 + 4 * l + g:65 + 4 * l + g], U[:, 0:ntq, g * 64:(g + 1) * 64],
                            ALU.add, ALU.mult).then_inc(sp_ev, 1)
                if name == "vc":
                    for c in range(2):
                        dve.wait_ge(yb_hi, count(p, "yb") + c + 1)
                        dve.tensor_tensor(YB[:, 1, c, 0:tok], BC[:, 0:tok], YB[:, 0, c, 0:tok].bitcast(F32),
                                          ALU.subtract).then_inc(yb_lo, 1)
                n += tiles
                if name == "qa_ka":
                    for t in range(TT):
                        h0 = 6 if last and t >= TLAT else 0
                        dve.wait_ge(mix_act, n0 + n - TT + t + 1)
                        link(dve.tensor_tensor(ROT[:, 0, h0 * 64:512], QA[:, t, h0 * 64:512], QA[:, t, h0 * 64:512],
                                               ALU.mult))
                        link(dve.tensor_reduce(AST[:, t, h0:8],
                                               ROT[:, 0, h0 * 64:512].rearrange("p (h d) -> p h d", d=DA),
                                               AX.X, ALU.add))
                    dve.tensor_scalar(AMS[:, :, :], AST[:, :, :], 1.0 / DA, EPS, ALU.mult, ALU.add).then_inc(a_ms, 1)
                if name == "c0":
                    if l == 0:
                        dve.wait_ge(rope_in, 64)
                    dve.wait_ge(a_rstd, l + 1)
                    for t in range(TT):
                        h0 = 6 if last and t >= TLAT else 0
                        x = QA[:, t, h0 * 64:512].rearrange("p (h d) -> p h d", d=DA)
                        link(dve.tensor_tensor(x, x, ASR[:, t, h0:8].unsqueeze(2).broadcast_to([P, 8 - h0, DA]),
                                               ALU.mult))
                        if h0 == 0:
                            xq = QA[:, t, 0:384].rearrange("p (h d) -> p h d", d=DA)
                            dve.tensor_tensor(xq, xq, GQK[:, 0, :].unsqueeze(1).broadcast_to([P, 6, DA]), ALU.mult)
                        xk = QA[:, t, 384:512].rearrange("p (h d) -> p h d", d=DA)
                        link(dve.tensor_tensor(xk, xk, GQK[:, 1, :].unsqueeze(1).broadcast_to([P, 2, DA]), ALU.mult))
                        if t < TLAT:
                            rotate(dve, link, x, ROPA[:, 0, t, :], ROPA[:, 1, t, :], 8, DA)
                    dve.tensor_scalar(GS[:, :], VEC[:, 72 + l:73 + l], 1.0 - init, None, ALU.mult).then_inc(qk_a, 1)

            att = Attention(last)
            sb, tb, hb, gb, cb = (count(p, k) for k in ("score", "tile", "half", "group", "yc"))

            def prep_lo(job):
                dst = prep_dst(job)
                for n, t0, m in prep_tiles(att, job):
                    dve.wait_ge(t_hi, hb + n + 1)
                    tok_ = slice(t0 * P, (t0 + m) * P)
                    for b in range(2):
                        rows = slice(64 * b, 64 * b + 64)
                        src = half_bank(n, m)[rows]
                        if job[1] == "q":
                            other = slice(64 - 64 * b, 128 - 64 * b)
                            ins = dve.tensor_tensor(dst[b][other, tok_], src, dst[b][rows, tok_].bitcast(F32),
                                                    ALU.subtract)
                        else:
                            for half in ((rows,) if job[0] == "C" else (slice(0, 64), slice(64, 128))):
                                ins = dve.tensor_tensor(dst[b][half, 1, tok_], src,
                                                        dst[b][rows, 0, tok_].bitcast(F32), ALU.subtract)
                    ins.then_inc(t_lo, 1)

            def maxima(i, c):
                nk, k0 = att.keys(i)
                b, j = att.score_buf(i, c), att.col(i, c)
                dve.wait_ge(s_mm, sb + att.job(i) + c + 1)
                dve.tensor_reduce(SM[:, j:j + 1], PF[:, b * 1024:b * 1024 + nk], AX.X, ALU.max, negate=True) \
                    .then_inc(mx_done, 1)

            def weights(i):
                nk, k0 = att.keys(i)
                nc_, pb, j = att.comps(i), att.prob_buf(i, 0), att.col(i, 0)
                dve.wait_ge(ex_done, sb + att.job(i) + nc_)
                link(dve.reciprocal(SM[:, 8 + j:8 + j + nc_], SM[:, 4 + j:4 + j + nc_]))
                if nc_ == 1:
                    dve.tensor_scalar(PB[:, pb, 0:nk], PB[:, pb, 0:nk], SM[:, 8 + j:9 + j], None, ALU.mult) \
                        .then_inc(p_done, 1)
                else:
                    link(dve.tensor_scalar(PB[:, 3, 0:nk], PB[:, 3, 0:nk], SM[:, 9 + j:10 + j], LM[:, 5:6],
                                           ALU.mult, ALU.mult))
                    dve.scalar_tensor_tensor(PB[:, pb, 0:nk], PB[:, pb, 0:nk], SM[:, 8 + j:9 + j],
                                             PB[:, 3, 0:nk], ALU.mult, ALU.subtract).then_inc(p_done, 1)

            for job in att.first_preps:
                prep_lo(job)
            for i in att.steps:
                if 0 <= i + 1 < att.n:
                    weights(i + 1)
                if 0 <= i + 3 < att.na:
                    maxima(i + 3, 0)
                if 0 <= i < att.n:
                    g = att.units[i][2]
                    q0 = (att.units[i][3] % 2) * P
                    for n, a, m in att.parts(i):
                        dve.wait_ge(t_hi, hb + n + 1)
                        dve.tensor_tensor(PT[:, g % 2, 1, a:a + m, q0:q0 + P],
                                          half_bank(n, m).rearrange("p (k q) -> p k q", q=P),
                                          PT[:, g % 2, 0, a:a + m, q0:q0 + P].bitcast(F32), ALU.subtract) \
                            .then_inc(t_lo, 1)
                g = att.ends(i, 4)
                if g is not None and g < att.nga:
                    part, h, toks, bank = y_places(att, g)
                    rows = slice(64 * (h // 3), 64 * (h // 3) + 64)
                    dve.wait_ge(y_hi, gb + g + 1)
                    dve.tensor_tensor(Y[rows, 1, h % 3, toks], PS[rows, bank, 0:2 * P],
                                      Y[rows, 0, h % 3, toks].bitcast(F32), ALU.subtract).then_inc(y_lo, 1)
                g = att.ends(i, 4)
                if g is not None and g >= att.nga:
                    dve.wait_ge(yst_mm, cb + g - att.nga + 1)
                    b = 2 * (g % 2)
                    dve.tensor_scalar(YMS[:, b:b + 2], PS[:, 7, 0:2], 1.0 / DV, EPS, ALU.mult, ALU.add) \
                        .then_inc(yms_done, 1)
                g = att.ends(i, 5)
                if g is not None and g >= att.nga:
                    dve.wait_ge(ybc_mm, cb + g - att.nga + 1)
                    dve.scalar_tensor_tensor(YSQ[0:DV, g % 2, :], PS[0:DV, 7, 0:2 * P], GS[0:DV, :],
                                             YRAW[0:DV, g % 2, :], ALU.mult, ALU.mult).then_inc(yn_done, 1)
                g = att.ends(i, 6)
                if g is not None and g >= att.nga:
                    part, h, toks, bank = y_places(att, g)
                    dve.wait_ge(y_hi, gb + g + 1)
                    dve.tensor_tensor(Y[0:DV, 1, 3 + h, toks], YSQ[0:DV, g % 2, :],
                                      Y[0:DV, 0, 3 + h, toks].bitcast(F32), ALU.subtract).then_inc(y_lo, 1)
                if att.na <= i + 3 < att.n:
                    maxima(i + 3, 0)
                    maxima(i + 3, 1)
                for job in att.preps.get(i, []):
                    prep_lo(job)
                if i == 4:
                    dve.wait_ge(lam_e, l + 1)
                    link(dve.tensor_tensor(LM[:, 4:5], LM[:, 2:3], LM[:, 3:4], ALU.subtract))
                    link(dve.tensor_scalar(LM[:, 5:6], LM[:, 4:5], init, None, ALU.add))
                if i in (att.n - 1, att.n):
                    split_lo(u0 + NMU + i - (att.n - 1))

        def pe_mix(pe, p, l, last, passes):
            u0, n0, lo0 = count(p, "units"), count(p, "mix_mm"), count(p, "mix_lo")
            ntq = TLAT if last else TT
            xl0 = AT[p]["xl"]
            owner = [name for name in MIX_UNITS for _ in range(mix_tiles(name, last))]
            n_lo = sum(name in ("va_vc", "vc") for name in owner)
            n = 0
            pe.wait_ge(evacuated, count(p, "evac"))
            pe.wait_ge(mod_ready, 1 + count(p, "fin"))
            for w, name in enumerate(MIX_UNITS):
                s = (u0 + w) % 2
                tiles = mix_tiles(name, last)
                pe.wait_ge(w_split, u0 + w + 1)

                def tile_mm(t, k, m):
                    sl = slice(t * P, (t + 1) * P)
                    return passes(PS[:, m % 6, 0:256], XN[:, 0, k, sl], XN[:, 1, k, sl],
                                  ring(0, s, k, 0, 256), ring(1, s, k, 0, 256), k == 0, k == KD - 1)

                def bank_free(m):
                    if m >= 6 and owner[m - 6] in ("va_vc", "vc"):
                        pe.wait_ge(mix_lo, lo0 + sum(name in ("va_vc", "vc") for name in owner[:m - 5]))
                    elif m >= 6:
                        pe.wait_ge(mix_act, n0 + m - 5)

                if name == "v":
                    for k in range(KD):
                        pe.wait_ge(xn_lo, xl0 - KD + k + 1)
                        for t in range(tiles):
                            ins = tile_mm(t, k, t)
                            if k == KD - 1:
                                ins.then_inc(mix_mm, 1)
                else:
                    for t in range(tiles):
                        bank_free(n + t)
                        for k in range(KD):
                            ins = tile_mm(t, k, n + t)
                        ins.then_inc(mix_mm, 1)
                n += tiles
                if name == "v":
                    pe.wait_ge(layer_in, 80 * (l + 1))
                    for g in range(4):
                        ins = pe.transpose(PS[:, 6, g * P:(g + 1) * P], WSR[:, g, :], IDENT[:, :])
                    ins.then_inc(ws_t, 1)
                if name == "va_vc":
                    pe.wait_ge(ws_lo, l + 1)
                    pe.wait_ge(v_lo, l + 1)
                    for g in range(4):
                        if g >= 2:
                            pe.wait_ge(sp_ev, count(p, "spatial") + g - 1)
                        cols = slice(g * 64, (g + 1) * 64)
                        passes(PS[:, 6 + g % 2, 0:ntq * 64], WST[:, 0, g, :], WST[:, 1, g, :],
                               VN[:, 0, 0:ntq, cols], VN[:, 1, 0:ntq, cols], True, True).then_inc(sp_mm, 1)
                if name == "vc":
                    pe.wait_ge(sp_ev, count(p, "spatial") + 4)
                    for c in range(2):
                        if c:
                            pe.wait_ge(yb_lo, count(p, "yb") + c)
                        for t in range(ntq):
                            ins = pe.transpose(BC[:, t * P:(t + 1) * P], VF[:, t, c * P:(c + 1) * P], IDENT[:, :])
                        ins.then_inc(yb_t, 1)

            att = Attention(last)
            sb, tb, hb, gb, cb = (count(p, k) for k in ("score", "tile", "half", "group", "yc"))

            def half_free(n):
                if n >= 2:
                    pe.wait_ge(t_lo, hb + n - 1)

            def prep(job):
                part, what, h = job
                if job == ("A", "q", 2):
                    pe.wait_ge(qk_c, l + 1)
                    pe.wait_ge(pad_done, l + 1)
                for n, t0, m in prep_tiles(att, job):
                    half_free(n)
                    for t in range(t0, t0 + m):
                        if part == "A":
                            src = QA[:, t, 384:512] if what == "k" else QA[:, t, h * 128:(h + 1) * 128]
                        else:
                            j = 2 * h + (8 if what == "k" else 0)
                            src = QC[:, t, j:j + 2, :].rearrange("p h d -> p (h d)")
                        ins = pe.transpose(PS[:, 4 + n % 2, (t - t0) * P:(t - t0 + 1) * P], src, IDENT[:, :])
                    ins.then_inc(t_mm, 1)

            def scores(i):
                part, h, g, t = att.units[i]
                nk, k0 = att.keys(i)
                if i == 0 or att.units[i - 1][:2] != (part, h):
                    pe.wait_ge(t_lo, hb + att.needs(i))
                for c in range(att.comps(i)):
                    b, n = att.score_buf(i, c), att.job(i) + c
                    if n >= 2:
                        pe.wait_ge(ex_done, sb + n - 1)
                    if part == "A":
                        q, k = prep_dst(("A", "q", h // 2))[h % 2], (K0, K1)[h // 3]
                    else:
                        q, k = c_q(h)[c], c_k(h)[c]
                    q = q[:, t * P:(t + 1) * P]
                    second = h % 2 if part == "A" else c
                    hi = slice(64 * second, 64 * second + 64)
                    for j0 in range(0, nk, 512):
                        jn = min(512, nk - j0)
                        dst = PF[:, b * 1024 + j0:b * 1024 + j0 + jn]
                        pe.matmul(dst, q[hi], k[hi, 1, k0 + j0:k0 + j0 + jn], start=True, stop=False)
                        ins = pe.matmul(dst, q, k[:, 0, k0 + j0:k0 + j0 + jn], start=False, stop=True)
                    ins.then_inc(s_mm, 1)

            def transposes(i, b):
                pe.wait_ge(p_done, tb + i + 1)
                nk, k0 = att.keys(i)
                pb = att.prob_buf(i, 0)
                n, a, m = att.parts(i)[b]
                half_free(n)
                for k in range(m):
                    c = a * P - k0 + k * P
                    ins = pe.transpose(PS[:, 4 + n % 2, k * P:(k + 1) * P], PB[:, pb, c:c + P], IDENT[:, :])
                ins.then_inc(t_mm, 1)

            def values(g):
                part, h, tiles, final = att.groups[g]
                nk, k0 = att.keys(final)
                pe.wait_ge(t_lo, hb + att.half[final] + 2)
                bank = y_places(att, g)[3]
                if g > att.nga:
                    pe.wait_ge(yr_done, cb + g - att.nga)
                elif g >= 2:
                    pe.wait_ge(y_lo, gb + g - 1)
                rows = P if part == "A" else DV
                kts = range(k0 // P, (k0 + nk) // P)
                for kt in kts:
                    v = [VA[:, i, kt, :] if part == "A" else VC[:, i, kt, h * DV:(h + 1) * DV] for i in range(2)]
                    ins = passes(PS[0:rows, bank, 0:2 * P], v[0], v[1], PT[:, g % 2, 0, kt, :],
                                 PT[:, g % 2, 1, kt, :], kt == kts[0], kt == kts[-1])
                ins.then_inc(pv_mm, 1)

            pe.wait_ge(mix_act, n0 + n)
            pe.wait_ge(mix_lo, lo0 + n_lo)
            pe.wait_ge(yb_lo, count(p, "yb") + 2)
            pe.wait_ge(qk_a, l + 1)
            for job in att.first_preps:
                prep(job)
            for i in att.steps:
                if att.na <= i + 3 < att.n:
                    scores(i + 3)
                g, early = att.ends(i, 1), ("C", "q", 1) in att.preps.get(i, [])
                if g is not None and early:
                    values(g)
                for job in att.preps.get(i, []):
                    prep(job)
                if i + 4 < att.na:
                    scores(i + 4)
                if 0 <= i + 1 < att.n:
                    transposes(i + 1, 0)
                if 0 <= i + 1 < att.n:
                    transposes(i + 1, 1)
                if g is not None and not early:
                    values(g)
                g = att.ends(i, 3)
                if g is not None and g >= att.nga:
                    pe.wait_ge(yr_done, cb + g - att.nga + 1)
                    if g == att.nga:
                        pe.wait_ge(y_lo, gb + g)
                    else:
                        pe.wait_ge(yn_done, cb + g - att.nga)
                    for t in range(2):
                        ins = pe.matmul(PS[:, 7, t:t + 1], YSQ[0:DV, g % 2, t * P:(t + 1) * P],
                                        ONE[0:DV, :], start=True, stop=True)
                    ins.then_inc(yst_mm, 1)
                g = att.ends(i, 4)
                if g is not None and g >= att.nga:
                    pe.wait_ge(yrs_done, cb + g - att.nga + 1)
                    for t in range(2):
                        j = 2 * (g % 2) + t
                        ins = pe.matmul(PS[:, 7, t * P:(t + 1) * P], YRS[:, j:j + 1].broadcast_to([P, P]),
                                        IDENT[:, :], start=True, stop=True)
                    ins.then_inc(ybc_mm, 1)

        @block.scalar
        def _(act):
            def split_hi(u, it=None):
                act.wait_ge(w_landed[u % 2], LANDED[u] if it is None else LANDED[u] + 32 * it)
                if u >= 2 or it is not None:
                    products_done(act, u - 2, it)
                src, dst = stage_ring(u)
                for r, a, b in UNIT_WORDS[u]:
                    ins = act.activation(dst[0:r, 0, u % 2, a:b], src[0:r, u % 2, a:b], ACT.Copy)
                ins.then_inc(w_hi, 1)

            act.wait_ge(vec_ev, 1)
            for i in range(2):
                ins = act.activation(SCV[:, :, i], VEC[:, i * KD:(i + 1) * KD], ACT.Silu)
            ins.then_inc(scv_done, 1)
            for p, (kind, l, which) in enumerate(PHASES):
                last = l == DEPTH - 1
                if kind == "norm":
                    both = has_ctx("norm", l, which)
                    tok = T if both else NLAT
                    shift = (NMOD * l + 3 * which) * KD
                    for k in range(KD - 2, KD):
                        if PHASES[p - 1][0] == "start":
                            act.wait_ge(xt_ev, k + 1)
                        elif PHASES[p - 1][0] == "out":
                            act.wait_ge(evacuated, count(p, "evac") - KD + k + 1)
                        else:
                            act.wait_ge(evacuated, count(p, "evac"))
                        act.activation(SQA[:, k % 2, 0:tok], X[:, k, 0:tok], ACT.Square).then_inc(sqa_done, 1)
                    if PHASES[p - 1][0] == "start":
                        split_hi(0)
                    act.wait_ge(ab_done, 3 * l + which + 1)
                    for k in range(KD):
                        act.wait_ge(nt_done, count(p, "nt") + k + 1)
                        if k >= 2:
                            act.wait_ge(xn_lo, count(p, "xl") + k - 1)
                        ins = act.activation(NY[:, k % 2, 0:NLAT], NT[:, k % 2, 0:NLAT], ACT.Identity,
                                             scale=AA[:, k, 0:1], bias=MODS[:, shift + k, 0:1])
                        if both:
                            ins = act.activation(NY[:, k % 2, NLAT:T], NT[:, k % 2, NLAT:T], ACT.Identity,
                                                 scale=AA[:, k, 1:2], bias=MODS[:, shift + k, 1:2])
                        ins.then_inc(ny_done, 1)
                        act.wait_ge(ny_done, count(p, "ny") + k + 1)
                        act.activation(XN[:, 0, k, 0:tok], NY[:, k % 2, 0:tok], ACT.Copy).then_inc(xn_hi, 1)
                if kind == "ffn":
                    tok = T if has_ctx("ffn", l, which) else NLAT
                    for g, part, u0, e0, h0, n, q in parts(p, l, which):
                        if part == "out":
                            for i in range(n):
                                if next_is_prefetched(p, u0 + i):
                                    split_hi(u0 + i + 1)
                            continue
                        act.preload_act_table(ACT.Silu)
                        with act.Fori(0, n // 2) as it:
                            for j in range(2):
                                u, c = u0 + j, 2 * it + j
                                split_hi(u + 1, it)
                                products_done(act, u, it)
                                act.activation(SG[:, 0:tok], PF[:, 1536 * ((e0 + j) % 2):1536 * ((e0 + j) % 2) + tok],
                                               ACT.Silu).then_inc(silu_done, 1)
                                act.wait_ge(evacuated, e0 + j + 1 + 2 * it)
                                act.activation(H[:, 0, ds(c, 1), 0:tok], HF[:, 0:tok].unsqueeze(1), ACT.Copy) \
                                    .then_inc(h_hi, 1)
                if kind == "mix":
                    u0, n0 = count(p, "units"), count(p, "mix_mm")
                    n = 0
                    for w, name in enumerate(MIX_UNITS):
                        if w + 1 < NMU:
                            split_hi(u0 + w + 1)
                        if name == "va_vc":
                            act.wait_ge(v_n, l + 1)
                            nt = TLAT if last else TT
                            act.activation(VN[:, 0, 0:nt, :], VF[:, 0:nt, :], ACT.Copy).then_inc(v_hi, 1)
                        for t in range(mix_tiles(name, last)):
                            act.wait_ge(mix_mm, n0 + n + 1)
                            b = PS[:, n % 6, 0:256]
                            if name == "v":
                                act.activation(VF[:, t, :], b, ACT.Gelu_apprx_tanh).then_inc(mix_act, 1)
                            elif name == "u":
                                act.activation(U[:, t, :], b, ACT.Gelu_apprx_tanh).then_inc(mix_act, 1)
                            elif name == "va_vc":
                                act.activation(VA[:, 0, t, :], b[:, 0:128], ACT.Copy)
                                act.activation(VC[:, 0, t, 0:128], b[:, 128:256], ACT.Copy).then_inc(mix_act, 1)
                            elif name == "vc":
                                act.activation(VC[:, 0, t, 128:384], b, ACT.Copy).then_inc(mix_act, 1)
                            elif name == "qa":
                                act.activation(QA[:, t, 0:256], b, ACT.Copy).then_inc(mix_act, 1)
                            elif name == "qa_ka":
                                act.activation(QA[:, t, 256:512], b, ACT.Copy).then_inc(mix_act, 1)
                            else:
                                for c0, h0, hn, j0, jn in c_pieces(int(name[1])):
                                    ins = act.activation(
                                        QC[:, t, h0:h0 + 2 * hn - 1:2, j0:j0 + jn],
                                        b[:, c0:c0 + hn * jn].rearrange("p (h j) -> p h j", j=jn), ACT.Copy,
                                        scale=SC_C if h0 < 8 else 1.0)
                                ins.then_inc(mix_act, 1)
                            if name == "v":
                                act.wait_ge(mix_act, n0 + n + 1)
                                act.activation(VJ[:, t, :], VF[:, t, :], ACT.Square,
                                               accum_out=VSS[:, t:t + 1]).then_inc(v_sq, 1)
                            n += 1
                        if name == "v":
                            act.wait_ge(ws_t, l + 1)
                            act.activation(WST[:, 0, :, :], PS[:, 6, :].rearrange("p (g q) -> p g q", g=4),
                                           ACT.Copy).then_inc(ws_hi, 1)
                        if name == "vc":
                            for c in range(2):
                                act.wait_ge(yb_t, count(p, "yb") + c + 1)
                                tok = NLAT if last else T
                                act.activation(YB[:, 0, c, 0:tok], BC[:, 0:tok], ACT.Copy).then_inc(yb_hi, 1)

                    att = Attention(last)
                    sb, tb, hb, gb, cb = (count(p, k) for k in ("score", "tile", "half", "group", "yc"))

                    def prep_hi(job):
                        dst = prep_dst(job)
                        for n, t0, m in prep_tiles(att, job):
                            act.wait_ge(t_mm, hb + n + 1)
                            tok_ = slice(t0 * P, (t0 + m) * P)
                            for b in range(2):
                                rows = slice(64 * b, 64 * b + 64)
                                src = half_bank(n, m)[rows]
                                if job[1] == "q":
                                    ins = act.activation(dst[b][rows, tok_], src, ACT.Copy)
                                else:
                                    act.activation(dst[b][0:64, 0, tok_], src, ACT.Copy)
                                    ins = act.activation(dst[b][64:128, 0, tok_], src, ACT.Copy)
                            ins.then_inc(t_hi, 1)

                    def exps(i, c):
                        nk, k0 = att.keys(i)
                        b, pb, j = att.score_buf(i, c), att.prob_buf(i, c), att.col(i, c)
                        act.wait_ge(mx_done, sb + att.job(i) + c + 1)
                        if c and i > att.na:
                            act.wait_ge(p_done, tb + i)
                        act.activation(PB[:, pb, 0:nk], PF[:, b * 1024:b * 1024 + nk], ACT.Exp,
                                       bias=SM[:, j:j + 1], accum_out=SM[:, 4 + j:5 + j]).then_inc(ex_done, 1)

                    for job in att.first_preps:
                        prep_hi(job)
                    act.wait_ge(lam_v, l + 1)
                    act.activation(LM[:, 2:4], LM[:, 0:2], ACT.Exp).then_inc(lam_e, 1)
                    for i in att.steps:
                        if 0 <= i + 2 < att.n:
                            exps(i + 2, 0)
                        g = att.ends(i, 3)
                        if g is not None:
                            part, h, toks, bank = y_places(att, g)
                            act.wait_ge(pv_mm, gb + g + 1)
                            if part == "A":
                                rows = slice(64 * (h // 3), 64 * (h // 3) + 64)
                                act.activation(Y[rows, 0, h % 3, toks], PS[rows, bank, 0:2 * P], ACT.Copy) \
                                    .then_inc(y_hi, 1)
                            else:
                                if g >= att.nga + 2:
                                    act.wait_ge(y_lo, gb + g - 1)
                                act.activation(YRAW[0:DV, g % 2, :], PS[0:DV, bank, 0:2 * P], ACT.Copy)
                                act.activation(YSQ[0:DV, g % 2, :], PS[0:DV, bank, 0:2 * P], ACT.Square) \
                                    .then_inc(yr_done, 1)
                        if 0 <= i < att.n:
                            g = att.units[i][2]
                            if g >= 2:
                                act.wait_ge(pv_mm, gb + g - 1)
                            q0 = (att.units[i][3] % 2) * P
                            for n, a, m in att.parts(i):
                                act.wait_ge(t_mm, hb + n + 1)
                                act.activation(PT[:, g % 2, 0, a:a + m, q0:q0 + P],
                                               half_bank(n, m).rearrange("p (k q) -> p k q", q=P),
                                               ACT.Copy).then_inc(t_hi, 1)
                        if att.na <= i + 2 < att.n:
                            exps(i + 2, 1)
                        for job in att.preps.get(i, []):
                            prep_hi(job)
                        if i in (att.n - 1, att.n):
                            split_hi(u0 + NMU + i - (att.n - 1))
                        g = att.ends(i, 5)
                        if g is not None and g >= att.nga:
                            part, h, toks, bank = y_places(att, g)
                            act.wait_ge(yn_done, cb + g - att.nga + 1)
                            act.activation(Y[0:DV, 0, 3 + h, toks], YSQ[0:DV, g % 2, :], ACT.Copy) \
                                .then_inc(y_hi, 1)

                if kind == "out":
                    u0 = count(p, "units")
                    for m in range(1, KD):
                        if next_is_prefetched(p, u0 + m):
                            split_hi(u0 + m + 1)
            for i, t in enumerate(FINAL_TILES):
                act.wait_ge(f_t, i + 1)
                if i >= 2:
                    act.wait_ge(f_sq, i - 1)
                act.activation(OJ[:, i % 2, :], PF[:, 1024 * t:1024 * t + D], ACT.Square,
                               accum_out=FSS[:, t:t + 1]).then_inc(f_sq, 1)

        @block.vector
        def _(dve):
            steps = [0]

            def link(ins):
                steps[0] += 1
                ins.then_inc(dve_step, 1)
                dve.wait_ge(dve_step, steps[0])

            def split_lo(u, it=None):
                dve.wait_ge(w_hi, u + 1 if it is None else u + 1 + 2 * it)
                src, dst = stage_ring(u)
                for r, a, b in UNIT_WORDS[u]:
                    ins = dve.tensor_tensor(dst[0:r, 1, u % 2, a:b], src[0:r, u % 2, a:b],
                                            dst[0:r, 0, u % 2, a:b].bitcast(F32), ALU.subtract)
                ins.then_inc(w_split, 1)

            def mod_piece(slot, k, piece, it=None):
                dve.wait_ge(mw_landed[slot], 16 * (piece // 2 + 1) if it is None else 16 * (piece // 2 + 1) + 16 * it)
                dve.wait_ge(mac_done, piece + 1 if it is None else piece + 1 + 2 * it)
                for v in range(2):
                    col = SCV[:, k, v:v + 1] if it is None else SCV[:, ds(2 * it + k, 1), v:v + 1]
                    ins = dve.scalar_tensor_tensor(ACC[:, v, :], MW[:, slot, :], col, ACC[:, v, :], ALU.mult, ALU.add)
                ins.then_inc(mac_done, 1)

            def clear_sums(n):
                dve.memset(ACC[:, :, :], 0.0).then_inc(acc_clear, 1)
                dve.wait_ge(acc_clear, n + 1)

            def finish_module(q, n, place=FN):
                dve.wait_ge(fin_mm, n + 1)
                dve.tensor_tensor(MODS[:, q * KD:(q + 1) * KD, :], place.rearrange("p (k v) -> p k v", v=2),
                                  BM[:, q * KD:(q + 1) * KD].unsqueeze(2).broadcast_to([P, KD, 2]), ALU.add) \
                    .then_inc(mod_ready, 1)
                dve.wait_ge(mod_ready, n + 2)

            dve.wait_ge(cst, 5)
            dve.tensor_copy(IDR[:, :], IDENT[:, :])
            dve.wait_ge(vec_t, 1)
            dve.tensor_copy(VEC[:, :], PS[:, 0, 0:80]).then_inc(h_lo, 1)
            dve.tensor_copy(BM[:, 0:72], PS[:, 1, 0:72]).then_inc(mac_done, 1)
            dve.tensor_copy(BM[:, 72:144], PS[:, 1, 128:200]).then_inc(vec_ev, 1)
            dve.wait_ge(vec_ev, 1)
            for k in range(KD):
                dve.wait_ge(xt_mm, k + 1)
                b = 2048 if k % 2 else 1024
                dve.tensor_copy(X[:, k, :], PF[:, b:b + T]).then_inc(xt_ev, 1)
            for i in range(2 * START_MODULES):
                dve.wait_ge(ms_used, i + 1)
                if i >= 2:
                    dve.wait_ge(mr_t, i - 1)
                dve.tensor_copy(MR[:, i % 2, :], PS[0:2, MS_BANKS[i], :]).then_inc(mr_done, 1)
            dve.wait_ge(mr_t, 2 * START_MODULES)
            n = START_MODULES * KD
            dve.tensor_tensor(MODS[:, 0:n, :], PS[:, 2, 0:2 * n].rearrange("p (k v) -> p k v", v=2),
                              BM[:, 0:n].unsqueeze(2).broadcast_to([P, n, 2]), ALU.add).then_inc(mod_ready, 1)
            dve.wait_ge(mod_ready, 1)

            for p, (kind, l, which) in enumerate(PHASES):
                last = l == DEPTH - 1
                if kind == "norm":
                    both = has_ctx("norm", l, which)
                    tok = T if both else NLAT
                    nt = tok // P
                    sc = (NMOD * l + 3 * which + 1) * KD
                    gcol = 16 + 16 * which + KD * l
                    dve.scalar_tensor_tensor(AA[:, :, :], MODS[:, sc:sc + KD, :], 1.0,
                                             VEC[:, gcol:gcol + KD].unsqueeze(2).broadcast_to([P, KD, 2]),
                                             ALU.add, ALU.mult).then_inc(ab_done, 1)
                    dve.wait_ge(st_mm, count(p, "stat") + 1)
                    link(dve.tensor_reduce(MSS[:, 0:nt], MS7.rearrange("p (a t) -> p t a", t=8)[:, 0:nt, :], AX.X,
                                           ALU.add))
                    dve.tensor_scalar(MSQ[:, 0:nt], MSS[:, 0:nt], 1.0 / D, EPS, ALU.mult, ALU.add).then_inc(ms_done, 1)
                    dve.wait_ge(rstd_done, count(p, "stat") + 1)
                    link(dve.tensor_copy(RSR[:, 0, 0:nt], RST[:, 0:nt]))
                    dve.tensor_tensor(RSR[:, 1, 0:nt], RST[:, 0:nt], RSR[:, 0, 0:nt].bitcast(F32), ALU.subtract) \
                        .then_inc(rs_split, 1)
                    dve.wait_ge(bc_mm, count(p, "stat") + 1)

                    def scaled(k):
                        if k >= 2:
                            dve.wait_ge(ny_done, count(p, "ny") + k - 1)
                        dve.tensor_tensor(NT[:, k % 2, 0:tok], X[:, k, 0:tok], BC[:, 0:tok], ALU.mult) \
                            .then_inc(nt_done, 1)

                    scaled(0)
                    scaled(1)
                    if PHASES[p - 1][0] == "start":
                        split_lo(0)
                    for k in range(KD):
                        if k == 2 and norm_module(p) is not None:
                            finish_module(norm_module(p), count(p, "fin") - 1, FN5)
                        if 2 <= k < KD - 1:
                            scaled(k + 1)
                        dve.wait_ge(xn_hi, count(p, "xh") + k + 1)
                        dve.tensor_tensor(XN[:, 1, k, 0:tok], NY[:, k % 2, 0:tok],
                                          XN[:, 0, k, 0:tok].bitcast(F32), ALU.subtract).then_inc(xn_lo, 1)
                        if k == 0:
                            scaled(2)
                if kind == "ffn":
                    both = has_ctx("ffn", l, which)
                    tok = T if both else NLAT
                    gate = (NMOD * l + (2 if which == 0 else 8)) * KD
                    pending = None
                    for g, part, u0, e0, h0, n, q in parts(p, l, which):
                        piece = 8 * modules_before(p, l, which, g, part)
                        late = pending if (g, part) == (len(GROUPS) - 1, "out") else None
                        if pending is not None and late is None:
                            finish_module(*pending)
                        pending = None
                        if q is not None:
                            if late is None:
                                clear_sums(modules_before(p, l, which, g, part))
                            pending = (q, modules_before(p, l, which, g, part))
                        if part == "in":
                            with dve.Fori(0, n // 2) as it:
                                for j in range(2):
                                    c = 2 * it + j
                                    split_lo(u0 + j + 1, it)
                                    if q is not None:
                                        mod_piece(j, j, piece + j, it)
                                    a_lat, a_ctx, b_ctx, b_lat = set_views((e0 + j) % 2)
                                    dve.wait_ge(silu_done, count(p, "hidden") + h0 + j + 1 + 2 * it)
                                    dve.wait_ge(h_lo, count(p, "hidden") + h0 + j + 1 + 2 * it)
                                    ins = dve.tensor_tensor(HF[:, 0:NLAT], b_lat, SG[:, 0:NLAT], ALU.mult)
                                    if both:
                                        ins = dve.tensor_tensor(HF[:, NLAT:T], b_ctx, SG[:, NLAT:T], ALU.mult)
                                    ins.then_inc(evacuated, 1)
                                    dve.wait_ge(h_hi, count(p, "hidden") + h0 + j + 1 + 2 * it)
                                    dve.tensor_tensor(H[:, 1, ds(c, 1), 0:tok], HF[:, 0:tok].unsqueeze(1),
                                                      H[:, 0, ds(c, 1), 0:tok].bitcast(F32), ALU.subtract) \
                                        .then_inc(h_lo, 1)
                            if q is not None:
                                for k in range(n, KD):
                                    mod_piece(k % 2, k, piece + k)
                            continue
                        if g == 0:
                            dve.tensor_scalar(GG[:, :, :], MODS[:, gate:gate + KD, :], 0.5, None, ALU.mult) \
                                .then_inc(gate_ready, 1)
                            dve.wait_ge(gate_ready, 2 * l + which + 1)
                        for i in range(n):
                            u = u0 + i
                            if next_is_prefetched(p, u):
                                split_lo(u + 1)
                            if q is not None and late is None:
                                for k in out_pieces(g, i):
                                    mod_piece(k % 2, k, piece + k)
                            products_done(dve, u)
                            a_lat, a_ctx, b_ctx, b_lat = set_views((e0 + i) % 2)
                            for b, lat, cx in ((0, a_lat, a_ctx), (1, b_lat, b_ctx)):
                                m = 2 * i + b
                                ins = dve.scalar_tensor_tensor(X[:, m, 0:NLAT], lat, GG[:, m, 0:1], X[:, m, 0:NLAT],
                                                               ALU.mult, ALU.add)
                                if both:
                                    ins = dve.scalar_tensor_tensor(X[:, m, NLAT:T], cx, GG[:, m, 1:2],
                                                                   X[:, m, NLAT:T], ALU.mult, ALU.add)
                            ins.then_inc(evacuated, 1)
                            if late is not None:
                                finish_module(*late)
                                late = None
                                clear_sums(modules_before(p, l, which, g, part))
                                for k in out_pieces(g, i):
                                    mod_piece(k % 2, k, piece + k)
                if kind == "mix":
                    dve_mix(dve, p, l, last, link, split_lo)
                if kind == "out":
                    u0, e0 = count(p, "units"), count(p, "evac")
                    gate = (NMOD * l + 5) * KD
                    for m in range(KD):
                        u = u0 + m
                        if m >= 1 and next_is_prefetched(p, u):
                            split_lo(u + 1)
                        products_done(dve, u)
                        a_lat, a_ctx, b_ctx, b_lat = set_views((e0 + m) % 2)
                        ins = dve.scalar_tensor_tensor(X[:, m, 0:NLAT], a_lat, MODS[:, gate + m, 0:1],
                                                       X[:, m, 0:NLAT], ALU.mult, ALU.add)
                        if not last:
                            ins = dve.scalar_tensor_tensor(X[:, m, NLAT:T], a_ctx, MODS[:, gate + m, 1:2],
                                                           X[:, m, NLAT:T], ALU.mult, ALU.add)
                        ins.then_inc(evacuated, 1)
            def output_tile(i):
                t = FINAL_TILES[i]
                dve.wait_ge(f_rs, i + 1)
                dve.scalar_tensor_tensor(OUTB[:, t, :], PF[:, 1024 * t:1024 * t + D], FRS[:, t:t + 1], GF[:, :],
                                         ALU.mult, ALU.mult).then_inc(f_n, 1)

            dve.wait_ge(gf_in, 16)
            for i, t in enumerate(FINAL_TILES):
                dve.wait_ge(f_sq, i + 1)
                dve.tensor_scalar(FMS[:, t:t + 1], FSS[:, t:t + 1], 1.0 / D, EPS, ALU.mult, ALU.add).then_inc(f_ms, 1)
                if i:
                    output_tile(i - 1)
            output_tile(TLAT - 1)


        @block.tensor
        def _(pe):
            def passes(out_, wh, wl, xh, xl, first, final):
                pe.matmul(out_, wh, xl, start=first, stop=False)
                pe.matmul(out_, wl, xh, start=False, stop=False)
                return pe.matmul(out_, wh, xh, start=False, stop=final)

            def unit(u, e, xh, xl, chunks, both, it=None, wait_chunk=None, blocks=2, rows=None, col=None):
                dyn = 0 if it is None else 2 * it
                pe.wait_ge(w_split, u + 1 + dyn)
                if e >= 2:
                    pe.wait_ge(evacuated, e - 1 + dyn)
                a_lat, a_ctx, b_ctx, b_lat = set_views(e % 2)
                s = u % 2
                w = col or (lambda hl, k, b: ring(hl, s, k, b * P, P))
                ins = None
                for k in range(chunks):
                    if wait_chunk is not None:
                        wait_chunk(k)
                    f, z = k == 0, k == chunks - 1
                    r = P if rows is None else rows(k)
                    for b, lat in ((0, a_lat), (1, b_lat))[:blocks]:
                        ins = passes(lat, w(0, k, b)[0:r], w(1, k, b)[0:r], xh(k, 0)[0:r], xl(k, 0)[0:r], f, z)
                        if b == 0 and both:
                            ins = passes(a_ctx, w(0, k, b)[0:r], w(1, k, b)[0:r], xh(k, 1)[0:r], xl(k, 1)[0:r], f, z)
                if both and blocks == 2:
                    for k in range(chunks):
                        ins = passes(b_ctx, w(0, k, 1), w(1, k, 1), xh(k, 1), xl(k, 1), k == 0, k == chunks - 1)
                ins.then_inc(unit_done, 1)

            def stream(s):
                return slice(0, NLAT) if s == 0 else slice(NLAT, T)

            pe.wait_ge(cst, 5)
            pe.wait_ge(vrow_in, 144)
            pe.transpose(PS[:, 0, 0:P], VROW[:, 0, :], IDENT[:, :]).then_inc(unit_done, 1)
            pe.transpose(PS[:, 1, 0:P], VROW[:, 1, :], IDENT[:, :])
            pe.transpose(PS[:, 1, P:2 * P], VROW[:, 2, :], IDENT[:, :]).then_inc(vec_t, 1)
            pe.wait_ge(x_in, 32)
            for k in range(KD):
                if k >= 2:
                    pe.wait_ge(xt_ev, k - 1)
                b = 2048 if k % 2 else 1024
                for t in range(TT):
                    ins = pe.transpose(PF[:, b + t * P:b + (t + 1) * P], XLOAD[:, t, k * P:(k + 1) * P], IDENT[:, :])
                ins.then_inc(xt_mm, 1)
            pe.wait_ge(scv_done, 1)

            def turn_rows(i):
                pe.wait_ge(mr_done, i + 1)
                for j in range(4):
                    o1 = 2 * (4 * i + j)
                    ins = pe.transpose(PS[:, 2, o1:o1 + 2], MR[:, i % 2, j * P:(j + 1) * P], IDENT[0:2, 0:2])
                ins.then_inc(mr_t, 1)

            pe.wait_ge(xt_ev, KD)
            for i in range(2 * START_MODULES):
                pe.wait_ge(ms_landed[i % 3], 16 * (i // 3 + 1))
                for k in range(KD):
                    ins = pe.matmul(PS[0:2, MS_BANKS[i], :], SCV[:, k, :], MSW[:, i % 3, k, :],
                                    start=k == 0, stop=k == KD - 1)
                ins.then_inc(ms_used, 1)
                if i:
                    turn_rows(i - 1)
            turn_rows(2 * START_MODULES - 1)

            def finish_module(n, place=FN):
                pe.wait_ge(mac_done, 8 * (n + 1) + 1)
                pe.wait_ge(mod_ready, n + 1)
                for k in range(KD):
                    for v in range(2):
                        ins = pe.matmul(place[:, 2 * k + v:2 * k + v + 1], ACC[:, v, k * P:(k + 1) * P],
                                        ONE[:, :], start=True, stop=True)
                ins.then_inc(fin_mm, 1)

            for p, (kind, l, which) in enumerate(PHASES):
                last = l == DEPTH - 1
                if kind == "norm":
                    nt = (T if has_ctx("norm", l, which) else NLAT) // P
                    pe.wait_ge(mod_ready, count(p, "fin") + (norm_module(p) is None))
                    for a in range(3):
                        if a == 0:
                            pe.wait_ge(ss_done, count(p, "ss") + KD - 2)
                        else:
                            pe.wait_ge(sqa_done, count(p, "sqa") + a)
                        for t in range(nt):
                            src = SS[:, t * P:(t + 1) * P] if a == 0 else SQA[:, a - 1, t * P:(t + 1) * P]
                            ins = pe.matmul(MS7[:, 8 * a + t:8 * a + t + 1], src, ONE[:, :], start=True, stop=True)
                    ins.then_inc(st_mm, 1)
                    pe.wait_ge(rs_split, count(p, "stat") + 1)
                    for t in range(nt):
                        for hl in range(2):
                            ins = pe.matmul(BC[:, t * P:(t + 1) * P], RSR[:, hl, t:t + 1].broadcast_to([P, P]),
                                            IDR[:, :], start=hl == 0, stop=hl == 1)
                    ins.then_inc(bc_mm, 1)
                    if norm_module(p) is not None:
                        finish_module(count(p, "fin") - 1, FN5)
                if kind == "ffn":
                    both = has_ctx("ffn", l, which)
                    xl0 = AT[p]["xl"]
                    pending = None

                    for g, part, u0, e0, h0, n, q in parts(p, l, which):
                        late = pending if (g, part) == (len(GROUPS) - 1, "out") else None
                        if pending is not None and late is None:
                            finish_module(pending)
                        pending = None
                        if q is not None:
                            pending = modules_before(p, l, which, g, part)
                        if part == "in":
                            xh = lambda k, s: XN[:, 0, k, stream(s)]
                            xl = lambda k, s: XN[:, 1, k, stream(s)]
                            lead = 0
                            if g == 0:
                                lead = 2
                                unit(u0, e0, xh, xl, KD, both,
                                     wait_chunk=lambda k: pe.wait_ge(xn_lo, xl0 - KD + k + 1))
                                pe.wait_ge(mod_ready, 1 + count(p, "fin"))
                                unit(u0 + 1, e0 + 1, xh, xl, KD, both)
                            with pe.Fori(lead // 2, n // 2) as it:
                                for j in range(2):
                                    unit(u0 + j, e0 + j, xh, xl, KD, both, it)
                        else:
                            xh = lambda k, s: H[:, 0, k, stream(s)]
                            xl = lambda k, s: H[:, 1, k, stream(s)]
                            hid = count(p, "hidden") + h0
                            for i in range(n):
                                unit(u0 + i, e0 + i, xh, xl, GROUPS[g], both,
                                     wait_chunk=(lambda k: pe.wait_ge(h_lo, hid + k + 2)) if i == 0 else None)
                                if late is not None:
                                    finish_module(late)
                                    late = None
                if kind == "mix":
                    pe_mix(pe, p, l, last, passes)
                if kind == "out":
                    u0, e0 = count(p, "units"), count(p, "evac")

                    def y_part(hl, k, s):
                        if k < 3:
                            return Y[:, hl, k, stream(s)]
                        if k < 5:
                            return YB[:, hl, k - 3, stream(s)]
                        return Y[:, hl, k - 2, stream(s)]

                    att = Attention(last)

                    def y_made(k):
                        n = att.nga if k < 5 else att.nga + (k - 4) * (att.ng - att.nga) // HC
                        pe.wait_ge(y_lo, count(p - 1, "group") + n)

                    for m in range(KD):
                        slot = (u0 + m) % 2
                        unit(u0 + m, e0 + m, lambda k, s: y_part(0, k, s), lambda k, s: y_part(1, k, s), 9, not last,
                             blocks=1, rows=lambda k: P if k < 5 else DV, wait_chunk=y_made if m == 0 else None,
                             col=lambda hl, k, b: OR[:, hl, slot, k * P:(k + 1) * P])
            for t in FINAL_TILES:
                for k in range(KD):
                    if t == FINAL_TILES[0]:
                        pe.wait_ge(evacuated, TOTAL["evac"] - 4 + k // 2 + 1)
                    ins = pe.transpose(PF[:, 1024 * t + k * P:1024 * t + (k + 1) * P],
                                       X[:, k, t * P:(t + 1) * P], IDENT[:, :])
                ins.then_inc(f_t, 1)


_INS = ["x", "c", "ctx", "c_ctx", "w_mod", "b_mod", "g_ffn1", "w_ffn1_in", "w_ffn1_out", "g_mix", "w_mix_in",
        "w_mix_out", "g_qnorm", "g_knorm", "g_vnorm", "w_spatial", "b_spatial", "lambda_vecs", "g_subln", "g_ffn2",
        "w_ffn2_in", "w_ffn2_out", "g_final"]
GRID_W = 64
ROPE_BASE = 10000.0


def rope_tables(d):
    half, m = d // 2, d // 4
    freqs = (1.0 / ROPE_BASE ** (np.arange(0, half, 2, dtype=np.float32) / half)).astype(np.float32)
    tokens = np.arange(NLAT)
    out = np.empty((2, NLAT, d), np.float32)
    for axis, pos in enumerate((tokens // GRID_W, tokens % GRID_W)):
        ang = (pos.astype(np.float32)[:, None] * freqs).astype(np.float32)
        o = axis * half
        out[0, :, o:o + half] = np.concatenate([np.cos(ang), np.cos(ang)], 1)
        out[1, :, o:o + half] = np.concatenate([-np.sin(ang), np.sin(ang)], 1)
    return np.ascontiguousarray(out.reshape(2, TLAT, P, d).transpose(0, 2, 1, 3))


def kernel(**inputs):
    import concourse.bacc as _bacc
    from concourse.bass_utils import run_bass_kernel_spmd as _run

    nc = _bacc.Bacc("TRN2", target_bir_lowering=False, num_devices=1)
    arrays = {name: np.ascontiguousarray(inputs[name]) for name in _INS}
    arrays["rope_a"], arrays["rope_c"] = rope_tables(DA), rope_tables(DC)
    A = {name: nc.dram_tensor(name, a.shape, mybir.dt.from_np(a.dtype), kind="ExternalInput").ap()
         for name, a in arrays.items()}
    out = nc.dram_tensor("out", (1, NLAT, D), F32, kind="ExternalOutput").ap()
    build(nc, A, out)
    return _run(nc, [arrays], core_ids=[0]).results[0]["out"]
```
